# Optimizing a Trainium2 kernel written in Bass

```python
import jax, jax.numpy as jnp
from jax import lax
import numpy as np

D_MODEL = 1024
BATCH = 1
SEQ = 512
DEPTH = 2

EPS = 1e-6
D_FF = 2816
CONV_WIDTH = 4
D_RG = D_MODEL // 2
RG_BLOCKS = 8
RG_C = 8.0
ML_HEADS = 4
D_ML = D_MODEL // 2
ML_HEAD_DIM = D_ML // ML_HEADS
ML_CHUNK = 128
D_AB_IN = 2 * D_RG + 4 * D_ML + 2 * ML_HEADS
NSA_HEADS = 16
NSA_GROUPS = 4
NSA_HEAD_DIM = 64
NSA_KV = NSA_GROUPS * NSA_HEAD_DIM
NSA_WIDTH = NSA_HEADS * NSA_HEAD_DIM
CMP_BLOCK = 32
CMP_STRIDE = 16
CMP_HIDDEN = 256
SEL_BLOCK = 64
SEL_TOPN = 8
WINDOW = 256
NSA_QBLOCK = 64
NSA_BRANCHES = 3
D_NSA_IN = NSA_WIDTH + 6 * NSA_KV + NSA_BRANCHES * NSA_HEADS
FORCED_SCORE = 1e6
N_EVEN = (DEPTH + 1) // 2
N_ODD = DEPTH // 2


def rmsnorm(x, g):
    xf = x.astype(jnp.float32)
    y = xf * lax.rsqrt(jnp.mean(xf * xf, axis=-1, keepdims=True) + EPS)
    return (y * g.astype(jnp.float32)).astype(x.dtype)

def swiglu_ffn(x, w_gu, w_down):
    gate, up = jnp.split(x @ w_gu, 2, axis=-1)
    return (jax.nn.silu(gate) * up) @ w_down

def causal_dwconv(x, w, b):
    k, c = w.shape
    y = lax.conv_general_dilated(x, w[:, None, :], window_strides=(1,), padding=[(k - 1, 0)],
                                 dimension_numbers=('NWC', 'WIO', 'NWC'), feature_group_count=c)
    return y + b

def masked_softmax(s, mask):
    s = jnp.where(mask, s.astype(jnp.float32), -1e30)
    return jax.nn.softmax(s, axis=-1) * mask

def rglru(x, w_r, b_r, w_i, b_i, lam):
    bsz, s, c = x.shape
    xb = x.reshape(bsz, s, RG_BLOCKS, c // RG_BLOCKS)
    r = jax.nn.sigmoid(jnp.einsum('bsnc,ncd->bsnd', xb, w_r).reshape(bsz, s, c) + b_r)
    ig = jax.nn.sigmoid(jnp.einsum('bsnc,ncd->bsnd', xb, w_i).reshape(bsz, s, c) + b_i)
    log_a = -RG_C * r.astype(jnp.float32) * jax.nn.softplus(-lam.astype(jnp.float32))
    a = jnp.exp(log_a)
    u = jnp.sqrt(-jnp.expm1(2.0 * log_a)) * (ig * x).astype(jnp.float32)

    def combine(left, right):
        a1, b1 = left
        a2, b2 = right
        return a1 * a2, a2 * b1 + b2

    _, h = lax.associative_scan(combine, (a, u), axis=1)
    return h.astype(x.dtype)

def mlstm_chunkwise(q, k, v, log_i, log_f):
    bsz, nh, s, dh = q.shape
    nc = s // ML_CHUNK
    q = q.reshape(bsz, nh, nc, ML_CHUNK, dh) * (dh ** -0.5)
    k = k.reshape(bsz, nh, nc, ML_CHUNK, dh)
    v = v.reshape(bsz, nh, nc, ML_CHUNK, dh)
    log_i = log_i.reshape(bsz, nh, nc, ML_CHUNK)
    b = jnp.cumsum(log_f.reshape(bsz, nh, nc, ML_CHUNK), axis=-1)
    g = b[..., -1]
    w = g[..., None] - b + log_i
    m_loc = jnp.max(w, axis=-1)
    wk = jnp.exp(w - m_loc[..., None])
    c_loc = jnp.einsum('bhcl,bhclv,bhclk->bhcvk', wk, v, k)
    n_loc = jnp.einsum('bhcl,bhclk->bhck', wk, k)

    def step(carry, xs):
        c_st, n_st, m_st = carry
        c_l, n_l, m_l, g_c = xs
        m_new = jnp.maximum(g_c + m_st, m_l)
        sa = jnp.exp(g_c + m_st - m_new)
        sb = jnp.exp(m_l - m_new)
        new = (sa[..., None, None] * c_st + sb[..., None, None] * c_l,
               sa[..., None] * n_st + sb[..., None] * n_l, m_new)
        return new, carry

    init = (jnp.zeros((bsz, nh, dh, dh), jnp.float32), jnp.zeros((bsz, nh, dh), jnp.float32),
            jnp.full((bsz, nh), -1e30, jnp.float32))
    xs = (jnp.moveaxis(c_loc, 2, 0), jnp.moveaxis(n_loc, 2, 0),
          jnp.moveaxis(m_loc, 2, 0), jnp.moveaxis(g, 2, 0))
    _, (c0, n0, m0) = lax.scan(step, init, xs)
    c0 = jnp.moveaxis(c0, 0, 2)
    n0 = jnp.moveaxis(n0, 0, 2)
    m0 = jnp.moveaxis(m0, 0, 2)
    causal = jnp.tril(jnp.ones((ML_CHUNK, ML_CHUNK), bool))
    d = jnp.where(causal, b[..., :, None] - b[..., None, :] + log_i[..., None, :], -jnp.inf)
    m_inter = b + m0[..., None]
    m = jnp.maximum(m_inter, jnp.max(d, axis=-1))
    p = jnp.exp(d - m[..., None]) * jnp.einsum('bhcjd,bhckd->bhcjk', q, k)
    sc = jnp.exp(m_inter - m)
    num = sc[..., None] * jnp.einsum('bhcvk,bhcjk->bhcjv', c0, q) + jnp.einsum('bhcjk,bhckv->bhcjv', p, v)
    den = sc * jnp.einsum('bhck,bhcjk->bhcj', n0, q) + jnp.sum(p, axis=-1)
    h = num / jnp.maximum(jnp.abs(den), jnp.exp(-m))[..., None]
    return h.reshape(bsz, nh, s, dh)

def mlstm_block(qk, v, o, i_pre, f_pre, conv_w, conv_b, b_i, b_f, norm_g):
    bsz, s, _ = v.shape
    qk = jax.nn.silu(causal_dwconv(qk, conv_w, conv_b))
    q, k = jnp.split(qk, 2, axis=-1)
    heads = lambda t: t.reshape(bsz, s, ML_HEADS, ML_HEAD_DIM).transpose(0, 2, 1, 3).astype(jnp.float32)
    log_i = (i_pre + b_i).astype(jnp.float32).transpose(0, 2, 1)
    log_f = jax.nn.log_sigmoid((f_pre + b_f).astype(jnp.float32)).transpose(0, 2, 1)
    h = mlstm_chunkwise(heads(q), heads(k), heads(v), log_i, log_f)
    h = h * lax.rsqrt(jnp.mean(h * h, axis=-1, keepdims=True) + EPS)
    h = h.transpose(0, 2, 1, 3).reshape(bsz, s, D_ML) * norm_g.astype(jnp.float32)
    return (jax.nn.sigmoid(o.astype(jnp.float32)) * h).astype(v.dtype)

def ab_mixer(xn, w_in, rg_conv_w, rg_conv_b, rg_w_r, rg_b_r, rg_w_i, rg_b_i, rg_lambda,
             ml_conv_w, ml_conv_b, ml_b_i, ml_b_f, ml_norm, w_out):
    proj = xn @ w_in
    cuts = [D_RG, 2 * D_RG, 2 * D_RG + 2 * D_ML, 2 * D_RG + 3 * D_ML, 2 * D_RG + 4 * D_ML,
            2 * D_RG + 4 * D_ML + ML_HEADS]
    xa, ga, qk, v, o, i_pre, f_pre = jnp.split(proj, cuts, axis=-1)
    ya = jax.nn.gelu(ga) * rglru(causal_dwconv(xa, rg_conv_w, rg_conv_b),
                                 rg_w_r, rg_b_r, rg_w_i, rg_b_i, rg_lambda)
    yb = mlstm_block(qk, v, o, i_pre, f_pre, ml_conv_w, ml_conv_b, ml_b_i, ml_b_f, ml_norm)
    return jnp.concatenate([ya, yb], axis=-1) @ w_out

def compress_blocks(kv, pe, w1, b1, w2):
    bsz, s, g, dk = kv.shape
    nb = (s - CMP_BLOCK) // CMP_STRIDE + 1
    idx = np.arange(nb)[:, None] * CMP_STRIDE + np.arange(CMP_BLOCK)[None, :]
    blk = kv[:, idx] + pe[:, None, :]
    blk = blk.transpose(0, 1, 3, 2, 4).reshape(bsz, nb, g, CMP_BLOCK * dk)
    return jax.nn.gelu(blk @ w1 + b1) @ w2

def cmp_to_sel_matrix(n_cmp, n_sel):
    cs = np.arange(n_cmp)[:, None] * CMP_STRIDE
    ss = np.arange(n_sel)[None, :] * SEL_BLOCK
    ov = np.clip(np.minimum(cs + CMP_BLOCK, ss + SEL_BLOCK) - np.maximum(cs, ss), 0, None)
    return jnp.asarray(ov / CMP_BLOCK, dtype=jnp.float32)

def nsa_mixer(xn, w_in, pe_k, k_w1, k_b1, k_w2, pe_v, v_w1, v_b1, v_w2, b_gate, w_out):
    bsz, s, _ = xn.shape
    g, r, dk = NSA_GROUPS, NSA_HEADS // NSA_GROUPS, NSA_HEAD_DIM
    proj = xn @ w_in
    cuts = list(np.cumsum([NSA_WIDTH] + [NSA_KV] * 6))
    q, kc, vc, ks, vs, kw, vw, gates = jnp.split(proj, cuts, axis=-1)
    q = q.reshape(bsz, s, g, r, dk) * (dk ** -0.5)
    kvh = lambda t: t.reshape(bsz, s, g, dk)
    kc = compress_blocks(kvh(kc), pe_k, k_w1, k_b1, k_w2)
    vc = compress_blocks(kvh(vc), pe_v, v_w1, v_b1, v_w2)
    n_cmp = kc.shape[1]
    n_sel = s // SEL_BLOCK
    top_n = min(SEL_TOPN, n_sel)
    m_sel = cmp_to_sel_matrix(n_cmp, n_sel)
    cmp_end = jnp.arange(n_cmp) * CMP_STRIDE + CMP_BLOCK - 1
    sel_blk = jnp.arange(n_sel)
    ks = kvh(ks).transpose(0, 2, 1, 3)
    vs = kvh(vs).transpose(0, 2, 1, 3)
    pad = jnp.zeros((bsz, WINDOW, g, dk), xn.dtype)
    kw = jnp.concatenate([pad, kvh(kw)], axis=1)
    vw = jnp.concatenate([pad, kvh(vw)], axis=1)
    gates = jax.nn.sigmoid(gates.reshape(bsz, s, g, r, NSA_BRANCHES) + b_gate.reshape(g, r, NSA_BRANCHES))

    def query_block(s0):
        t = s0 + jnp.arange(NSA_QBLOCK)
        qb = lax.dynamic_slice_in_dim(q, s0, NSA_QBLOCK, axis=1)
        gb = lax.dynamic_slice_in_dim(gates, s0, NSA_QBLOCK, axis=1)
        sc = jnp.einsum('bqgrd,bngd->bgrqn', qb, kc)
        p_cmp = masked_softmax(sc, cmp_end[None, :] <= t[:, None])
        o_cmp = jnp.einsum('bgrqn,bngd->bqgrd', p_cmp.astype(vc.dtype), vc)
        score = jnp.einsum('bgqn,nj->bgqj', jnp.sum(p_cmp, axis=2), m_sel)
        cur = (t // SEL_BLOCK)[:, None]
        valid = sel_blk[None, :] * SEL_BLOCK <= t[:, None]
        forced = (sel_blk[None, :] == 0) | (sel_blk[None, :] == cur) | (sel_blk[None, :] == cur - 1)
        score = jnp.where(forced & valid, FORCED_SCORE, jnp.where(valid, score, -1.0))
        _, idx = lax.top_k(score, top_n)
        key_idx = (idx[..., None] * SEL_BLOCK + jnp.arange(SEL_BLOCK)).reshape(bsz, g, -1)
        n_keys = top_n * SEL_BLOCK
        k_sel = jnp.take_along_axis(ks, key_idx[..., None], axis=2).reshape(bsz, g, NSA_QBLOCK, n_keys, dk)
        v_sel = jnp.take_along_axis(vs, key_idx[..., None], axis=2).reshape(bsz, g, NSA_QBLOCK, n_keys, dk)
        ss = jnp.einsum('bqgrd,bgqkd->bgrqk', qb, k_sel)
        sel_mask = key_idx.reshape(bsz, g, 1, NSA_QBLOCK, n_keys) <= t[:, None]
        p_slc = masked_softmax(ss, sel_mask)
        o_slc = jnp.einsum('bgrqk,bgqkd->bqgrd', p_slc.astype(v_sel.dtype), v_sel)
        k_win = lax.dynamic_slice_in_dim(kw, s0, WINDOW + NSA_QBLOCK, axis=1)
        v_win = lax.dynamic_slice_in_dim(vw, s0, WINDOW + NSA_QBLOCK, axis=1)
        pos = s0 - WINDOW + jnp.arange(WINDOW + NSA_QBLOCK)
        win_mask = (pos[None, :] <= t[:, None]) & (pos[None, :] > t[:, None] - WINDOW) & (pos[None, :] >= 0)
        sw = jnp.einsum('bqgrd,bkgd->bgrqk', qb, k_win)
        p_win = masked_softmax(sw, win_mask)
        o_win = jnp.einsum('bgrqk,bkgd->bqgrd', p_win.astype(v_win.dtype), v_win)
        out = gb[..., 0:1] * o_cmp + gb[..., 1:2] * o_slc + gb[..., 2:3] * o_win
        return out.reshape(bsz, NSA_QBLOCK, NSA_WIDTH)

    starts = jnp.arange(s // NSA_QBLOCK) * NSA_QBLOCK
    out = lax.map(query_block, starts)
    out = out.transpose(1, 0, 2, 3).reshape(bsz, s, NSA_WIDTH)
    return out @ w_out

def first_inputs(seed: int = 0) -> dict:
    key = jax.random.key(seed)
    keys = iter(jax.random.split(key, 40))
    nrm = lambda shape, scale: scale * jax.random.normal(next(keys), shape, jnp.float32)
    gain = lambda shape: 1.0 + 0.05 * jax.random.normal(next(keys), shape, jnp.float32)
    a8 = jax.random.uniform(next(keys), (N_EVEN, D_RG), jnp.float32, 0.9, 0.999)
    a0 = a8 ** (1.0 / RG_C)
    rg_lambda = jnp.log(a0) - jnp.log1p(-a0)
    ml_b_f = jnp.linspace(3.0, 6.0, ML_HEADS, dtype=jnp.float32)[None, :] + nrm((N_EVEN, ML_HEADS), 0.1)
    flat = CMP_BLOCK * NSA_HEAD_DIM
    return {
        "x": nrm((BATCH, SEQ, D_MODEL), 1.0),
        "ffn1_norm": gain((DEPTH, D_MODEL)),
        "ffn1_w_gu": nrm((DEPTH, D_MODEL, 2 * D_FF), D_MODEL ** -0.5),
        "ffn1_w_down": nrm((DEPTH, D_FF, D_MODEL), D_FF ** -0.5),
        "mix_norm": gain((DEPTH, D_MODEL)),
        "ffn2_norm": gain((DEPTH, D_MODEL)),
        "ffn2_w_gu": nrm((DEPTH, D_MODEL, 2 * D_FF), D_MODEL ** -0.5),
        "ffn2_w_down": nrm((DEPTH, D_FF, D_MODEL), D_FF ** -0.5),
        "ab_w_in": nrm((N_EVEN, D_MODEL, D_AB_IN), D_MODEL ** -0.5),
        "rg_conv_w": nrm((N_EVEN, CONV_WIDTH, D_RG), CONV_WIDTH ** -0.5),
        "rg_conv_b": nrm((N_EVEN, D_RG), 0.02),
        "rg_w_r": nrm((N_EVEN, RG_BLOCKS, D_RG // RG_BLOCKS, D_RG // RG_BLOCKS), (D_RG // RG_BLOCKS) ** -0.5),
        "rg_b_r": nrm((N_EVEN, D_RG), 0.02),
        "rg_w_i": nrm((N_EVEN, RG_BLOCKS, D_RG // RG_BLOCKS, D_RG // RG_BLOCKS), (D_RG // RG_BLOCKS) ** -0.5),
        "rg_b_i": nrm((N_EVEN, D_RG), 0.02),
        "rg_lambda": rg_lambda,
        "ml_conv_w": nrm((N_EVEN, CONV_WIDTH, 2 * D_ML), CONV_WIDTH ** -0.5),
        "ml_conv_b": nrm((N_EVEN, 2 * D_ML), 0.02),
        "ml_b_i": nrm((N_EVEN, ML_HEADS), 0.1),
        "ml_b_f": ml_b_f,
        "ml_norm": gain((N_EVEN, D_ML)),
        "ab_w_out": nrm((N_EVEN, D_RG + D_ML, D_MODEL), (D_RG + D_ML) ** -0.5),
        "nsa_w_in": nrm((N_ODD, D_MODEL, D_NSA_IN), D_MODEL ** -0.5),
        "nsa_pe_k": nrm((N_ODD, CMP_BLOCK, NSA_HEAD_DIM), 0.1),
        "nsa_k_w1": nrm((N_ODD, flat, CMP_HIDDEN), flat ** -0.5),
        "nsa_k_b1": nrm((N_ODD, CMP_HIDDEN), 0.02),
        "nsa_k_w2": nrm((N_ODD, CMP_HIDDEN, NSA_HEAD_DIM), CMP_HIDDEN ** -0.5),
        "nsa_pe_v": nrm((N_ODD, CMP_BLOCK, NSA_HEAD_DIM), 0.1),
        "nsa_v_w1": nrm((N_ODD, flat, CMP_HIDDEN), flat ** -0.5),
        "nsa_v_b1": nrm((N_ODD, CMP_HIDDEN), 0.02),
        "nsa_v_w2": nrm((N_ODD, CMP_HIDDEN, NSA_HEAD_DIM), CMP_HIDDEN ** -0.5),
        "nsa_b_gate": nrm((N_ODD, NSA_BRANCHES * NSA_HEADS), 0.1),
        "nsa_w_out": nrm((N_ODD, NSA_WIDTH, D_MODEL), NSA_WIDTH ** -0.5),
        "final_norm": gain((D_MODEL,)),
    }

def first_block(x, ffn1_norm, ffn1_w_gu, ffn1_w_down, mix_norm, ffn2_norm, ffn2_w_gu, ffn2_w_down,
              ab_w_in, rg_conv_w, rg_conv_b, rg_w_r, rg_b_r, rg_w_i, rg_b_i, rg_lambda,
              ml_conv_w, ml_conv_b, ml_b_i, ml_b_f, ml_norm, ab_w_out,
              nsa_w_in, nsa_pe_k, nsa_k_w1, nsa_k_b1, nsa_k_w2, nsa_pe_v, nsa_v_w1, nsa_v_b1, nsa_v_w2,
              nsa_b_gate, nsa_w_out, final_norm):
    for i in range(DEPTH):
        j = i // 2
        x = x + 0.5 * swiglu_ffn(rmsnorm(x, ffn1_norm[i]), ffn1_w_gu[i], ffn1_w_down[i])
        xn = rmsnorm(x, mix_norm[i])
        if i % 2 == 0:
            x = x + ab_mixer(xn, ab_w_in[j], rg_conv_w[j], rg_conv_b[j], rg_w_r[j], rg_b_r[j],
                             rg_w_i[j], rg_b_i[j], rg_lambda[j], ml_conv_w[j], ml_conv_b[j],
                             ml_b_i[j], ml_b_f[j], ml_norm[j], ab_w_out[j])
        else:
            x = x + nsa_mixer(xn, nsa_w_in[j], nsa_pe_k[j], nsa_k_w1[j], nsa_k_b1[j], nsa_k_w2[j],
                              nsa_pe_v[j], nsa_v_w1[j], nsa_v_b1[j], nsa_v_w2[j], nsa_b_gate[j], nsa_w_out[j])
        x = x + 0.5 * swiglu_ffn(rmsnorm(x, ffn2_norm[i]), ffn2_w_gu[i], ffn2_w_down[i])
    return rmsnorm(x, final_norm)


GRID_W = 64
QBLOCK = 128
NORM_EPS = 1e-6
ROPE_THETA = 10000.0
NEG_INF = -1e30

MLA_HEADS = 8
MLA_Q_RANK = 384
MLA_KV_RANK = 256
MLA_NOPE = 64
MLA_ROPE = 32
MLA_V = 64

DIL_PAIRS = ((128, 1), (512, 4), (2048, 16))
DIL_HALF = 64
DIL_SLOTS = 4
DIL_GROUPS = len(DIL_PAIRS)
DIL_HEADS = DIL_SLOTS * DIL_GROUPS
DIL_HEAD_DIM = 64

GQA_HEADS = 16
GQA_KV_HEADS = 4
GQA_HEAD_DIM = 64

FFN_HIDDEN = -(-8 * D_MODEL // (3 * 256)) * 256

IN_A = MLA_Q_RANK + MLA_KV_RANK + MLA_ROPE
IN_B = 3 * DIL_HEADS * DIL_HEAD_DIM
MIX_IN = IN_A + IN_B
MIX_OUT = MLA_HEADS * MLA_V + DIL_SLOTS * DIL_HEAD_DIM
N_EVEN_2 = (DEPTH + 1) // 2
N_ODD_2 = DEPTH // 2


def rmsnorm_2(x, g):
    xf = x.astype(jnp.float32)
    y = xf * lax.rsqrt(jnp.mean(xf * xf, axis=-1, keepdims=True) + NORM_EPS)
    return (y * g.astype(jnp.float32)).astype(x.dtype)

def rope_angles(pos, dim):
    freqs = ROPE_THETA ** (-jnp.arange(0, dim, 2, dtype=jnp.float32) / dim)
    ang = pos.astype(jnp.float32)[:, None] * freqs[None, :]
    return jnp.cos(ang), jnp.sin(ang)

def apply_rope(x, cos, sin):
    xf = x.astype(jnp.float32)
    x1, x2 = jnp.split(xf, 2, axis=-1)
    return jnp.concatenate([x1 * cos - x2 * sin, x1 * sin + x2 * cos], axis=-1).astype(x.dtype)

def blocked_attention(q, k, v, scale):
    b, h, s, dk = q.shape
    g = k.shape[1]
    r = h // g
    nq = s // QBLOCK
    qb = q.reshape(b, g, r, nq, QBLOCK, dk).transpose(3, 0, 1, 2, 4, 5)

    def one_block(qblk):
        sc = jnp.einsum('bgrqd,bgkd->bgrqk', qblk, k, preferred_element_type=jnp.float32) * scale
        p = jax.nn.softmax(sc, axis=-1)
        return jnp.einsum('bgrqk,bgkd->bgrqd', p.astype(v.dtype), v)

    out = lax.map(one_block, qb)
    return out.transpose(1, 2, 3, 0, 4, 5).reshape(b, h, s, -1)

def mla_mixer(h_a, q_norm_g, kv_norm_g, w_uq, w_ukv, cos, sin):
    b, s, _ = h_a.shape
    cq, ckv, k_rope = jnp.split(h_a, [MLA_Q_RANK, MLA_Q_RANK + MLA_KV_RANK], axis=-1)
    cq = rmsnorm_2(cq, q_norm_g)
    ckv = rmsnorm_2(ckv, kv_norm_g)
    q = jnp.einsum('bsr,rhd->bhsd', cq, w_uq)
    kv = jnp.einsum('bsr,rhd->bhsd', ckv, w_ukv)
    q_nope, q_rope = q[..., :MLA_NOPE], q[..., MLA_NOPE:]
    k_nope, v = kv[..., :MLA_NOPE], kv[..., MLA_NOPE:]
    q_rope = apply_rope(q_rope, cos, sin)
    k_rope = apply_rope(k_rope, cos, sin)[:, None]
    k_rope = jnp.broadcast_to(k_rope, (b, MLA_HEADS, s, MLA_ROPE))
    qh = jnp.concatenate([q_nope, q_rope], axis=-1)
    kh = jnp.concatenate([k_nope, k_rope], axis=-1)
    o = blocked_attention(qh, kh, v, (MLA_NOPE + MLA_ROPE) ** -0.5)
    return o.transpose(0, 2, 1, 3).reshape(b, s, MLA_HEADS * MLA_V)

def dilated_group_attention(q, k, v, dilation, slopes):
    b, hg, s, dh = q.shape
    P = DIL_HALF
    L = s // dilation
    nb = -(-L // P)
    Lp = nb * P

    def to_residue(t):
        return t.reshape(b, hg, L, dilation, dh).transpose(0, 1, 3, 2, 4)

    qr, kr, vr = to_residue(q), to_residue(k), to_residue(v)
    qb = jnp.pad(qr, ((0, 0), (0, 0), (0, 0), (0, Lp - L), (0, 0))).reshape(b, hg, dilation, nb, P, dh)

    def band(t):
        tb = jnp.pad(t, ((0, 0), (0, 0), (0, 0), (P, Lp - L + P), (0, 0))).reshape(b, hg, dilation, nb + 2, P, dh)
        return jnp.concatenate([tb[:, :, :, :-2], tb[:, :, :, 1:-1], tb[:, :, :, 2:]], axis=4)

    kb, vb = band(kr), band(vr)
    sc = jnp.einsum('bhrnqd,bhrnkd->bhrnqk', qb, kb, preferred_element_type=jnp.float32) * dh ** -0.5

    i = jnp.arange(P)[:, None]
    c = jnp.arange(3 * P)[None, :]
    rel = c - P - i
    uk = jnp.arange(nb)[:, None, None] * P + c - P
    valid = (jnp.abs(rel) <= DIL_HALF)[None] & (uk >= 0) & (uk < L)
    dist = (dilation * jnp.abs(rel)).astype(jnp.float32)
    bias = -slopes.astype(jnp.float32)[:, None, None, None, None] * dist

    sc = jnp.where(valid, sc + bias, NEG_INF)
    m = jnp.max(sc, axis=-1, keepdims=True)
    e = jnp.exp(sc - m)
    den = jnp.sum(e, axis=-1, keepdims=True)
    o = jnp.einsum('bhrnqk,bhrnkd->bhrnqd', (e / den).astype(v.dtype), vb)
    lse = (m + jnp.log(den))[..., 0]

    o = o.reshape(b, hg, dilation, Lp, dh)[:, :, :, :L].transpose(0, 1, 3, 2, 4).reshape(b, hg, s, dh)
    lse = lse.reshape(b, hg, dilation, Lp)[:, :, :, :L].transpose(0, 1, 3, 2).reshape(b, hg, s)
    return o, lse

def dilated_mixer(h_b, slopes):
    b, s, _ = h_b.shape

    def heads(t):
        return t.reshape(b, s, DIL_GROUPS, DIL_SLOTS, DIL_HEAD_DIM).transpose(2, 0, 3, 1, 4)

    q, k, v = (heads(t) for t in jnp.split(h_b, 3, axis=-1))
    outs, lses = [], []
    for g, (_, dil) in enumerate(DIL_PAIRS):
        o, lse = dilated_group_attention(q[g], k[g], v[g], dil, slopes[g * DIL_SLOTS:(g + 1) * DIL_SLOTS])
        outs.append(o)
        lses.append(lse)
    outs = jnp.stack(outs, axis=0)
    wts = jax.nn.softmax(jnp.stack(lses, axis=0), axis=0)
    comb = jnp.sum(wts[..., None] * outs.astype(jnp.float32), axis=0).astype(h_b.dtype)
    return comb.transpose(0, 2, 1, 3).reshape(b, s, DIL_SLOTS * DIL_HEAD_DIM)

def gqa_axial_mixer(hn, w_q, w_kv, q_gain, k_gain, w_o, cos_r, sin_r, cos_c, sin_c):
    b, s, _ = hn.shape
    q = (hn @ w_q).reshape(b, s, GQA_HEADS, GQA_HEAD_DIM).transpose(0, 2, 1, 3)
    kv = (hn @ w_kv).reshape(b, s, 2, GQA_KV_HEADS, GQA_HEAD_DIM)
    k = kv[:, :, 0].transpose(0, 2, 1, 3)
    v = kv[:, :, 1].transpose(0, 2, 1, 3)
    q = rmsnorm_2(q, q_gain)
    k = rmsnorm_2(k, k_gain)
    half = GQA_HEAD_DIM // 2

    def axial(t):
        return jnp.concatenate([apply_rope(t[..., :half], cos_r, sin_r),
                                apply_rope(t[..., half:], cos_c, sin_c)], axis=-1)

    o = blocked_attention(axial(q), axial(k), v, GQA_HEAD_DIM ** -0.5)
    return o.transpose(0, 2, 1, 3).reshape(b, s, GQA_HEADS * GQA_HEAD_DIM) @ w_o

def swiglu(hn, w_in, w_out):
    gate, up = jnp.split(hn @ w_in, 2, axis=-1)
    return (jax.nn.silu(gate) * up) @ w_out

def second_inputs(seed: int = 0) -> dict:
    key = jax.random.key(seed)
    ks = jax.random.split(key, 18)
    f32 = jnp.float32

    def w(k, shape, fan_in):
        return jax.random.normal(k, shape, f32) * fan_in ** -0.5

    def gain(k, shape):
        return 1.0 + 0.02 * jax.random.normal(k, shape, f32)

    ne, no = N_EVEN_2, N_ODD_2
    return {
        "x": jax.random.normal(ks[0], (BATCH, SEQ, D_MODEL), f32),
        "mix_norm_ab": gain(ks[1], (ne, D_MODEL)),
        "w_in_ab": w(ks[2], (ne, D_MODEL, MIX_IN), D_MODEL),
        "mla_q_norm": gain(ks[3], (ne, MLA_Q_RANK)),
        "mla_kv_norm": gain(ks[4], (ne, MLA_KV_RANK)),
        "mla_w_uq": w(ks[5], (ne, MLA_Q_RANK, MLA_HEADS, MLA_NOPE + MLA_ROPE), MLA_Q_RANK),
        "mla_w_ukv": w(ks[6], (ne, MLA_KV_RANK, MLA_HEADS, MLA_NOPE + MLA_V), MLA_KV_RANK),
        "w_out_ab": w(ks[7], (ne, MIX_OUT, D_MODEL), MIX_OUT),
        "mix_norm_c": gain(ks[8], (no, D_MODEL)),
        "gqa_w_q": w(ks[9], (no, D_MODEL, GQA_HEADS * GQA_HEAD_DIM), D_MODEL),
        "gqa_w_kv": w(ks[10], (no, D_MODEL, 2 * GQA_KV_HEADS * GQA_HEAD_DIM), D_MODEL),
        "gqa_q_norm": gain(ks[11], (no, GQA_HEAD_DIM)),
        "gqa_k_norm": gain(ks[12], (no, GQA_HEAD_DIM)),
        "gqa_w_o": w(ks[13], (no, GQA_HEADS * GQA_HEAD_DIM, D_MODEL), GQA_HEADS * GQA_HEAD_DIM),
        "ffn_norm": gain(ks[14], (DEPTH, D_MODEL)),
        "ffn_w_in": w(ks[15], (DEPTH, D_MODEL, 2 * FFN_HIDDEN), D_MODEL),
        "ffn_w_out": w(ks[16], (DEPTH, FFN_HIDDEN, D_MODEL), FFN_HIDDEN),
        "final_norm": gain(ks[17], (D_MODEL,)),
    }

def second_block(x, mix_norm_ab, w_in_ab, mla_q_norm, mla_kv_norm, mla_w_uq, mla_w_ukv, w_out_ab,
              mix_norm_c, gqa_w_q, gqa_w_kv, gqa_q_norm, gqa_k_norm, gqa_w_o,
              ffn_norm, ffn_w_in, ffn_w_out, final_norm):
    s = x.shape[1]
    rows = s // GRID_W
    pos = jnp.arange(s)
    cos_t, sin_t = rope_angles(pos, MLA_ROPE)
    row_idx = jnp.broadcast_to(jnp.arange(rows)[:, None], (rows, GRID_W)).reshape(-1)
    col_idx = jnp.broadcast_to(jnp.arange(GRID_W)[None, :], (rows, GRID_W)).reshape(-1)
    cos_r, sin_r = rope_angles(row_idx, GQA_HEAD_DIM // 2)
    cos_c, sin_c = rope_angles(col_idx, GQA_HEAD_DIM // 2)
    slopes = jnp.exp2(-8.0 * jnp.arange(1, DIL_HEADS + 1, dtype=jnp.float32) / DIL_HEADS)

    for layer in range(DEPTH):
        i = layer // 2
        if layer % 2 == 0:
            z = rmsnorm_2(x, mix_norm_ab[i]) @ w_in_ab[i]
            o_a = mla_mixer(z[..., :IN_A], mla_q_norm[i], mla_kv_norm[i], mla_w_uq[i], mla_w_ukv[i],
                            cos_t, sin_t)
            o_b = dilated_mixer(z[..., IN_A:], slopes)
            x = x + jnp.concatenate([o_a, o_b], axis=-1) @ w_out_ab[i]
        else:
            x = x + gqa_axial_mixer(rmsnorm_2(x, mix_norm_c[i]), gqa_w_q[i], gqa_w_kv[i], gqa_q_norm[i],
                                    gqa_k_norm[i], gqa_w_o[i], cos_r, sin_r, cos_c, sin_c)
        x = x + swiglu(rmsnorm_2(x, ffn_norm[layer]), ffn_w_in[layer], ffn_w_out[layer])
    return rmsnorm_2(x, final_norm)


def setup_inputs(seed=0):
    out = dict(first_inputs(seed))
    for name, value in second_inputs(seed + 1).items():
        if name != "x":
            out[name + "_2"] = value
    return out


def reference(
    x, ffn1_norm, ffn1_w_gu, ffn1_w_down, mix_norm, ffn2_norm, ffn2_w_gu, ffn2_w_down, ab_w_in,
    rg_conv_w, rg_conv_b, rg_w_r, rg_b_r, rg_w_i, rg_b_i, rg_lambda, ml_conv_w, ml_conv_b,
    ml_b_i, ml_b_f, ml_norm, ab_w_out, nsa_w_in, nsa_pe_k, nsa_k_w1, nsa_k_b1, nsa_k_w2,
    nsa_pe_v, nsa_v_w1, nsa_v_b1, nsa_v_w2, nsa_b_gate, nsa_w_out, final_norm, mix_norm_ab_2,
    w_in_ab_2, mla_q_norm_2, mla_kv_norm_2, mla_w_uq_2, mla_w_ukv_2, w_out_ab_2, mix_norm_c_2,
    gqa_w_q_2, gqa_w_kv_2, gqa_q_norm_2, gqa_k_norm_2, gqa_w_o_2, ffn_norm_2, ffn_w_in_2,
    ffn_w_out_2, final_norm_2,
):
    x = first_block(
        x, ffn1_norm, ffn1_w_gu, ffn1_w_down, mix_norm, ffn2_norm, ffn2_w_gu, ffn2_w_down,
        ab_w_in, rg_conv_w, rg_conv_b, rg_w_r, rg_b_r, rg_w_i, rg_b_i, rg_lambda, ml_conv_w,
        ml_conv_b, ml_b_i, ml_b_f, ml_norm, ab_w_out, nsa_w_in, nsa_pe_k, nsa_k_w1, nsa_k_b1,
        nsa_k_w2, nsa_pe_v, nsa_v_w1, nsa_v_b1, nsa_v_w2, nsa_b_gate, nsa_w_out, final_norm,
    )
    return second_block(
        x, mix_norm_ab_2, w_in_ab_2, mla_q_norm_2, mla_kv_norm_2, mla_w_uq_2, mla_w_ukv_2,
        w_out_ab_2, mix_norm_c_2, gqa_w_q_2, gqa_w_kv_2, gqa_q_norm_2, gqa_k_norm_2, gqa_w_o_2,
        ffn_norm_2, ffn_w_in_2, ffn_w_out_2, final_norm_2,
    )


_drawn_inputs = setup_inputs


def setup_inputs(seed=0):
    import zlib

    import numpy as np

    out = dict(_drawn_inputs(seed))
    spreads = {}
    factors = {'rg_b_r': 8.0,
     'rg_b_i': 8.0,
     'ml_conv_b': 6.174,
     'ml_b_i': 200.0,
     'nsa_pe_k': 8.0,
     'nsa_k_b1': 8.0,
     'nsa_v_b1': 7.851,
     'nsa_b_gate': 4.164,
     'mix_norm_ab_2': 7.399,
     'mla_q_norm_2': 8.0,
     'mla_kv_norm_2': 8.0,
     'mix_norm_c_2': 8.0,
     'gqa_q_norm_2': 8.0,
     'gqa_k_norm_2': 8.0,
     'ffn_norm_2': 2.8,
     'final_norm_2': 22.935}
    for name, (base, spread) in spreads.items():
        noise = np.random.default_rng([zlib.crc32(name.encode()), seed]).standard_normal(out[name].shape)
        drawn = base * np.exp(spread * noise) if base else spread * noise
        out[name] = __import__('jax').numpy.asarray(drawn.astype(out[name].dtype))
    for name, factor in factors.items():
        out[name] = (out[name] * factor).astype(out[name].dtype)
    return out
```

```python
from contextlib import ExitStack, contextmanager

import numpy as np

import concourse.bass as bass
from concourse import mybir

F32 = mybir.dt.float32
F32R = mybir.dt.float32r
ARENA = 26800
ACT = mybir.ActivationFunctionType
ALU = mybir.AluOpType
AX = mybir.AxisListType.X
ds = bass.ds

P = 128
T = 512
D = 1024
KD = D // P
D_FF = 2816
KF = D_FF // P
EPS = 1e-6
LEAD = 2048
SLOT = 4096
NSLOT = 2
UNIT = KF // 2 * P
NEG = -1e30
BIG = 1e30

DIL_SLOTS, DIL_GROUPS, DIL_CLASSES = 4, 3, 4
N_CMP = (T - 32) // 16 + 1


TABLES = {
    "all": ["ident", "ones"],
    "ab": ["future", "sel4"],
    "nsa": ["causal", "window", "cmp_add", "cmp_mul"],
    "m2": ["dist0", "dist1", "dist2", "slopes", "mla_cos", "mla_sin", "mla_rot"],
    "gqa": ["gqa_cos", "gqa_sin", "gqa_rot", "ones64"],
}


def rope_tables(pos, dim):
    freqs = (np.float32(10000.0) ** (-np.arange(0, dim, 2, dtype=np.float32) / np.float32(dim))).astype(np.float32)
    ang = pos.astype(np.float32)[:, None] * freqs[None, :]
    return np.cos(ang).astype(np.float32).T, np.sin(ang).astype(np.float32).T


def rotation(width, starts, half):
    m = np.zeros((P, width), np.float32)
    for s in starts:
        for i in range(half):
            m[s + half + i, s + i] = -1.0
            m[s + i, s + half + i] = 1.0
    return m


def make_tables():
    q = np.arange(P)[:, None]
    k = np.arange(P)[None, :]
    pos = np.arange(T)
    t = {}
    t["ident"] = np.eye(P)
    t["ones"] = np.ones((P, P))
    t["ones64"] = (q // 64 == k // 64) * 1.0
    t["causal"] = np.where(k <= q, 0.0, NEG)
    t["window"] = np.concatenate([np.where(k > q, 0.0, NEG), np.zeros((P, P)), np.where(k <= q, 0.0, NEG)], 1)
    t["future"] = np.tile(np.where(q <= k, 0.0, BIG), (1, 4))
    ok = np.concatenate([(np.arange(N_CMP) * 16 + 31)[None, :] <= (P * i + q) for i in range(4)], 1)
    t["cmp_add"] = np.where(ok, 0.0, NEG)
    t["cmp_mul"] = ok * 1.0
    near = []
    for c in range(DIL_CLASSES):
        u = (4 * k + np.arange(4)[:, None, None])
        dist = np.abs(4 * q[None] + c - u)
        near.append(np.where(dist <= 64, dist, 1e33).transpose(1, 0, 2).reshape(P, T))
    t["dist0"] = np.concatenate(near, 1)
    t["dist1"] = np.where(np.abs(q - k) <= 64, 4 * np.abs(q - k), 1e33)
    t["dist2"] = np.where((q - k) % 4 == 0, 4 * np.abs(q - k), 1e33)
    n = np.arange(1, DIL_SLOTS * DIL_GROUPS + 1, dtype=np.float32)
    t["slopes"] = np.tile(-np.exp2(np.float32(-8.0) * n / np.float32(12.0)), (P, 1))
    c, s = rope_tables(pos, 32)
    full = np.zeros((2, P, T), np.float32)
    full[0, :64] = 1.0
    full[0, 64:96], full[1, 64:96] = np.tile(c, (2, 1)), np.tile(s, (2, 1))
    t["mla_cos"], t["mla_sin"] = full
    cr, sr = rope_tables(pos // 64, 32)
    cc, sc = rope_tables(pos % 64, 32)
    t["gqa_cos"] = np.concatenate([cr, cr, cc, cc] * 2, 0)
    t["gqa_sin"] = np.concatenate([sr, sr, sc, sc] * 2, 0)
    t["mla_rot"] = rotation(96, [64], 16)
    t["gqa_rot"] = rotation(P, [0, 32, 64, 96], 16)
    t["sel4"] = np.concatenate([np.eye(4), np.zeros((P - 4, 4))], 0)
    t = {name: np.ascontiguousarray(a, np.float32) for name, a in t.items()}
    return {stage: {n: t[n] for n in names} for stage, names in TABLES.items()}


def offsets(parts):
    at, out = 0, {}
    for name, a in parts.items():
        out[name] = (at, a.shape[1])
        at += a.shape[1]
    return out, at


def m_tiles(w, width=P):
    k, m = w.shape
    return w.reshape(k // P, P, m // width, width).transpose(2, 1, 0, 3).reshape(m // width, P, -1)


def cols(w, at, width):
    return m_tiles(w[:, at:at + width], width)[0]


def twice(w, at, width):
    return m_tiles(np.concatenate([w[:, at:at + width]] * 2, 1))[0]


def column(v):
    return v.reshape(-1, P).T


def padded(v):
    v = v.reshape(v.shape[0], -1)
    out = np.zeros((P, v.shape[1]), v.dtype)
    out[:v.shape[0]] = v
    return out


def lay_out(i):
    w = {}
    gu, down = [], []
    for a, b in [(i["ffn1_w_gu"][0], i["ffn1_w_down"][0]), (i["ffn2_w_gu"][0], i["ffn2_w_down"][0]),
                 (i["ffn1_w_gu"][1], i["ffn1_w_down"][1]), (i["ffn2_w_gu"][1], i["ffn2_w_down"][1]),
                 (i["ffn_w_in_2"][0], i["ffn_w_out_2"][0]), (i["ffn_w_in_2"][1], i["ffn_w_out_2"][1])]:
        gu.append(np.concatenate([m_tiles(a[:, :D_FF]), m_tiles(a[:, D_FF:])], 2))
        down.append(m_tiles(b))
    w["gate_up"], w["down"] = np.concatenate(gu), np.concatenate(down)

    ab = i["ab_w_in"][0]
    w["ab_gates"] = np.concatenate([cols(ab, 3072, 4), cols(ab, 3076, 4)], 1)[None]
    rg, ml = [], []
    for t in range(4):
        pair = []
        for name in ("rg_w_r", "rg_w_i"):
            z = np.zeros((P, P), ab.dtype)
            z[:64, :64], z[64:, 64:] = i[name][0, 2 * t], i[name][0, 2 * t + 1]
            pair.append(z)
        rg.append(np.concatenate([cols(ab, P * t, P), *pair], 1))
        rg.append(padded_free(cols(ab, 512 + P * t, P), 1280))
        ml.append(np.concatenate([cols(ab, 1024 + P * t, P), cols(ab, 1536 + P * t, P)], 1))
        ml.append(np.concatenate([cols(ab, 2048 + P * t, P), cols(ab, 2560 + P * t, P)], 1))
    w["rg"], w["ml"] = np.stack(rg), np.stack(ml)
    w["ab_out"] = m_tiles(i["ab_w_out"][0])

    ns = i["nsa_w_in"][0]
    w["nsa_gates"] = cols(ns, 2560, 48)[None]
    w["nsa_w1"] = np.stack([i[n][0].reshape(16, P, 256).transpose(1, 0, 2).reshape(P, -1) for n in ("nsa_k_w1", "nsa_v_w1")])
    a, b = [], []
    for g in range(4):
        kv = [1024 + 256 * j + 64 * g for j in range(6)]
        a.append(np.concatenate([cols(ns, 256 * g, P), cols(ns, 256 * g + P, P), twice(ns, kv[2], 64), twice(ns, kv[4], 64)], 1))
        both = np.concatenate([ns[:, kv[3]:kv[3] + 64], ns[:, kv[5]:kv[5] + 64]], 1)
        b.append(np.concatenate([twice(ns, kv[0], 64), twice(ns, kv[1], 64), m_tiles(both)[0]], 1))
    w["nsa_a"], w["nsa_b"] = np.stack(a), np.stack(b)
    w["nsa_out"] = m_tiles(i["nsa_w_out"][0])

    z = i["w_in_ab_2"][0]
    w["mla_z"] = np.stack([np.concatenate([cols(z, P * t, P) for t in range(3)], 1),
                           padded_free(np.concatenate([cols(z, 384, P), cols(z, 512, P), cols(z, 576, 96)], 1), 3072)])
    uq, ukv = i["mla_w_uq_2"][0], i["mla_w_ukv_2"][0]
    w["mla_q"] = np.stack([np.concatenate([cols(uq[:, 2 * h + e], 0, 96) for e in range(2)], 1) for h in range(4)])
    w["mla_kv"] = np.stack([np.concatenate(
        [cols(ukv[:, 2 * h + e], 0, 64) for e in range(2)] +
        [m_tiles(np.concatenate([ukv[:, 2 * h, 64:], ukv[:, 2 * h + 1, 64:]], 1))[0]], 1) for h in range(4)])
    qk, v = [], []
    for s in range(2):
        for j in range(2):
            qk.append(np.concatenate([cols(z, 672 + 768 * j + 256 * g + P * s, P) for g in range(3)], 1))
        v.append(np.concatenate([z[:, 672 + 1536 + 256 * g + P * s:][:, :P] for g in range(3)], 1))
    w["dil_qk"] = np.stack(qk)
    w["dil_va"] = np.stack([cols(u, 0, 256) for u in v])
    w["dil_vb"] = np.stack([cols(u, 256, P) for u in v])
    w["ab2_out"] = m_tiles(i["w_out_ab_2"][0])

    gq, gkv = i["gqa_w_q_2"][0], i["gqa_w_kv_2"][0]
    w["gqa_qk"] = np.stack([np.concatenate([cols(gq, 256 * g, P), cols(gq, 256 * g + P, P), twice(gkv, 64 * g, 64)], 1) for g in range(4)])
    w["gqa_v"] = np.stack([cols(gkv, 256 + 64 * g, 64) for g in range(4)])
    w["gqa_out"] = m_tiles(i["gqa_w_o_2"][0])

    c = {}
    gains = [i["ffn1_norm"][0], i["mix_norm"][0], i["ffn2_norm"][0], i["ffn1_norm"][1], i["mix_norm"][1], i["ffn2_norm"][1],
             i["final_norm"], i["mix_norm_ab_2"][0], i["ffn_norm_2"][0], i["mix_norm_c_2"][0], i["ffn_norm_2"][1], i["final_norm_2"]]
    c["gains"] = np.concatenate([column(g) for g in gains], 1)
    taps = lambda a: a.reshape(4, -1, P).transpose(2, 1, 0).reshape(P, -1)
    c["rg_taps"] = taps(i["rg_conv_w"][0])
    c["rg_cb"], c["rg_br"], c["rg_bi"], c["rg_lam"] = (column(i[n][0]) for n in ("rg_conv_b", "rg_b_r", "rg_b_i", "rg_lambda"))
    c["ml_taps"] = taps(i["ml_conv_w"][0])
    c["ml_cb"], c["ml_norm"] = column(i["ml_conv_b"][0]), column(i["ml_norm"][0])
    c["ml_bi"], c["ml_bf"] = padded(i["ml_b_i"][0]), padded(i["ml_b_f"][0])
    c["nsa_pe"] = np.concatenate([i[n][0].reshape(16, P).T for n in ("nsa_pe_k", "nsa_pe_v")], 1)
    c["nsa_b1"] = np.concatenate([column(i[n][0]) for n in ("nsa_k_b1", "nsa_v_b1")], 1)
    k2 = i["nsa_k_w2"][0]
    c["nsa_k_w2"] = m_tiles(np.concatenate([k2, k2], 1))[0]
    c["nsa_v_w2"] = cols(i["nsa_v_w2"][0], 0, 64)
    c["nsa_bg"] = padded(i["nsa_b_gate"][0][None])
    c["mla_gq"], c["mla_gkv"] = column(i["mla_q_norm_2"][0]), column(i["mla_kv_norm_2"][0])
    c["gqa_gq"] = np.concatenate([i["gqa_q_norm_2"][0]] * 2)[:, None]
    c["gqa_gk"] = np.concatenate([i["gqa_k_norm_2"][0]] * 2)[:, None]
    return w, c


def padded_free(a, width):
    return np.concatenate([a, np.zeros((P, width - a.shape[1]), a.dtype)], 1)


class Count:

    def __init__(self, name, known, seen, by, lead):
        self.name, self.known, self.seen, self.by, self.lead = name, known, seen, by, lead
        self.count, self.loop = 0, None

    def mark(self, what=None):
        self.count += self.by
        if what is not None:
            assert (self.name, what) not in self.seen, what
            self.seen[self.name, what] = (self.count, self.loop)
        return self.by

    def per(self, loop):
        return self.known.get((self.name, "per", loop), (1, 1))

    def at(self, what, it, loop, back):
        assert not self.known or (self.name, what) in self.known, (self.name, what)
        count, within = self.known.get((self.name, what), (1, None))
        if within is None:
            return self.lead + count
        per, trips = self.per(within)
        if it is None or within != loop:
            return self.lead + count + per * (trips - 1)
        return it * per + (self.lead + count - back * per)


class Engine:

    def __init__(self, eng, own, counts, more=()):
        self.eng, self.own, self.counts = eng, own, counts
        self.raised = ([own] if own else []) + list(more)
        self.it = self.loop_tag = None
        self.chunk = 0

    def mark(self, what=None):
        return self.own.mark(what)

    def now(self):
        if self.it is None:
            return self.own.lead + self.own.count
        return self.it * self.own.per(self.loop_tag)[0] + (self.own.lead + self.own.count)

    def at(self, who, what, back=0):
        return self.counts[who].at(what, self.it, self.loop_tag, back)

    def slot(self):
        return self.chunk % NSLOT

    def loaded(self):
        self.chunk += 1
        return self.counts[f"slot{(self.chunk - 1) % NSLOT}"].mark(("chunk", self.chunk - 1))

    def chunk_loaded(self):
        return self.at(f"slot{self.slot()}", ("chunk", self.chunk))

    def used(self):
        self.chunk += 1
        return self.own.mark(("chunk", self.chunk - 1))

    @contextmanager
    def loop(self, trips, tag):
        base = {c.name: c.count for c in self.raised}
        with self.eng.Fori(0, trips) as it:
            self.it, self.loop_tag = it, tag
            for c in self.raised:
                c.loop = tag
            yield it
        for c in self.raised:
            per = c.count - base[c.name]
            c.seen[c.name, "per", tag] = (per, trips)
            c.count = base[c.name] + per * trips
            c.loop = None
        self.it = self.loop_tag = None


def build(nc, arrays, columns_at, tables_at, out, marks, stages=None):
    seen = {}
    with ExitStack() as ctx:
        sb = lambda name, n, parts=P: ctx.enter_context(nc.sbuf_tensor(name, [parts, n], F32))
        x = sb("x", KD * T)[:, :].rearrange("p (k t) -> p k t", k=KD)
        ring = sb("ring", NSLOT * SLOT)[:, :].rearrange("p (s n) -> p s n", s=NSLOT)
        colbuf = sb("colbuf", sum(n for _, n in columns_at.values()))
        tabbuf = {"all": sb("table_all", tables_at["all"][1])}
        rstd = sb("rstd", T)
        with ExitStack() as room:
            xn = room.enter_context(nc.sbuf_tensor("xn", [P, KD * T], F32))[:, :].rearrange("p (k t) -> p k t", k=KD)
            arena = room.enter_context(nc.sbuf_tensor("arena", [P, ARENA], F32))
            shared = room.enter_context(nc.sbuf_tensor("tables", [P, max(n for s, (_, n) in tables_at.items() if s != "all")], F32))
        tabbuf.update({stage: shared for stage in tables_at if stage != "all"})
        room = ctx.enter_context(ExitStack())
        fr = lambda name, n, k: room.enter_context(nc.sbuf_tensor(name, [P, n * k], F32R))[:, :].rearrange("p (k t) -> p k t", k=k)
        x_hi, x_lo = fr("x_hi", T, KD), fr("x_lo", T, KD)
        hid_hi, hid_lo = fr("hid_hi", T, KF), fr("hid_lo", T, KF)
        w_hi, w_lo = fr("w_hi", UNIT, 2), fr("w_lo", UNIT, 2)
        work = room.enter_context(nc.sbuf_tensor("work", [P, 4 * T], F32))[:, :].rearrange("p (k t) -> p k t", k=4)
        psum = ctx.enter_context(nc.psum_tensor("psum", [P, 8, T], F32))
        bank = lambda b: psum[:, b, :]

        def col(name, a=0, n=None):
            at, width = columns_at[name]
            return colbuf[:, at + a:at + a + (width - a if n is None else n)]

        def tab(name, a=0, n=None):
            stage = next(s for s, names in TABLES.items() if name in names)
            at, width = tables_at[stage][0][name]
            return tabbuf[stage][:, at + a:at + a + (width - a if n is None else n)]

        def dyn_col(name, it, step, a=0, n=1):
            at, _ = columns_at[name]
            return colbuf[:, ds(it * step + (at + a), n)]

        sem = lambda name: ctx.enter_context(nc.semaphore(name))
        tensor_done, scalar_done, vector_done = sem("tensor_done"), sem("scalar_done"), sem("vector_done")
        slot_loaded = [sem(f"slot{k}_loaded") for k in range(NSLOT)]
        consts_loaded, x_loaded, w1_loaded, stored = (sem(n) for n in ("consts_loaded", "x_loaded", "w1_loaded", "stored"))
        tables_loaded = sem("tables_loaded")
        unit_hi, unit_ready, unit_used, silu_ready, hidden_ready, x_updated = (
            sem(n) for n in ("unit_hi", "unit_ready", "unit_used", "silu_ready", "hidden_ready", "x_updated"))
        counts = {n: Count(n, marks, seen, 1, LEAD) for n in ("tensor", "scalar", "vector")}
        counts.update({n: Count(n, marks, seen, 16, 0) for n in ("slot0", "slot1")})

        carve_at = [0]

        def carve_reset(to=0):
            carve_at[0] = to

        def carve(n, *shape):
            a = arena[:, carve_at[0]:carve_at[0] + n * int(np.prod(shape or (1,)))]
            carve_at[0] += n * int(np.prod(shape or (1,)))
            assert carve_at[0] <= ARENA, carve_at[0]
            if shape:
                names = "abcd"[:len(shape) + 1]
                sizes = {c: s for c, s in zip(names, (n, *shape))}
                a = a.rearrange(f"p ({' '.join(names)}) -> p {' '.join(names)}", **sizes)
            return a


        def load(sp, src, n, trip=None):
            k = sp.chunk
            if k - NSLOT >= sp.base:
                sp.eng.wait_ge(tensor_done, sp.at("tensor", ("chunk", k - NSLOT)))
            if trip is not None and k - sp.first < NSLOT:
                sp.eng.wait_ge(tensor_done, sp.at("tensor", ("chunk", k - NSLOT + trip), back=1))
            sp.eng.dma_start(ring[:, k % NSLOT, 0:n], src).then_inc(slot_loaded[k % NSLOT], sp.loaded())

        def product(out, w, rhs, n, width=P, at=0, tile=None):
            for k in range(n):
                ins = nc.tensor.matmul(out, w[:, at + k * width:at + (k + 1) * width], rhs[k],
                                       start=k == 0, stop=k == n - 1)
            return ins

        xn_tiles = [xn[:, k, :] for k in range(KD)]
        ones, ident = tab("ones"), tab("ident")

        def start_sync(sp):
            sp.eng.dma_start(tabbuf["all"][:, :], arrays["t_all"]).then_inc(consts_loaded, 16)
            sp.eng.dma_start(colbuf[:, :], arrays["columns"]).then_inc(consts_loaded, 16)
            for i in range(4):
                sp.eng.dma_start(x_rows[:, i, :], arrays["x"][P * i:P * (i + 1), :]).then_inc(x_loaded, 16)

        x_rows = arena[:, 0:4 * D].rearrange("p (i n) -> p i n", i=4)
        all_consts = 16 * 2

        def start_tensor(pe):
            pe.eng.wait_ge(consts_loaded, all_consts)
            pe.eng.wait_ge(x_loaded, 16 * 4)
            for k in range(KD):
                for i in range(4):
                    ins = nc.tensor.transpose(bank(k)[:, P * i:P * (i + 1)], x_rows[:, i, P * k:P * (k + 1)], ident)
                ins.then_inc(tensor_done, pe.mark(("x", k)))

        def start_vector(dve):
            dve.eng.wait_ge(consts_loaded, all_consts)
            for k in range(KD):
                dve.eng.wait_ge(tensor_done, dve.at("tensor", ("x", k)))
                nc.vector.tensor_copy(x[:, k, :], bank(k)).then_inc(vector_done, dve.mark("x" if k == KD - 1 else None))

        def norm_scalar(act, tag, src, dst, n, ready):
            act.eng.wait_ge(*ready)
            for k in range(n):
                nc.scalar.activation(dst[k], src[k], ACT.Square).then_inc(scalar_done, act.mark((tag, "square", k)))
            act.eng.wait_ge(vector_done, act.at("vector", (tag, "mean")))
            nc.scalar.activation(rstd[:, :], rstd[:, :], ACT.Sqrt).then_inc(scalar_done, act.mark((tag, "rstd")))

        def norm_tensor(pe, tag, dst, n, b=0):
            for k in range(n):
                pe.eng.wait_ge(scalar_done, pe.at("scalar", (tag, "square", k)))
                ins = nc.tensor.matmul(bank(b), ones, dst[k], start=k == 0, stop=k == n - 1)
            ins.then_inc(tensor_done, pe.mark((tag, "sum")))

        def norm_vector(dve, tag, src, dst, n, gain, b=0):
            dve.eng.wait_ge(tensor_done, dve.at("tensor", (tag, "sum")))
            dve.eng.wait_ge(vector_done, dve.now())
            nc.vector.tensor_scalar(rstd[:, :], bank(b), 1.0 / (n * P), EPS, ALU.mult, ALU.add).then_inc(vector_done, dve.mark())
            dve.eng.wait_ge(vector_done, dve.now())
            nc.vector.reciprocal(rstd[:, :], rstd[:, :]).then_inc(vector_done, dve.mark((tag, "mean")))
            dve.eng.wait_ge(vector_done, dve.now())
            dve.eng.wait_ge(scalar_done, dve.at("scalar", (tag, "rstd")))
            for k in range(n):
                nc.vector.scalar_tensor_tensor(dst[k], src[k], gain(k), rstd[:, :], ALU.mult, ALU.mult).then_inc(vector_done, dve.mark((tag, "normed", k)))

        x_tiles = [x[:, k, :] for k in range(KD)]

        def model_norm(n):
            return lambda k: col("gains", n * KD + k, 1)

        UP, DOWN = 2 * KF, 2 * KD
        UNITS = UP + DOWN

        def place_of(h, j, ahead=0):
            return (h + (j + ahead) // 2, (j + ahead) % 2)

        def unit_size(up):
            return (KD if up else KF // 2) * P

        def ffn_slot(e, j):
            return (e.chunk + j) % 2

        def ffn_slot_loaded(e, tag, h, j):
            return h * 16 + (16 + e.at(f"slot{ffn_slot(e, j)}", ("base", tag)))

        def ffn_sync(sp, tag, n, after_mixer):
            if after_mixer:
                for k in (1, 2):
                    sp.eng.wait_ge(tensor_done, sp.at("tensor", ("chunk", sp.chunk - k)))
            for k in range(2):
                c = counts[f"slot{k}"]
                seen[c.name, ("base", tag)] = (c.count, None)
            with sp.eng.Fori(0, KF // 2) as it:
                for j in range(2):
                    sp.eng.wait_ge(unit_ready, it * 4 + (UNITS * n + 2 * j + 2))
                    sp.eng.dma_start(ring[:, ffn_slot(sp, j), 0:2 * unit_size(True)],
                                     arrays["gate_up"][ds(it * 2 + (KF * n + j), 1)].rearrange("a p n -> (a p) n")).then_inc(slot_loaded[ffn_slot(sp, j)], 16)
            with sp.eng.Fori(0, KD // 2) as it:
                for j in range(2):
                    sp.eng.wait_ge(unit_ready, it * 4 + (UNITS * n + UP + 2 * j + 2))
                    sp.eng.dma_start(ring[:, ffn_slot(sp, j), 0:2 * unit_size(False)],
                                     arrays["down"][ds(it * 2 + (KD * n + j), 1)].rearrange("a p n -> (a p) n")).then_inc(slot_loaded[ffn_slot(sp, j)], 16)
            for k in range(2):
                counts[f"slot{k}"].count += 16 * UNITS // 4
            sp.chunk += UNITS // 2

        def split_product(out, b, hi, lo, tiles, start, stop):
            for m, k in enumerate(tiles):
                wh, wl = w_hi[:, b, P * m:P * (m + 1)], w_lo[:, b, P * m:P * (m + 1)]
                nc.tensor.matmul(out, wh, hi[:, k, :], start=start and m == 0, stop=False)
                nc.tensor.matmul(out, wh, lo[:, k, :], start=False, stop=False)
                ins = nc.tensor.matmul(out, wl, hi[:, k, :], start=False, stop=stop and m == len(tiles) - 1)
            return ins

        def ffn_tensor(pe, tag, n):
            for k in range(KD):
                pe.eng.wait_ge(scalar_done, pe.at("scalar", (tag, "square", k)))
                nc.tensor.matmul(bank(7), ones, work[:, k % 4, :], start=k == 0, stop=k == KD - 1).then_inc(
                    tensor_done, pe.mark((tag, "sum") if k == KD - 1 else (tag, "square used", k)))
            pe.eng.wait_ge(vector_done, pe.at("vector", (tag, "normed")))
            with pe.eng.Fori(0, KF // 2) as it:
                for j in range(2):
                    pe.eng.wait_ge(hidden_ready, it * 2 + (KF * n + j + 1))
                    pe.eng.wait_ge(unit_ready, it * 4 + (UNITS * n + 2 * j + 5))
                    split_product(bank(2 * j), 0, x_hi, x_lo, range(KD), True, True).then_inc(unit_used, 1)
                    pe.eng.wait_ge(unit_ready, it * 4 + (UNITS * n + 2 * j + 6))
                    split_product(bank(2 * j + 1), 1, x_hi, x_lo, range(KD), True, True).then_inc(unit_used, 1)
            pe.eng.wait_ge(hidden_ready, KF * (n + 1) + 2)
            with pe.eng.Fori(0, KD // 2) as it:
                for j in range(2):
                    pe.eng.wait_ge(x_updated, it * 2 + (KD * n + j + 1))
                    pe.eng.wait_ge(unit_ready, it * 4 + (UNITS * n + UP + 2 * j + 5))
                    split_product(bank(4 + j), 0, hid_hi, hid_lo, range(KF // 2), True, False).then_inc(unit_used, 1)
                    pe.eng.wait_ge(unit_ready, it * 4 + (UNITS * n + UP + 2 * j + 6))
                    split_product(bank(4 + j), 1, hid_hi, hid_lo, range(KF // 2, KF), False, True).then_inc(unit_used, 1)
            pe.chunk += UNITS // 2

        def ffn_scalar(act, tag, n, ready):
            act.eng.wait_ge(*ready)
            for k in range(KD):
                if k >= 4:
                    act.eng.wait_ge(tensor_done, act.at("tensor", (tag, "square used", k - 4)))
                nc.scalar.activation(work[:, k % 4, :], x[:, k, :], ACT.Square).then_inc(scalar_done, act.mark((tag, "square", k)))

            def split_hi(h, j, up):
                for b in range(2):
                    if b == 0:
                        act.eng.wait_ge(slot_loaded[ffn_slot(act, j)], ffn_slot_loaded(act, tag, h, j))
                    act.eng.wait_ge(unit_used, h * 4 + (UNITS * n + 2 * j + b + 1))
                    nc.scalar.copy(w_hi[:, b, 0:unit_size(up)],
                                   ring[:, ffn_slot(act, j), unit_size(up) * b:unit_size(up) * (b + 1)]).then_inc(unit_hi, 1)
                    if b == 0:
                        yield

            def up_step(h, j, last=False):
                ahead = split_hi(*place_of(h, j, 1), up=not last)
                next(ahead)
                act.eng.wait_ge(unit_used, h * 4 + (UNITS * n + 2 * j + 3))
                act.eng.wait_ge(hidden_ready, h * 2 + (KF * n + j + 1))
                nc.scalar.activation(work[:, j, :], bank(2 * j), ACT.Silu).then_inc(silu_ready, 1)
                for _ in ahead:
                    pass

            for _ in split_hi(0, 0, True):
                pass
            act.eng.wait_ge(vector_done, act.at("vector", (tag, "mean")))
            nc.scalar.activation(rstd[:, :], rstd[:, :], ACT.Sqrt).then_inc(scalar_done, act.mark((tag, "rstd")))
            for k in range(KD):
                act.eng.wait_ge(vector_done, act.at("vector", (tag, "y", k)))
                nc.scalar.copy(x_hi[:, k, :], work[:, k % 4, :]).then_inc(scalar_done, act.mark((tag, "x_hi", k)))
            with act.eng.Fori(0, KF // 2 - 1) as it:
                for j in range(2):
                    up_step(it, j)
            up_step(KF // 2 - 1, 0)
            up_step(KF // 2 - 1, 1, last=True)
            with act.eng.Fori(0, KD // 2 - 1) as it:
                for j in range(2):
                    for _ in split_hi(*place_of(it + KF // 2, j, 1), up=False):
                        pass
            for _ in split_hi(KF // 2 + KD // 2 - 1, 1, up=False):
                pass
            act.chunk += UNITS // 2

        def ffn_vector(dve, tag, n, gain, scale):
            def split_lo(h, j, up):
                for b in range(2):
                    dve.eng.wait_ge(unit_hi, h * 4 + (UNITS * n + 2 * j + b + 1))
                    size = unit_size(up)
                    nc.vector.tensor_tensor(w_lo[:, b, 0:size], ring[:, ffn_slot(dve, j), size * b:size * (b + 1)],
                                            w_hi[:, b, 0:size].bitcast(F32), ALU.subtract).then_inc(unit_ready, 1)

            def up_step(h, j, last=False):
                split_lo(*place_of(h, j, 1), up=not last)
                dve.eng.wait_ge(silu_ready, h * 2 + (KF * n + j + 1))
                dve.eng.wait_ge(unit_used, h * 4 + (UNITS * n + 2 * j + 4))
                dve.eng.wait_ge(hidden_ready, h * 2 + (KF * n + j + 1))
                prod = work[:, 2 + j, :]
                tile = lambda t: (t[:, ds(h * 2 + j, 1), :]).rearrange("p a t -> p (a t)")
                nc.vector.tensor_tensor(prod, work[:, j, :], bank(2 * j + 1), ALU.mult).then_inc(vector_done, dve.mark())
                dve.eng.wait_ge(vector_done, dve.now())
                nc.vector.tensor_copy(tile(hid_hi), prod).then_inc(vector_done, dve.mark())
                dve.eng.wait_ge(vector_done, dve.now())
                nc.vector.tensor_tensor(tile(hid_lo), prod, tile(hid_hi).bitcast(F32), ALU.subtract).then_inc(hidden_ready, 1)

            def down_step(h, j, last=False):
                if not last:
                    split_lo(*place_of(h + KF // 2, j, 1), up=False)
                dve.eng.wait_ge(unit_used, h * 4 + (UNITS * n + UP + 2 * j + 4))
                tile = x[:, ds(h * 2 + j, 1), :].rearrange("p a t -> p (a t)")
                nc.vector.scalar_tensor_tensor(tile, bank(4 + j), scale, tile, ALU.mult, ALU.add).then_inc(x_updated, 1)

            dve.eng.wait_ge(tensor_done, dve.at("tensor", (tag, "sum")))
            nc.vector.tensor_scalar(rstd[:, :], bank(7), 1.0 / D, EPS, ALU.mult, ALU.add).then_inc(vector_done, dve.mark())
            dve.eng.wait_ge(vector_done, dve.now())
            nc.vector.reciprocal(rstd[:, :], rstd[:, :]).then_inc(vector_done, dve.mark((tag, "mean")))
            split_lo(0, 0, True)
            dve.eng.wait_ge(scalar_done, dve.at("scalar", (tag, "rstd")))
            for k in range(KD + 1):
                if k < KD:
                    if k >= 4:
                        dve.eng.wait_ge(vector_done, dve.at("vector", (tag, "x_lo", k - 4)))
                    nc.vector.scalar_tensor_tensor(work[:, k % 4, :], x[:, k, :], col("gains", gain * KD + k, 1), rstd[:, :],
                                                   ALU.mult, ALU.mult).then_inc(vector_done, dve.mark((tag, "y", k)))
                if k >= 1:
                    dve.eng.wait_ge(scalar_done, dve.at("scalar", (tag, "x_hi", k - 1)))
                    dve.eng.wait_ge(vector_done, dve.at("vector", (tag, "y", k - 1)))
                    nc.vector.tensor_tensor(x_lo[:, k - 1, :], work[:, (k - 1) % 4, :], x_hi[:, k - 1, :].bitcast(F32),
                                            ALU.subtract).then_inc(vector_done, dve.mark((tag, "normed") if k == KD else (tag, "x_lo", k - 1)))
            with dve.loop(KF // 2 - 1, (tag, "up")) as it:
                for j in range(2):
                    up_step(it, j)
            up_step(KF // 2 - 1, 0)
            up_step(KF // 2 - 1, 1, last=True)
            with dve.eng.Fori(0, KD // 2 - 1) as it:
                for j in range(2):
                    down_step(it, j)
            down_step(KD // 2 - 1, 0)
            down_step(KD // 2 - 1, 1, last=True)
            dve.chunk += UNITS // 2

        def out_sync(sp, tag, name, n):
            with sp.loop(KD // 2, (tag, "out")) as it:
                sp.first = sp.chunk
                for j in range(2):
                    load(sp, arrays[name][ds(it * 2 + j, 1)].rearrange("a p n -> (a p) n"), n * P, 2)

        def out_tensor(pe, tag, mixed, n):
            with pe.loop(KD // 2, (tag, "out")):
                for j in range(2):
                    pe.eng.wait_ge(slot_loaded[pe.slot()], pe.chunk_loaded())
                    w = ring[:, pe.slot(), :]
                    pe.eng.wait_ge(vector_done, pe.at("vector", (tag, "x", j), back=1))
                    product(bank(j), w, mixed, n).then_inc(tensor_done, pe.used())

        def out_vector(dve, tag):
            first = dve.chunk
            with dve.loop(KD // 2, (tag, "out")) as it:
                for j in range(2):
                    dve.eng.wait_ge(tensor_done, dve.at("tensor", ("chunk", first + j)))
                    tile = x[:, ds(it * 2 + j, 1), :].rearrange("p a t -> p (a t)")
                    nc.vector.tensor_tensor(tile, bank(j), tile, ALU.add).then_inc(vector_done, dve.mark((tag, "x", j)))
            dve.chunk += 2

        y_rows = arena[:, 0:4 * D].rearrange("p (i n) -> p i n", i=4)

        def end_tensor(pe, ready):
            pe.eng.wait_ge(vector_done, pe.at("vector", ready))
            for i in range(4):
                for h in range(2):
                    for k in range(4):
                        ins = nc.tensor.transpose(bank(2 * i + h)[:, P * k:P * (k + 1)],
                                                  xn[:, 4 * h + k, P * i:P * (i + 1)], ident)
                    ins.then_inc(tensor_done, pe.mark(("y", i, h)))

        def end_vector(dve):
            for i in range(4):
                for h in range(2):
                    dve.eng.wait_ge(tensor_done, dve.at("tensor", ("y", i, h)))
                    nc.vector.tensor_copy(y_rows[:, i, 512 * h:512 * (h + 1)], bank(2 * i + h)).then_inc(vector_done, dve.mark(("y", i, h)))

        def end_sync(sp):
            for i in range(4):
                sp.eng.wait_ge(vector_done, sp.at("vector", ("y", i, 1)))
                sp.eng.dma_start(out[P * i:P * (i + 1), :], y_rows[:, i, :]).then_inc(stored, 16)
            sp.eng.wait_ge(stored, 16 * 4)

        MIXERS = {}

        CH = 128
        NC_ = T // CH
        carve_reset()
        ab_mixed = carve(8, T)
        ab_mixed_tiles = [ab_mixed[:, k, :] for k in range(8)]
        rows = carve(14, T)
        ROW = {n: i for i, n in enumerate(["li", "f", "af", "lf", "b", "c", "M", "m", "sc", "wk", "one", "em", "t0", "t1"])}
        row = lambda n, a=0, w=T: rows[0:4, ROW[n], a:a + w]
        spread = carve(3, 4, T)
        rcol = carve(2, NC_, 4)
        lam = carve(12, 4)
        lamx = lambda i: lam[:, i, :]
        small0 = carve_at[0]
        rg = carve(10, T)
        RG = {n: i for i, n in enumerate(["conv", "r", "ig", "a", "t", "u", "gelu", "h", "v", "w"])}
        rgt = lambda n: rg[:, RG[n], :]
        carve_reset(small0)
        ml = carve(12, T)
        ML = {n: i for i, n in enumerate(["q", "k", "qs", "E", "P", "kw", "ho", "o", "den", "sq", "rs", "cq"])}
        mlt = lambda n: ml[:, ML[n], :]
        mv = carve(NC_, 2 * P)
        state = carve(3, 2 * P)

        def ab_sync(sp):
            load(sp, arrays["ab_gates"][0], 64)
            with sp.loop(4, "rg") as it:
                sp.first = sp.chunk
                for j, n in enumerate((1280, 1024)):
                    load(sp, arrays["rg"][ds(it * 2 + j, 1), :, 0:n].rearrange("a p n -> (a p) n"), n, 2)
            with sp.loop(4, "ml") as it:
                sp.first = sp.chunk
                for j in range(2):
                    load(sp, arrays["ml"][ds(it * 2 + j, 1)].rearrange("a p n -> (a p) n"), 2048, 2)
            out_sync(sp, "ab", "ab_out", 8)

        def ab_tensor(pe):
            norm_tensor(pe, "ab", xn_tiles, KD)
            pe.eng.wait_ge(vector_done, pe.at("vector", ("ab", "normed", KD - 1)))
            pe.eng.wait_ge(slot_loaded[pe.slot()], pe.chunk_loaded())
            w = ring[:, pe.slot(), :]
            product(bank(1)[0:4, :], w, xn_tiles, KD, width=4).then_inc(tensor_done, pe.mark("ml i"))
            product(bank(2)[0:4, :], w, xn_tiles, KD, width=4, at=32).then_inc(tensor_done, pe.used())
            pe.eng.wait_ge(scalar_done, pe.at("scalar", "ml wk"))
            for a, n in enumerate(("c", "wk")):
                for c in range(NC_):
                    ins = nc.tensor.transpose(bank(3)[:, (a * NC_ + c) * 4:(a * NC_ + c) * 4 + 4], row(n, c * CH, CH), ident[0:4, 0:4])
            ins.then_inc(tensor_done, pe.mark("ml cols"))
            with pe.loop(4, "rg"):
                pe.eng.wait_ge(vector_done, pe.at("vector", "rg mixed", back=1))
                pe.eng.wait_ge(slot_loaded[pe.slot()], pe.chunk_loaded())
                w = ring[:, pe.slot(), :]
                product(bank(4), w, xn_tiles, KD).then_inc(tensor_done, pe.mark("rg xa"))
                pe.eng.wait_ge(vector_done, pe.at("vector", "rg conv"))
                nc.tensor.matmul(bank(6), w[:, 1024:1152], rgt("conv"), start=True, stop=True).then_inc(tensor_done, pe.mark("rg r"))
                nc.tensor.matmul(bank(7), w[:, 1152:1280], rgt("conv"), start=True, stop=True).then_inc(tensor_done, pe.used())
                pe.eng.wait_ge(slot_loaded[pe.slot()], pe.chunk_loaded())
                w = ring[:, pe.slot(), :]
                product(bank(5), w, xn_tiles, KD).then_inc(tensor_done, pe.used())
            pe.eng.wait_ge(vector_done, pe.at("vector", "rg mixed"))
            pe.eng.wait_ge(vector_done, pe.at("vector", "ml rows"))
            with pe.loop(4, "ml") as it:
                pe.eng.wait_ge(vector_done, pe.at("vector", "ml mixed", back=1))
                pe.eng.wait_ge(slot_loaded[pe.slot()], pe.chunk_loaded())
                w = ring[:, pe.slot(), :]
                product(bank(0), w, xn_tiles, KD).then_inc(tensor_done, pe.mark("ml q"))
                product(bank(1), w, xn_tiles, KD, at=1024).then_inc(tensor_done, pe.used())
                pe.eng.wait_ge(slot_loaded[pe.slot()], pe.chunk_loaded())
                w = ring[:, pe.slot(), :]
                for i in range(NC_):
                    for k in range(KD):
                        ins = nc.tensor.matmul(bank(2)[:, P * i:P * (i + 1)], xn[:, k, P * i:P * (i + 1)],
                                               w[:, P * k:P * (k + 1)], start=k == 0, stop=k == KD - 1)
                ins.then_inc(tensor_done, pe.mark("ml v"))
                product(bank(3), w, xn_tiles, KD, at=1024).then_inc(tensor_done, pe.used())
                nc.tensor.matmul(bank(4), ones[0:4, :], spread[0:4, 0, ds(it, 1), :].rearrange("p a t -> p (a t)"), start=True, stop=False)
                nc.tensor.matmul(bank(4), ident, tab("future"), start=False, stop=True).then_inc(tensor_done, pe.mark("ml M"))
                nc.tensor.matmul(bank(5), ones[0:4, :], spread[0:4, 1, ds(it, 1), :].rearrange("p a t -> p (a t)"), start=True, stop=True).then_inc(tensor_done, pe.mark("ml sc"))
                nc.tensor.matmul(bank(6), ones[0:4, :], spread[0:4, 2, ds(it, 1), :].rearrange("p a t -> p (a t)"), start=True, stop=True).then_inc(tensor_done, pe.mark("ml em"))
                pe.eng.wait_ge(scalar_done, pe.at("scalar", "ml qk silu"))
                for c in range(NC_):
                    ins = nc.tensor.matmul(bank(7)[:, c * CH:(c + 1) * CH], mlt("k")[:, c * CH:(c + 1) * CH],
                                           mlt("q")[:, c * CH:(c + 1) * CH], start=True, stop=True)
                ins.then_inc(tensor_done, pe.mark("ml s"))
                for c in range(NC_ - 1):
                    ins = nc.tensor.transpose(bank(0)[:, c * CH:(c + 1) * CH], mlt("k")[:, c * CH:(c + 1) * CH], ident)
                ins.then_inc(tensor_done, pe.mark("ml kT"))
                pe.eng.wait_ge(vector_done, pe.at("vector", "ml v"))
                pe.eng.wait_ge(vector_done, pe.at("vector", "ml kw"))
                for c in range(NC_ - 1):
                    ins = nc.tensor.matmul(bank(1 + c // 2)[:, 256 * (c % 2):256 * (c % 2) + 256],
                                           mlt("kw")[:, c * CH:(c + 1) * CH], mv[:, c, :], start=True, stop=True)
                ins.then_inc(tensor_done, pe.mark("ml state"))
                pe.eng.wait_ge(vector_done, pe.at("vector", "ml P"))
                pe.eng.wait_ge(vector_done, pe.at("vector", "ml states"))
                for c in range(NC_):
                    at = slice(c * CH, (c + 1) * CH)
                    nc.tensor.matmul(bank(4)[:, at], mv[:, c, 0:P], mlt("P")[:, at], start=True, stop=c == 0)
                    if c:
                        nc.tensor.matmul(bank(4)[:, at], state[:, c - 1, 0:P], mlt("qs")[:, at], start=False, stop=True)
                for c in range(NC_):
                    at = slice(c * CH, (c + 1) * CH)
                    ins = nc.tensor.matmul(bank(7)[:, at], ones, mlt("P")[:, at], start=True, stop=c == 0)
                    if c:
                        ins = nc.tensor.matmul(bank(7)[:, at], state[:, c - 1, P:2 * P], mlt("qs")[:, at], start=False, stop=True)
                ins.then_inc(tensor_done, pe.mark("ml den"))
                pe.eng.wait_ge(scalar_done, pe.at("scalar", "ml sq"))
                nc.tensor.matmul(bank(0), ones, mlt("sq"), start=True, stop=True).then_inc(tensor_done, pe.mark("ml ss"))
            pe.eng.wait_ge(vector_done, pe.at("vector", "ml mixed"))
            out_tensor(pe, "ab", ab_mixed_tiles, 8)

        def ab_scalar(act, ready):
            norm_scalar(act, "ab", x_tiles, xn_tiles, KD, ready)
            act.eng.wait_ge(vector_done, act.at("vector", "rg |lam|"))
            nc.scalar.activation(lamx(1), lamx(0), ACT.Exp, scale=-1.0).then_inc(scalar_done, act.mark("rg exp lam"))
            act.eng.wait_ge(vector_done, act.at("vector", "ml |f|"))
            nc.scalar.activation(row("t0"), row("af"), ACT.Exp, scale=-1.0).then_inc(scalar_done, act.mark())
            act.eng.wait_ge(scalar_done, act.now())
            nc.scalar.activation(row("t1"), row("t0"), ACT.Ln, bias=1.0).then_inc(scalar_done, act.mark("ml ln"))
            act.eng.wait_ge(vector_done, act.at("vector", "ml m"))
            nc.scalar.activation(row("sc"), row("t0"), ACT.Exp).then_inc(scalar_done, act.mark("ml sc"))
            nc.scalar.activation(row("em"), row("m"), ACT.Exp, scale=-1.0).then_inc(scalar_done, act.mark("ml em"))
            nc.scalar.activation(row("wk"), row("t1"), ACT.Exp).then_inc(scalar_done, act.mark("ml wk"))
            with act.loop(4, "rg") as it:
                act.eng.wait_ge(tensor_done, act.at("tensor", "rg r"))
                nc.scalar.activation(rgt("r"), bank(6), ACT.Sigmoid, bias=dyn_col("rg_br", it, 1)).then_inc(scalar_done, act.mark())
                act.eng.wait_ge(tensor_done, act.at("tensor", ("chunk", act.chunk + 1)))
                nc.scalar.activation(rgt("ig"), bank(7), ACT.Sigmoid, bias=dyn_col("rg_bi", it, 1)).then_inc(scalar_done, act.mark("rg ig"))
                act.eng.wait_ge(scalar_done, act.now())
                nc.scalar.activation(rgt("a"), rgt("r"), ACT.Exp, scale=lam[:, 11, ds(it, 1)]).then_inc(scalar_done, act.mark("rg a"))
                nc.scalar.activation(rgt("t"), rgt("r"), ACT.Tanh, scale=lam[:, 11, ds(it, 1)]).then_inc(scalar_done, act.mark("rg t"))
                act.eng.wait_ge(vector_done, act.at("vector", "rg u2"))
                nc.scalar.activation(rgt("u"), rgt("u"), ACT.Sqrt).then_inc(scalar_done, act.mark("rg sqrt"))
                act.eng.wait_ge(tensor_done, act.at("tensor", ("chunk", act.chunk + 2)))
                nc.scalar.activation(rgt("gelu"), bank(5), ACT.Gelu_apprx_tanh).then_inc(scalar_done, act.mark("rg gelu"))
            with act.loop(4, "ml") as it:
                act.eng.wait_ge(vector_done, act.at("vector", "ml qk conv"))
                nc.scalar.activation(mlt("q"), mlt("qs"), ACT.Silu).then_inc(scalar_done, act.mark())
                nc.scalar.activation(mlt("k"), mlt("cq"), ACT.Silu).then_inc(scalar_done, act.mark("ml qk silu"))
                act.eng.wait_ge(tensor_done, act.at("tensor", ("chunk", act.chunk + 4)))
                nc.scalar.activation(mlt("o"), bank(3), ACT.Sigmoid).then_inc(scalar_done, act.mark("ml o"))
                act.eng.wait_ge(tensor_done, act.at("tensor", "ml M"))
                for c in range(NC_):
                    at = slice(c * CH, (c + 1) * CH)
                    nc.scalar.activation(mlt("E")[:, at], bank(4)[:, at], ACT.Exp, scale=-1.0,
                                                  bias=rcol[:, 0, c, ds(it, 1)]).then_inc(scalar_done, act.mark("ml E" if c == NC_ - 1 else None))
                act.eng.wait_ge(tensor_done, act.at("tensor", "ml den"))
                nc.scalar.activation(mlt("den"), bank(7), ACT.Abs).then_inc(scalar_done, act.mark("ml |den|"))
                act.eng.wait_ge(vector_done, act.at("vector", "ml h"))
                nc.scalar.activation(mlt("sq"), mlt("ho"), ACT.Square).then_inc(scalar_done, act.mark("ml sq"))
                act.eng.wait_ge(vector_done, act.at("vector", "ml mean"))
                nc.scalar.activation(mlt("rs"), mlt("rs"), ACT.Sqrt).then_inc(scalar_done, act.mark("ml rstd"))
            act.chunk += 7

        def conv4(dve, out, src, taps, bias):
            nc.vector.tensor_scalar(out, src, taps(3), bias, ALU.mult, ALU.add).then_inc(vector_done, dve.mark())
            dve.eng.wait_ge(vector_done, dve.now())
            for j in (1, 2, 3):
                ins = nc.vector.scalar_tensor_tensor(out[:, j:T], src[:, 0:T - j], taps(3 - j), out[:, j:T], ALU.mult, ALU.add)
                if j < 3:
                    ins.then_inc(vector_done, dve.mark())
                    dve.eng.wait_ge(vector_done, dve.now())
            return ins

        def ab_vector(dve):
            norm_vector(dve, "ab", x_tiles, xn_tiles, KD, model_norm(1))
            first = dve.chunk
            la = col("rg_lam")
            nc.vector.scalar_tensor_tensor(lamx(0), la, -1.0, la, ALU.mult, ALU.max).then_inc(vector_done, dve.mark("rg |lam|"))
            dve.eng.wait_ge(vector_done, dve.now())
            dve.eng.wait_ge(scalar_done, dve.at("scalar", "rg exp lam"))
            nc.vector.tensor_scalar(lamx(2), lamx(1), 2.0, None, ALU.add).then_inc(vector_done, dve.mark())
            dve.eng.wait_ge(vector_done, dve.now())
            nc.vector.reciprocal(lamx(2), lamx(2)).then_inc(vector_done, dve.mark())
            dve.eng.wait_ge(vector_done, dve.now())
            nc.vector.tensor_tensor(lamx(3), lamx(1), lamx(2), ALU.mult).then_inc(vector_done, dve.mark())
            dve.eng.wait_ge(vector_done, dve.now())
            nc.vector.tensor_tensor(lamx(4), lamx(3), lamx(3), ALU.mult).then_inc(vector_done, dve.mark())
            dve.eng.wait_ge(vector_done, dve.now())
            nc.vector.tensor_scalar(lamx(5), lamx(4), 1.0 / 17, None, ALU.mult).then_inc(vector_done, dve.mark())
            dve.eng.wait_ge(vector_done, dve.now())
            for n in (15, 13, 11, 9, 7, 5, 3):
                nc.vector.scalar_tensor_tensor(lamx(5), lamx(5), 1.0 / n, lamx(4), ALU.add, ALU.mult).then_inc(vector_done, dve.mark())
                dve.eng.wait_ge(vector_done, dve.now())
            nc.vector.scalar_tensor_tensor(lamx(5), lamx(5), 1.0, lamx(3), ALU.add, ALU.mult).then_inc(vector_done, dve.mark())
            dve.eng.wait_ge(vector_done, dve.now())
            nc.vector.tensor_scalar(lamx(6), la, -1.0, 0.0, ALU.mult, ALU.max).then_inc(vector_done, dve.mark())
            dve.eng.wait_ge(vector_done, dve.now())
            nc.vector.scalar_tensor_tensor(lamx(7), lamx(5), 2.0, lamx(6), ALU.mult, ALU.add).then_inc(vector_done, dve.mark())
            dve.eng.wait_ge(vector_done, dve.now())
            nc.vector.tensor_scalar(lamx(11), lamx(7), -8.0, None, ALU.mult).then_inc(vector_done, dve.mark())
            dve.eng.wait_ge(vector_done, dve.now())
            dve.eng.wait_ge(tensor_done, dve.at("tensor", "ml i"))
            nc.vector.tensor_scalar(row("li"), bank(1)[0:4, :], col("ml_bi")[0:4, :], None, ALU.add).then_inc(vector_done, dve.mark())
            dve.eng.wait_ge(tensor_done, dve.at("tensor", ("chunk", first)))
            nc.vector.tensor_scalar(row("f"), bank(2)[0:4, :], col("ml_bf")[0:4, :], None, ALU.add).then_inc(vector_done, dve.mark())
            dve.eng.wait_ge(vector_done, dve.now())
            nc.vector.scalar_tensor_tensor(row("af"), row("f"), -1.0, row("f"), ALU.mult, ALU.max).then_inc(vector_done, dve.mark("ml |f|"))
            nc.vector.memset(row("one"), 1.0).then_inc(vector_done, dve.mark())
            dve.eng.wait_ge(scalar_done, dve.at("scalar", "ml ln"))
            nc.vector.scalar_tensor_tensor(row("lf"), row("f"), 0.0, row("t1"), ALU.min, ALU.subtract).then_inc(vector_done, dve.mark())
            dve.eng.wait_ge(vector_done, dve.now())
            for c in range(NC_):
                ins = nc.vector.tensor_tensor_scan(row("b", c * CH, CH), row("one", c * CH, CH), row("lf", c * CH, CH), 0.0, ALU.mult, ALU.add)
                ins.then_inc(vector_done, dve.mark())
            dve.eng.wait_ge(vector_done, dve.now())
            nc.vector.tensor_tensor(row("c"), row("li"), row("b"), ALU.subtract).then_inc(vector_done, dve.mark())
            dve.eng.wait_ge(vector_done, dve.now())
            for c in range(NC_):
                m0 = NEG if c == 0 else row("m", c * CH - 1, 1)
                nc.vector.tensor_tensor_scan(row("M", c * CH, CH), row("c", c * CH, CH), row("c", c * CH, CH), m0, ALU.max, ALU.max).then_inc(vector_done, dve.mark())
                dve.eng.wait_ge(vector_done, dve.now())
                nc.vector.tensor_tensor(row("m", c * CH, CH), row("M", c * CH, CH), row("b", c * CH, CH), ALU.add).then_inc(vector_done, dve.mark())
                nc.vector.tensor_scalar(row("t0", c * CH, CH), row("M", c * CH, CH), -1.0, m0, ALU.mult, ALU.add).then_inc(vector_done, dve.mark())
                nc.vector.tensor_scalar(row("t1", c * CH, CH), row("c", c * CH, CH), row("M", (c + 1) * CH - 1, 1), None, ALU.subtract).then_inc(vector_done, dve.mark("ml m" if c == NC_ - 1 else None))
                dve.eng.wait_ge(vector_done, dve.now())
            dve.eng.wait_ge(scalar_done, dve.at("scalar", "ml wk"))
            for a, n in enumerate(("M", "sc", "em")):
                for h in range(4):
                    nc.vector.tensor_scalar(spread[0:4, a, h, :], row(n), tab("sel4", h, 1)[0:4, :], None, ALU.mult).then_inc(vector_done, dve.mark())
            dve.eng.wait_ge(tensor_done, dve.at("tensor", "ml cols"))
            nc.vector.tensor_copy(rcol[:, :, :, :], bank(3)[:, 0:2 * NC_ * 4].rearrange("p (a c h) -> p a c h", a=2, c=NC_)).then_inc(vector_done, dve.mark("ml rows"))
            with dve.loop(4, "rg") as it:
                dve.eng.wait_ge(tensor_done, dve.at("tensor", "rg xa"))
                conv4(dve, rgt("conv"), bank(4), lambda j: dyn_col("rg_taps", it, 4, j), dyn_col("rg_cb", it, 1)).then_inc(vector_done, dve.mark("rg conv"))
                dve.eng.wait_ge(scalar_done, dve.at("scalar", "rg t"))
                nc.vector.tensor_tensor(rgt("v"), rgt("a"), rgt("a"), ALU.mult).then_inc(vector_done, dve.mark())
                dve.eng.wait_ge(vector_done, dve.now())
                nc.vector.scalar_tensor_tensor(rgt("w"), rgt("v"), 1.0, rgt("t"), ALU.add, ALU.mult).then_inc(vector_done, dve.mark())
                dve.eng.wait_ge(vector_done, dve.now())
                nc.vector.tensor_scalar(rgt("u"), rgt("w"), -1.0, 0.0, ALU.mult, ALU.max).then_inc(vector_done, dve.mark("rg u2"))
                dve.eng.wait_ge(vector_done, dve.now())
                nc.vector.tensor_tensor(rgt("v"), rgt("ig"), rgt("conv"), ALU.mult).then_inc(vector_done, dve.mark())
                dve.eng.wait_ge(vector_done, dve.now())
                dve.eng.wait_ge(scalar_done, dve.at("scalar", "rg sqrt"))
                nc.vector.tensor_tensor(rgt("w"), rgt("v"), rgt("u"), ALU.mult).then_inc(vector_done, dve.mark())
                dve.eng.wait_ge(vector_done, dve.now())
                nc.vector.tensor_tensor_scan(rgt("h"), rgt("a"), rgt("w"), 0.0, ALU.mult, ALU.add).then_inc(vector_done, dve.mark())
                dve.eng.wait_ge(vector_done, dve.now())
                dve.eng.wait_ge(scalar_done, dve.at("scalar", "rg gelu"))
                nc.vector.tensor_tensor(ab_mixed[:, ds(it, 1), :].rearrange("p a t -> p (a t)"), rgt("gelu"), rgt("h"), ALU.mult).then_inc(vector_done, dve.mark("rg mixed"))
            for c in range(NC_):
                nc.vector.memset(mv[:, c, P:2 * P], 1.0).then_inc(vector_done, dve.mark())
            scale = float(P) ** -0.5
            with dve.loop(4, "ml") as it:
                dve.eng.wait_ge(tensor_done, dve.at("tensor", "ml q"))
                conv4(dve, mlt("qs"), bank(0), lambda j: dyn_col("ml_taps", it, 4, j), dyn_col("ml_cb", it, 1)).then_inc(vector_done, dve.mark())
                dve.eng.wait_ge(tensor_done, dve.at("tensor", ("chunk", first + 3)))
                conv4(dve, mlt("cq"), bank(1), lambda j: dyn_col("ml_taps", it, 4, 16 + j), dyn_col("ml_cb", it, 1, 4)).then_inc(vector_done, dve.mark("ml qk conv"))
                dve.eng.wait_ge(tensor_done, dve.at("tensor", "ml v"))
                nc.vector.tensor_copy(mv[:, :, 0:P], bank(2).rearrange("p (c n) -> p c n", c=NC_)).then_inc(vector_done, dve.mark("ml v"))
                dve.eng.wait_ge(tensor_done, dve.at("tensor", "ml kT"))
                for c in range(NC_ - 1):
                    nc.vector.tensor_scalar(mlt("kw")[:, c * CH:(c + 1) * CH], bank(0)[:, c * CH:(c + 1) * CH],
                                                     rcol[:, 1, c, ds(it, 1)], None, ALU.mult).then_inc(vector_done, dve.mark("ml kw" if c == NC_ - 2 else None))
                dve.eng.wait_ge(scalar_done, dve.at("scalar", "ml E"))
                dve.eng.wait_ge(tensor_done, dve.at("tensor", "ml s"))
                nc.vector.scalar_tensor_tensor(mlt("P"), bank(7), scale, mlt("E"), ALU.mult, ALU.mult).then_inc(vector_done, dve.mark("ml P"))
                dve.eng.wait_ge(tensor_done, dve.at("tensor", "ml sc"))
                nc.vector.scalar_tensor_tensor(mlt("qs"), mlt("q"), scale, bank(5), ALU.mult, ALU.mult).then_inc(vector_done, dve.mark())
                dve.eng.wait_ge(tensor_done, dve.at("tensor", "ml state"))
                nc.vector.tensor_copy(mlt("rs")[:, 0:4], bank(5)[:, CH - 1:T:CH]).then_inc(vector_done, dve.mark())
                nc.vector.tensor_copy(state[:, 0, :], bank(1)[:, 0:256]).then_inc(vector_done, dve.mark())
                dve.eng.wait_ge(vector_done, dve.now())
                for c in (1, 2):
                    nc.vector.scalar_tensor_tensor(state[:, c, :], state[:, c - 1, :], mlt("rs")[:, c:c + 1],
                                                             bank(1 + c // 2)[:, 256 * (c % 2):256 * (c % 2) + 256], ALU.mult, ALU.add).then_inc(vector_done, dve.mark("ml states" if c == 2 else None))
                    dve.eng.wait_ge(vector_done, dve.now())
                dve.eng.wait_ge(scalar_done, dve.at("scalar", "ml |den|"))
                nc.vector.tensor_tensor(mlt("den"), mlt("den"), bank(6), ALU.max).then_inc(vector_done, dve.mark())
                dve.eng.wait_ge(vector_done, dve.now())
                nc.vector.reciprocal(mlt("den"), mlt("den")).then_inc(vector_done, dve.mark())
                dve.eng.wait_ge(vector_done, dve.now())
                nc.vector.tensor_tensor(mlt("ho"), mlt("den"), bank(4), ALU.mult).then_inc(vector_done, dve.mark("ml h"))
                dve.eng.wait_ge(vector_done, dve.now())
                dve.eng.wait_ge(tensor_done, dve.at("tensor", "ml ss"))
                nc.vector.tensor_scalar(mlt("rs"), bank(0), 1.0 / P, EPS, ALU.mult, ALU.add).then_inc(vector_done, dve.mark())
                dve.eng.wait_ge(vector_done, dve.now())
                nc.vector.reciprocal(mlt("rs"), mlt("rs")).then_inc(vector_done, dve.mark("ml mean"))
                dve.eng.wait_ge(vector_done, dve.now())
                dve.eng.wait_ge(scalar_done, dve.at("scalar", "ml rstd"))
                nc.vector.scalar_tensor_tensor(mlt("den"), mlt("ho"), dyn_col("ml_norm", it, 1), mlt("rs"), ALU.mult, ALU.mult).then_inc(vector_done, dve.mark())
                dve.eng.wait_ge(vector_done, dve.now())
                nc.vector.tensor_tensor(ab_mixed[:, ds(it + 4, 1), :].rearrange("p a t -> p (a t)"), mlt("den"), mlt("o"), ALU.mult).then_inc(vector_done, dve.mark("ml mixed"))
            dve.chunk += 5
            out_vector(dve, "ab")

        MIXERS["ab"] = {"sync": ab_sync, "tensor": ab_tensor, "scalar": ab_scalar, "vector": ab_vector}

        class Step:

            def __init__(self, scores, masks, parts, values, out, group, last):
                self.scores, self.masks, self.parts = scores, masks, parts
                self.values, self.out, self.group, self.last = values, out, group, last

        def att_scores(pe, tag, n, step, buf):
            area = psum[:, 2 * (n % 2):2 * (n % 2) + 2, :].rearrange("p b t -> p (b t)")
            for q, k, at in step.scores:
                ins = nc.tensor.matmul(area[:, at:at + k.free_size()], q, k, start=True, stop=True)
            ins.then_inc(tensor_done, pe.mark((tag, "scores", n)))

        def att_tensor(pe, tag, steps, buf):
            p, pT, _ = buf
            turned = psum[:, 4:6, :].rearrange("p b t -> p (b t)")

            def values(n):
                step = steps[n]
                pe.eng.wait_ge(vector_done, pe.at("vector", (tag, "turned", n)))
                pe.eng.wait_ge(scalar_done, pe.at("scalar", (tag, "turned", n)))
                b, parts, where = step.out
                for m, (_, keys, v) in enumerate(step.values):
                    ins = nc.tensor.matmul(bank(b)[parts, where], v, pT[0:keys, n % 2, P * place(step, m):P * place(step, m) + P],
                                           start=m == 0, stop=m == len(step.values) - 1)
                ins.then_inc(tensor_done, pe.mark((tag, "out", n)))

            att_scores(pe, tag, 0, steps[0], buf)
            for n, step in enumerate(steps):
                if n + 1 < len(steps):
                    att_scores(pe, tag, n + 1, steps[n + 1], buf)
                pe.eng.wait_ge(vector_done, pe.at("vector", (tag, "p", n)))
                if n >= 1:
                    pe.eng.wait_ge(vector_done, pe.at("vector", (tag, "turned", n - 1)))
                    pe.eng.wait_ge(scalar_done, pe.at("scalar", (tag, "turned", n - 1)))
                for m, (at, keys, _) in enumerate(step.values):
                    ins = nc.tensor.transpose(turned[0:keys, P * place(step, m):P * place(step, m) + P], p[:, n % 2, at:at + keys], ident)
                ins.then_inc(tensor_done, pe.mark((tag, "turn", n)))
                if n >= 1:
                    if steps[n - 1].first and steps[n - 1].group >= 2:
                        pe.eng.wait_ge(vector_done, pe.at("vector", (tag, "group", steps[n - 1].group - 2)))
                    values(n - 1)
            values(len(steps) - 1)

        def place(step, m):
            first = len(step.values) // 2
            return m if m < first else 4 + m - first

        def turned_blocks(step, b):
            runs = []
            for m, (_, keys, _) in enumerate(step.values):
                at = place(step, m)
                if at // 4 == b:
                    if runs and runs[-1][2] == keys:
                        runs[-1] = (runs[-1][0], at + 1, keys)
                    else:
                        runs.append((at, at + 1, keys))
            return runs

        def att_scalar(act, tag, steps, buf, scale=1.0):
            p, pT, stats = buf

            def exps(n):
                step = steps[n]
                act.eng.wait_ge(vector_done, act.at("vector", (tag, "max", n)))
                area = psum[:, 2 * (n % 2):2 * (n % 2) + 2, :].rearrange("p b t -> p (b t)")
                for m, (a, b, _, _) in enumerate(step.parts):
                    src = p[:, n % 2, a:b] if step.masks else area[:, a:b]
                    ins = nc.scalar.activation(p[:, n % 2, a:b], src, ACT.Exp, scale=scale, bias=stats[:, n % 2, m:m + 1],
                                               accum_out=stats[:, n % 2, 4 + m:5 + m])
                    ins.then_inc(scalar_done, act.mark((tag, "exp", n) if m == len(step.parts) - 1 else None))

            exps(0)
            for n, step in enumerate(steps):
                if n + 1 < len(steps):
                    exps(n + 1)
                act.eng.wait_ge(tensor_done, act.at("tensor", (tag, "turn", n)))
                if n >= 2:
                    act.eng.wait_ge(tensor_done, act.at("tensor", (tag, "out", n - 2)))
                other = turned_blocks(step, 1)
                for i, (a, b, keys) in enumerate(other):
                    src = psum[0:keys, 4:6, :].rearrange("p b t -> p (b t)")[:, P * a:P * b]
                    nc.scalar.copy(pT[0:keys, n % 2, P * a:P * b], src).then_inc(scalar_done, act.mark((tag, "turned", n) if i == len(other) - 1 else None))

        def att_vector(dve, tag, steps, buf, copy_out, scale=1.0):
            p, pT, stats = buf

            def maxima(n):
                step = steps[n]
                area = psum[:, 2 * (n % 2):2 * (n % 2) + 2, :].rearrange("p b t -> p (b t)")
                dve.eng.wait_ge(tensor_done, dve.at("tensor", (tag, "scores", n)))
                if n >= 2:
                    dve.eng.wait_ge(tensor_done, dve.at("tensor", (tag, "turn", n - 2)))
                for mask in step.masks:
                    mask(dve, p[:, n % 2, :], area).then_inc(vector_done, dve.mark())
                if step.masks:
                    dve.eng.wait_ge(vector_done, dve.now())
                for m, (a, b, _, _) in enumerate(step.parts):
                    src = p[:, n % 2, a:b] if step.masks else area[:, a:b]
                    ins = nc.vector.tensor_reduce(stats[:, n % 2, m:m + 1], src, AX, ALU.max, negate=True)
                    last = m == len(step.parts) - 1
                    if scale != 1.0:
                        ins.then_inc(vector_done, dve.mark())
                        dve.eng.wait_ge(vector_done, dve.now())
                        ins = nc.vector.tensor_scalar(stats[:, n % 2, m:m + 1], stats[:, n % 2, m:m + 1], scale, None, ALU.mult)
                    ins.then_inc(vector_done, dve.mark((tag, "max", n) if last else None))

            maxima(0)
            for n, step in enumerate(steps):
                k = len(step.parts)
                dve.eng.wait_ge(scalar_done, dve.at("scalar", (tag, "exp", n)))
                nc.vector.reciprocal(stats[:, n % 2, 8:8 + k], stats[:, n % 2, 4:4 + k]).then_inc(vector_done, dve.mark())
                dve.eng.wait_ge(vector_done, dve.now())
                gated = [m for m in range(k) if step.parts[m][2] is not None]
                for m in gated:
                    nc.vector.tensor_tensor(stats[:, n % 2, 8 + m:9 + m], stats[:, n % 2, 8 + m:9 + m],
                                                     step.parts[m][2](dve), ALU.mult).then_inc(vector_done, dve.mark())
                if gated:
                    dve.eng.wait_ge(vector_done, dve.now())
                for m, (a, b, _, factor) in enumerate(step.parts):
                    r = stats[:, n % 2, 8 + m:9 + m]
                    at = p[:, n % 2, a:b]
                    if factor is None:
                        ins = nc.vector.tensor_scalar(at, at, r, None, ALU.mult)
                    else:
                        ins = nc.vector.scalar_tensor_tensor(at, at, r, factor, ALU.mult, ALU.mult)
                    ins.then_inc(vector_done, dve.mark((tag, "p", n) if m == k - 1 else None))
                if n + 1 < len(steps):
                    maxima(n + 1)
                dve.eng.wait_ge(tensor_done, dve.at("tensor", (tag, "turn", n)))
                if n >= 2:
                    dve.eng.wait_ge(tensor_done, dve.at("tensor", (tag, "out", n - 2)))
                mine = turned_blocks(step, 0)
                for i, (a, b, keys) in enumerate(mine):
                    src = psum[0:keys, 4:6, :].rearrange("p b t -> p (b t)")[:, P * a:P * b]
                    nc.vector.tensor_copy(pT[0:keys, n % 2, P * a:P * b], src).then_inc(vector_done, dve.mark((tag, "turned", n) if i == len(mine) - 1 else None))
                if n >= 1 and steps[n - 1].last:
                    dve.eng.wait_ge(tensor_done, dve.at("tensor", (tag, "out", n - 1)))
                    copy_out(dve, steps[n - 1].group).then_inc(vector_done, dve.mark((tag, "group", steps[n - 1].group)))
            dve.eng.wait_ge(tensor_done, dve.at("tensor", (tag, "out", len(steps) - 1)))
            copy_out(dve, steps[-1].group).then_inc(vector_done, dve.mark((tag, "group", steps[-1].group)))

        def order(steps):
            group = None
            for s in steps:
                s.first = s.group != group
                group = s.group
            return steps

        carve_reset()
        ns_mixed = carve(8, T)
        ns_mixed_tiles = [ns_mixed[:, k, :] for k in range(8)]
        ns_w1 = carve(2, SLOT)
        ns_gates = carve(4, 48)
        ns_q = carve(2, T)
        ns_ks, ns_kw = carve(T), carve(T)
        ns_c = carve(2, T)
        ns_v = carve(4, P)
        ns_h = carve(4, 32)
        ns_b1 = carve(4)
        ns_kc = carve(32)
        ns_vc = carve(64)
        att_buf = (carve(2, 2 * T), carve(2, 2 * T), carve(2, 12))

        def ns_steps():
            steps = []
            for h in range(4):
                half = slice(64 * (h % 2), 64 * (h % 2) + 64)
                for i in range(4):
                    q = ns_q[half, h // 2, P * i:P * (i + 1)]
                    lo = max(0, i - 2)
                    wide, win = P * (i + 1), P * (i + 1 - lo)
                    scores = [(q, ns_ks[half, 0:wide], 0), (q, ns_kw[half, P * lo:P * (i + 1)], T), (q, ns_kc[half, 0:N_CMP], T + 384)]

                    def diag(dve, p, s, wide=wide):
                        return nc.vector.tensor_tensor(p[:, wide - P:wide], s[:, wide - P:wide], tab("causal"), ALU.add)

                    def full(dve, p, s, wide=wide):
                        return nc.vector.tensor_copy(p[:, 0:wide - P], s[:, 0:wide - P])

                    def window(dve, p, s, win=win):
                        return nc.vector.tensor_tensor(p[:, T:T + win], s[:, T:T + win], tab("window", 384 - win, win), ALU.add)

                    def compressed(dve, p, s, i=i):
                        return nc.vector.tensor_tensor(p[:, T + 384:T + 384 + N_CMP], s[:, T + 384:T + 384 + N_CMP],
                                                       tab("cmp_add", N_CMP * i, N_CMP), ALU.add)

                    gate = lambda b, i=i, h=h: lambda dve: ns_gates[:, i, ds(dve.it * 12 + (3 * h + b), 1)]
                    parts = [(0, wide, gate(1), None), (T, T + win, gate(2), None),
                             (T + 384, T + 384 + N_CMP, gate(0), tab("cmp_mul", N_CMP * i, N_CMP))]
                    values = [(P * j, P, ns_v[:, j, 0:64]) for j in range(i + 1)]
                    values += [(T + P * j, P, ns_v[:, lo + j, 64:128]) for j in range(i + 1 - lo)]
                    values += [(T + 384, N_CMP, ns_vc[0:N_CMP, :])]
                    steps.append(Step(scores, [diag] + [full] * (i > 0) + [window, compressed], parts, values,
                                      (6 + h // 2, half, slice(P * i, P * (i + 1))), h // 2, h % 2 == 1 and i == 3))
            return order(steps)

        def nsa_sync(sp):
            load(sp, arrays["nsa_gates"][0], 384)
            sp.eng.wait_ge(tensor_done, sp.at("tensor", ("nsa", "sum")))
            for a in range(2):
                sp.eng.dma_start(ns_w1[:, a, :], arrays["nsa_w1"][a]).then_inc(w1_loaded, 16)
            with sp.loop(4, "nsa") as it:
                sp.first = sp.chunk
                load(sp, arrays["nsa_a"][ds(it, 1)].rearrange("a p n -> (a p) n"), 4096, 2)
                load(sp, arrays["nsa_b"][ds(it, 1)].rearrange("a p n -> (a p) n"), 3072, 2)
            out_sync(sp, "nsa", "nsa_out", 8)

        def nsa_tensor(pe):
            norm_tensor(pe, "nsa", xn_tiles, KD)
            pe.eng.wait_ge(vector_done, pe.at("vector", ("nsa", "normed", KD - 1)))
            pe.eng.wait_ge(slot_loaded[pe.slot()], pe.chunk_loaded())
            w = ring[:, pe.slot(), :]
            for i in range(4):
                for k in range(KD):
                    nc.tensor.matmul(bank(1)[:, 48 * i:48 * i + 48], xn[:, k, P * i:P * (i + 1)], w[:, 48 * k:48 * k + 48],
                                     start=k == 0, stop=False)
                ins = nc.tensor.matmul(bank(1)[:, 48 * i:48 * i + 48], ones[0:1, :], col("nsa_bg")[0:1, :], start=False, stop=True)
            ins.then_inc(tensor_done, pe.used())
            pe.eng.wait_ge(w1_loaded, 16 * 2)
            for a in range(2):
                for m in range(2):
                    for l in range(16):
                        ins = nc.tensor.matmul(bank(2)[:, 2 * a + m:2 * a + m + 1], ns_w1[:, a, 256 * l + P * m:256 * l + P * m + P],
                                               col("nsa_pe", 16 * a + l, 1), start=l == 0, stop=l == 15)
            ins.then_inc(tensor_done, pe.mark("nsa pe"))
            pe.eng.wait_ge(vector_done, pe.at("vector", "nsa b1"))
            pe.eng.wait_ge(scalar_done, pe.at("scalar", "nsa gates"))
            steps = ns_steps()
            with pe.loop(4, "nsa"):
                pe.eng.wait_ge(vector_done, pe.at("vector", ("nsa", "group", 1), back=1))
                pe.eng.wait_ge(slot_loaded[pe.slot()], pe.chunk_loaded())
                w = ring[:, pe.slot(), :]
                for j in range(2):
                    product(bank(j), w, xn_tiles, KD, at=1024 * j).then_inc(tensor_done, pe.mark(("nsa q", j)))
                product(bank(2), w, xn_tiles, KD, at=2048).then_inc(tensor_done, pe.mark("nsa ks"))
                product(bank(3), w, xn_tiles, KD, at=3072).then_inc(tensor_done, pe.used())
                pe.eng.wait_ge(slot_loaded[pe.slot()], pe.chunk_loaded())
                w = ring[:, pe.slot(), :]
                product(bank(4), w, xn_tiles, KD).then_inc(tensor_done, pe.mark("nsa kc"))
                product(bank(5), w, xn_tiles, KD, at=1024).then_inc(tensor_done, pe.mark("nsa vc"))
                for i in range(4):
                    for k in range(KD):
                        ins = nc.tensor.matmul(bank(6)[:, P * i:P * (i + 1)], xn[:, k, P * i:P * (i + 1)],
                                               w[:, 2048 + P * k:2048 + P * (k + 1)], start=k == 0, stop=k == KD - 1)
                ins.then_inc(tensor_done, pe.used())
                pe.eng.wait_ge(vector_done, pe.at("vector", "nsa c"))
                for a in range(2):
                    for m in range(2):
                        for l in range(16):
                            ins = nc.tensor.matmul(bank(7)[:, 32 * (2 * a + m):32 * (2 * a + m) + N_CMP],
                                                   ns_w1[:, a, 256 * l + P * m:256 * l + P * m + P],
                                                   ns_c[:, a, 2 * l:2 * l + 16 * (N_CMP - 1) + 1:16], start=l == 0, stop=l == 15)
                ins.then_inc(tensor_done, pe.mark("nsa h"))
                pe.eng.wait_ge(scalar_done, pe.at("scalar", "nsa h"))
                for m in range(2):
                    ins = nc.tensor.matmul(bank(4)[:, 0:N_CMP], col("nsa_k_w2", P * m, P), ns_h[:, m, 0:N_CMP], start=m == 0, stop=m == 1)
                for m in range(2):
                    ins = nc.tensor.matmul(bank(5)[0:N_CMP, 0:64], ns_h[:, 2 + m, 0:N_CMP], col("nsa_v_w2", 64 * m, 64), start=m == 0, stop=m == 1)
                ins.then_inc(tensor_done, pe.mark("nsa kvc"))
                pe.eng.wait_ge(scalar_done, pe.at("scalar", "nsa kw"))
                pe.eng.wait_ge(vector_done, pe.at("vector", "nsa kvc"))
                att_tensor(pe, "nsa", steps, att_buf)
            pe.eng.wait_ge(vector_done, pe.at("vector", ("nsa", "group", 1)))
            out_tensor(pe, "nsa", ns_mixed_tiles, 8)

        def nsa_scalar(act, ready):
            norm_scalar(act, "nsa", x_tiles, xn_tiles, KD, ready)
            act.eng.wait_ge(tensor_done, act.at("tensor", ("chunk", act.chunk)))
            nc.scalar.activation(ns_gates[:, :, :], bank(1)[:, 0:192].rearrange("p (i n) -> p i n", i=4), ACT.Sigmoid).then_inc(scalar_done, act.mark("nsa gates"))
            steps = ns_steps()
            with act.loop(4, "nsa"):
                for j in range(2):
                    act.eng.wait_ge(tensor_done, act.at("tensor", ("nsa q", j)))
                    nc.scalar.mul(ns_q[:, j, :], bank(j), 0.125).then_inc(scalar_done, act.mark())
                act.eng.wait_ge(tensor_done, act.at("tensor", "nsa ks"))
                nc.scalar.copy(ns_ks, bank(2)).then_inc(scalar_done, act.mark())
                act.eng.wait_ge(tensor_done, act.at("tensor", ("chunk", act.chunk + 1)))
                nc.scalar.copy(ns_kw, bank(3)).then_inc(scalar_done, act.mark("nsa kw"))
                act.eng.wait_ge(tensor_done, act.at("tensor", "nsa h"))
                for j in range(4):
                    nc.scalar.activation(ns_h[:, j, 0:N_CMP], bank(7)[:, 32 * j:32 * j + N_CMP], ACT.Gelu_apprx_tanh,
                                                  bias=ns_b1[:, j:j + 1]).then_inc(scalar_done, act.mark("nsa h" if j == 3 else None))
                att_scalar(act, "nsa", steps, att_buf)
            act.chunk += 5

        def nsa_vector(dve):
            norm_vector(dve, "nsa", x_tiles, xn_tiles, KD, model_norm(4))
            first = dve.chunk
            dve.eng.wait_ge(tensor_done, dve.at("tensor", "nsa pe"))
            nc.vector.tensor_tensor(ns_b1, bank(2)[:, 0:4], col("nsa_b1"), ALU.add).then_inc(vector_done, dve.mark("nsa b1"))
            nc.vector.memset(ns_c[64:128, :, T - 1:T], 0.0).then_inc(vector_done, dve.mark())
            steps = ns_steps()

            def copy_out(dve, group):
                return nc.vector.tensor_copy(ns_mixed[:, ds(dve.it * 2 + group, 1), :].rearrange("p a t -> p (a t)"), bank(6 + group))

            with dve.loop(4, "nsa"):
                for a, n in enumerate(("nsa kc", "nsa vc")):
                    dve.eng.wait_ge(tensor_done, dve.at("tensor", n))
                    nc.vector.tensor_copy(ns_c[0:64, a, :], bank(4 + a)[0:64, :]).then_inc(vector_done, dve.mark())
                    nc.vector.tensor_copy(ns_c[64:128, a, 0:T - 1], bank(4 + a)[64:128, 1:T]).then_inc(vector_done, dve.mark("nsa c" if a == 1 else None))
                dve.eng.wait_ge(tensor_done, dve.at("tensor", ("chunk", first + 2)))
                nc.vector.tensor_copy(ns_v[:, :, :], bank(6).rearrange("p (i n) -> p i n", i=4)).then_inc(vector_done, dve.mark())
                dve.eng.wait_ge(tensor_done, dve.at("tensor", "nsa kvc"))
                nc.vector.tensor_copy(ns_kc[:, 0:N_CMP], bank(4)[:, 0:N_CMP]).then_inc(vector_done, dve.mark())
                nc.vector.tensor_copy(ns_vc[0:N_CMP, :], bank(5)[0:N_CMP, 0:64]).then_inc(vector_done, dve.mark("nsa kvc"))
                att_vector(dve, "nsa", steps, att_buf, copy_out)
            dve.chunk += 3
            out_vector(dve, "nsa")

        MIXERS["nsa"] = {"sync": nsa_sync, "tensor": nsa_tensor, "scalar": nsa_scalar, "vector": nsa_vector}

        carve_reset()
        m2_mixed = carve(6, T)
        m2_mixed_tiles = [m2_mixed[:, k, :] for k in range(6)]
        lat = carve(6, T)
        lat_n = carve(5, T)
        m2_t = carve(2, T)
        mla_q, mla_k = carve(2, T), carve(2, T)
        mla_v = carve(4, P)
        m2_buf = (carve(2, 2 * T), carve(2, 2 * T), carve(2, 12))
        carve_reset(6 * T)
        dil_q, dil_k = carve(3, T), carve(3, T)
        dil_v = carve(4, 384)
        dil_buf = (carve(2, 2 * T), carve(2, 2 * T), carve(2, 12))
        MLA_SCALE = float(96) ** -0.5
        by_class = lambda ap: ap.rearrange("p (q c) -> p c q", c=4)
        in_order = lambda ap: ap.rearrange("p (c q) -> p c q", c=4)

        def mla_steps():
            steps = []
            for h in range(2):
                for i in range(4):
                    steps.append(Step([(mla_q[0:96, h, P * i:P * (i + 1)], mla_k[0:96, h, :], 0)], [], [(0, T, None, None)],
                                      [(P * j, P, mla_v[:, j, 64 * h:64 * h + 64]) for j in range(4)],
                                      (6, slice(64 * h, 64 * h + 64), slice(P * i, P * (i + 1))), 0, h == 1 and i == 3))
            return order(steps)

        def dil_steps():
            steps = []
            for s in range(2):
                half = slice(64 * s, 64 * s + 64)
                for c in range(DIL_CLASSES):
                    own = slice(P * c, P * (c + 1))
                    scores = [(dil_q[half, 0, own], dil_k[half, 0, :], 0)]
                    scores += [(dil_q[half, g, own], dil_k[half, g, own], T + P * (g - 1)) for g in (1, 2)]

                    def bias(g, a, n, table, s=s):
                        def put(dve, p, area):
                            slope = tab("slopes")[:, ds(dve.it * 2 + (4 * g + s), 1)]
                            return nc.vector.scalar_tensor_tensor(p[:, a:a + n], table, slope, area[:, a:a + n], ALU.mult, ALU.add)
                        return put

                    masks = [bias(0, 0, T, tab("dist0", T * c, T)), bias(1, T, P, tab("dist1")), bias(2, T + P, P, tab("dist2"))]
                    values = [(P * j, P, dil_v[:, j, 64 * s:64 * s + 64]) for j in range(4)]
                    values += [(T + P * (g - 1), P, dil_v[:, c, P * g + 64 * s:P * g + 64 * s + 64]) for g in (1, 2)]
                    steps.append(Step(scores, masks, [(0, T + 2 * P, None, None)], values, (6, half, own), 0, s == 1 and c == 3))
            return order(steps)

        def m2_sync(sp):
            load(sp, arrays["mla_z"][0], 3072)
            load(sp, arrays["mla_z"][1][:, 0:2816], 2816)
            with sp.loop(4, "mla") as it:
                sp.first = sp.chunk
                load(sp, arrays["mla_q"][ds(it, 1)].rearrange("a p n -> (a p) n"), 576, 2)
                load(sp, arrays["mla_kv"][ds(it, 1)].rearrange("a p n -> (a p) n"), 512, 2)
            with sp.loop(2, "dil") as it:
                sp.first = sp.chunk
                for j in range(2):
                    load(sp, arrays["dil_qk"][ds(it * 2 + j, 1)].rearrange("a p n -> (a p) n"), 3072, 4)
                load(sp, arrays["dil_va"][ds(it, 1)].rearrange("a p n -> (a p) n"), 2048, 4)
                load(sp, arrays["dil_vb"][ds(it, 1)].rearrange("a p n -> (a p) n"), 1024, 4)
            out_sync(sp, "m2", "ab2_out", 6)

        lat_q = [lat[:, k, :] for k in range(3)]
        lat_kv = [lat[:, 3 + k, :] for k in range(2)]
        lat_qn = [lat_n[:, k, :] for k in range(3)]
        lat_kvn = [lat_n[:, 3 + k, :] for k in range(2)]

        def m2_tensor(pe):
            norm_tensor(pe, "m2", xn_tiles, KD)
            pe.eng.wait_ge(vector_done, pe.at("vector", ("m2", "normed", KD - 1)))
            pe.eng.wait_ge(slot_loaded[pe.slot()], pe.chunk_loaded())
            w = ring[:, pe.slot(), :]
            for j in range(3):
                ins = product(bank(j), w, xn_tiles, KD, at=1024 * j)
                if j < 2:
                    ins.then_inc(tensor_done, pe.mark(("m2 z", j)))
            ins.then_inc(tensor_done, pe.used())
            pe.eng.wait_ge(slot_loaded[pe.slot()], pe.chunk_loaded())
            w = ring[:, pe.slot(), :]
            for j in range(2):
                product(bank(3 + j), w, xn_tiles, KD, at=1024 * j).then_inc(tensor_done, pe.mark(("m2 z", 3 + j)))
            product(bank(5)[0:96, :], w, xn_tiles, KD, width=96, at=2048).then_inc(tensor_done, pe.used())
            norm_tensor(pe, "mla gq", lat_qn, 3, b=6)
            norm_tensor(pe, "mla gkv", lat_kvn, 2, b=7)
            pe.eng.wait_ge(vector_done, pe.at("vector", "m2 z"))
            nc.tensor.matmul(bank(0)[0:96, :], tab("mla_rot")[0:96, :], lat[0:96, 5, :], start=True, stop=True).then_inc(tensor_done, pe.mark("mla rot k"))
            pe.eng.wait_ge(vector_done, pe.at("vector", "mla k rope"))
            pe.eng.wait_ge(vector_done, pe.at("vector", ("mla gkv", "normed", 1)))
            steps = mla_steps()
            with pe.loop(4, "mla"):
                pe.eng.wait_ge(vector_done, pe.at("vector", ("mla", "group", 0), back=1))
                pe.eng.wait_ge(slot_loaded[pe.slot()], pe.chunk_loaded())
                w = ring[:, pe.slot(), :]
                product(bank(0)[0:96, :], w, lat_qn, 3, width=96).then_inc(tensor_done, pe.mark(("mla q", 0)))
                product(bank(1)[0:96, :], w, lat_qn, 3, width=96, at=288).then_inc(tensor_done, pe.used())
                pe.eng.wait_ge(slot_loaded[pe.slot()], pe.chunk_loaded())
                w = ring[:, pe.slot(), :]
                for h in range(2):
                    product(bank(2 + h)[0:64, :], w, lat_kvn, 2, width=64, at=128 * h).then_inc(tensor_done, pe.mark(("mla k", h)))
                for i in range(4):
                    for k in range(2):
                        ins = nc.tensor.matmul(bank(4)[:, P * i:P * (i + 1)], lat_kvn[k][:, P * i:P * (i + 1)],
                                               w[:, 256 + P * k:256 + P * (k + 1)], start=k == 0, stop=k == 1)
                ins.then_inc(tensor_done, pe.used())
                for h in range(2):
                    pe.eng.wait_ge(scalar_done, pe.at("scalar", ("mla raw", h)))
                    nc.tensor.matmul(bank(5 + h)[0:96, :], tab("mla_rot")[0:96, :], m2_t[0:96, h, :], start=True, stop=True).then_inc(tensor_done, pe.mark(("mla rot", h)))
                pe.eng.wait_ge(scalar_done, pe.at("scalar", ("mla k", 1)))
                pe.eng.wait_ge(vector_done, pe.at("vector", ("mla q", 1)))
                att_tensor(pe, "mla", steps, m2_buf)
            pe.eng.wait_ge(vector_done, pe.at("vector", ("mla", "group", 0)))
            steps = dil_steps()
            with pe.loop(2, "dil"):
                pe.eng.wait_ge(vector_done, pe.at("vector", ("dil", "group", 0), back=1))
                for n in range(2):
                    pe.eng.wait_ge(slot_loaded[pe.slot()], pe.chunk_loaded())
                    w = ring[:, pe.slot(), :]
                    for j in range(3):
                        ins = product(bank(3 * n + j), w, xn_tiles, KD, at=1024 * j)
                        if j < 2:
                            ins.then_inc(tensor_done, pe.mark(("dil qk", 3 * n + j)))
                    ins.then_inc(tensor_done, pe.used())
                pe.eng.wait_ge(slot_loaded[pe.slot()], pe.chunk_loaded())
                w = ring[:, pe.slot(), :]
                for c in range(4):
                    for k in range(KD):
                        ins = nc.tensor.matmul(bank(6 + c // 2)[:, 256 * (c % 2):256 * (c % 2) + 256], by_class(xn[:, k, :])[:, c, :],
                                               w[:, 256 * k:256 * (k + 1)], start=k == 0, stop=k == KD - 1)
                ins.then_inc(tensor_done, pe.used())
                pe.eng.wait_ge(slot_loaded[pe.slot()], pe.chunk_loaded())
                w = ring[:, pe.slot(), :]
                pe.eng.wait_ge(scalar_done, pe.at("scalar", "dil q"))
                for c in range(4):
                    for k in range(KD):
                        ins = nc.tensor.matmul(bank(0)[:, P * c:P * (c + 1)], by_class(xn[:, k, :])[:, c, :],
                                               w[:, P * k:P * (k + 1)], start=k == 0, stop=k == KD - 1)
                ins.then_inc(tensor_done, pe.used())
                pe.eng.wait_ge(vector_done, pe.at("vector", "dil v"))
                pe.eng.wait_ge(scalar_done, pe.at("scalar", "dil q"))
                att_tensor(pe, "dil", steps, dil_buf)
            pe.eng.wait_ge(vector_done, pe.at("vector", ("dil", "group", 0)))
            out_tensor(pe, "m2", m2_mixed_tiles, 6)

        def m2_scalar(act, ready):
            norm_scalar(act, "m2", x_tiles, xn_tiles, KD, ready)
            latents = (vector_done, act.at("vector", "m2 z"))
            norm_scalar(act, "mla gq", lat_q, lat_qn, 3, latents)
            norm_scalar(act, "mla gkv", lat_kv, lat_kvn, 2, latents)
            steps = mla_steps()
            with act.loop(4, "mla"):
                act.eng.wait_ge(tensor_done, act.at("tensor", ("mla q", 0)))
                nc.scalar.copy(m2_t[0:96, 0, :], bank(0)[0:96, :]).then_inc(scalar_done, act.mark(("mla raw", 0)))
                act.eng.wait_ge(tensor_done, act.at("tensor", ("chunk", act.chunk + 2)))
                nc.scalar.copy(m2_t[0:96, 1, :], bank(1)[0:96, :]).then_inc(scalar_done, act.mark(("mla raw", 1)))
                for h in range(2):
                    act.eng.wait_ge(tensor_done, act.at("tensor", ("mla k", h)))
                    nc.scalar.copy(mla_k[0:64, h, :], bank(2 + h)[0:64, :]).then_inc(scalar_done, act.mark(("mla k", h)))
                att_scalar(act, "mla", steps, m2_buf)
            act.eng.wait_ge(vector_done, act.at("vector", ("mla", "group", 0)))
            steps = dil_steps()
            with act.loop(2, "dil"):
                for j in range(3):
                    act.eng.wait_ge(tensor_done, act.at("tensor", ("dil qk", j) if j < 2 else ("chunk", act.chunk + 4)))
                    nc.scalar.mul(in_order(dil_q[:, j, :]), by_class(bank(j)), 0.125).then_inc(scalar_done, act.mark("dil q" if j == 2 else None))
                att_scalar(act, "dil", steps, dil_buf)
            act.chunk += 10

        def m2_vector(dve):
            norm_vector(dve, "m2", x_tiles, xn_tiles, KD, model_norm(7))
            first = dve.chunk
            for j in range(6):
                dve.eng.wait_ge(tensor_done, dve.at("tensor", ("chunk", first) if j == 2 else ("chunk", first + 1) if j == 5 else ("m2 z", j)))
                n = 96 if j == 5 else P
                nc.vector.tensor_copy(lat[0:n, j, :], bank(j)[0:n, :]).then_inc(vector_done, dve.mark("m2 z" if j == 5 else None))
            norm_vector(dve, "mla gq", lat_q, lat_qn, 3, lambda k: col("mla_gq", k, 1), b=6)
            norm_vector(dve, "mla gkv", lat_kv, lat_kvn, 2, lambda k: col("mla_gkv", k, 1), b=7)
            dve.eng.wait_ge(tensor_done, dve.at("tensor", "mla rot k"))
            at = slice(64, 96)
            nc.vector.tensor_tensor(m2_t[at, 0, :], lat[at, 5, :], tab("mla_cos")[at, :], ALU.mult).then_inc(vector_done, dve.mark())
            nc.vector.tensor_tensor(m2_t[at, 1, :], tab("mla_sin")[at, :], bank(0)[at, :], ALU.mult).then_inc(vector_done, dve.mark())
            dve.eng.wait_ge(vector_done, dve.now())
            for h in range(2):
                nc.vector.tensor_tensor(mla_k[at, h, :], m2_t[at, 0, :], m2_t[at, 1, :], ALU.add).then_inc(vector_done, dve.mark("mla k rope" if h else None))
            steps = mla_steps()
            with dve.loop(4, "mla"):
                for h in range(2):
                    dve.eng.wait_ge(tensor_done, dve.at("tensor", ("mla rot", h)))
                    nc.vector.scalar_tensor_tensor(mla_q[0:96, h, :], m2_t[0:96, h, :], MLA_SCALE, tab("mla_cos")[0:96, :], ALU.mult, ALU.mult).then_inc(vector_done, dve.mark())
                    dve.eng.wait_ge(vector_done, dve.now())
                    nc.vector.scalar_tensor_tensor(m2_t[0:96, h, :], bank(5 + h)[0:96, :], MLA_SCALE, tab("mla_sin")[0:96, :], ALU.mult, ALU.mult).then_inc(vector_done, dve.mark())
                    dve.eng.wait_ge(vector_done, dve.now())
                    nc.vector.tensor_tensor(mla_q[0:96, h, :], mla_q[0:96, h, :], m2_t[0:96, h, :], ALU.add).then_inc(vector_done, dve.mark())
                dve.eng.wait_ge(tensor_done, dve.at("tensor", ("chunk", first + 3)))
                nc.vector.tensor_copy(mla_v[:, :, :], bank(4).rearrange("p (i n) -> p i n", i=4)).then_inc(vector_done, dve.mark(("mla q", 1)))

                def mla_out(dve, group):
                    return nc.vector.tensor_copy(m2_mixed[:, ds(dve.it, 1), :].rearrange("p a t -> p (a t)"), bank(6))

                att_vector(dve, "mla", steps, m2_buf, mla_out)
            steps = dil_steps()
            with dve.loop(2, "dil"):
                for j in range(3):
                    dve.eng.wait_ge(tensor_done, dve.at("tensor", ("dil qk", 3 + j) if j < 2 else ("chunk", first + 5)))
                    nc.vector.tensor_copy(in_order(dil_k[:, j, :]), by_class(bank(3 + j))).then_inc(vector_done, dve.mark())
                dve.eng.wait_ge(tensor_done, dve.at("tensor", ("chunk", first + 6)))
                for b in range(2):
                    nc.vector.tensor_copy(dil_v[:, 2 * b:2 * b + 2, 0:256], bank(6 + b).rearrange("p (c n) -> p c n", c=2)).then_inc(vector_done, dve.mark())
                dve.eng.wait_ge(tensor_done, dve.at("tensor", ("chunk", first + 7)))
                nc.vector.tensor_copy(dil_v[:, :, 256:384], bank(0).rearrange("p (c n) -> p c n", c=4)).then_inc(vector_done, dve.mark("dil v"))

                def dil_out(dve, group):
                    to = m2_mixed[:, ds(dve.it + 4, 1), :].rearrange("p a (q c) -> p (a c) q", c=4)
                    return nc.vector.tensor_copy(to, in_order(bank(6)))

                att_vector(dve, "dil", steps, dil_buf, dil_out)
            dve.chunk += 8
            out_vector(dve, "m2")

        MIXERS["m2"] = {"sync": m2_sync, "tensor": m2_tensor, "scalar": m2_scalar, "vector": m2_vector}

        carve_reset()
        gq_mixed = carve(8, T)
        gq_mixed_tiles = [gq_mixed[:, k, :] for k in range(8)]
        gq_raw, gq_sq, gq_n = carve(3, T), carve(3, T), carve(3, T)
        gq_qk = carve(3, T)
        gq_v = carve(4, 64)
        gq_buf = (carve(2, 2 * T), carve(2, 2 * T), carve(2, 12))

        def gqa_steps():
            steps = []
            for h in range(4):
                half = slice(64 * (h % 2), 64 * (h % 2) + 64)
                for i in range(4):
                    steps.append(Step([(gq_qk[half, h // 2, P * i:P * (i + 1)], gq_qk[half, 2, :], 0)], [], [(0, T, None, None)],
                                      [(P * j, P, gq_v[:, j, :]) for j in range(4)],
                                      (6 + h // 2, half, slice(P * i, P * (i + 1))), h // 2, h % 2 == 1 and i == 3))
            return order(steps)

        def gqa_sync(sp):
            with sp.loop(4, "gqa") as it:
                sp.first = sp.chunk
                load(sp, arrays["gqa_qk"][ds(it, 1)].rearrange("a p n -> (a p) n"), 3072, 2)
                load(sp, arrays["gqa_v"][ds(it, 1)].rearrange("a p n -> (a p) n"), 512, 2)
            out_sync(sp, "gqa", "gqa_out", 8)

        def gqa_tensor(pe):
            norm_tensor(pe, "gqa", xn_tiles, KD)
            pe.eng.wait_ge(vector_done, pe.at("vector", ("gqa", "normed", KD - 1)))
            steps = gqa_steps()
            with pe.loop(4, "gqa"):
                pe.eng.wait_ge(vector_done, pe.at("vector", ("gqa", "group", 1), back=1))
                pe.eng.wait_ge(slot_loaded[pe.slot()], pe.chunk_loaded())
                w = ring[:, pe.slot(), :]
                for j in range(2):
                    product(bank(j), w, xn_tiles, KD, at=1024 * j).then_inc(tensor_done, pe.mark(("gqa raw", j)))
                product(bank(2), w, xn_tiles, KD, at=2048).then_inc(tensor_done, pe.used())
                pe.eng.wait_ge(slot_loaded[pe.slot()], pe.chunk_loaded())
                w = ring[:, pe.slot(), :]
                for i in range(4):
                    for k in range(KD):
                        ins = nc.tensor.matmul(bank(3)[:, 64 * i:64 * (i + 1)], xn[:, k, P * i:P * (i + 1)],
                                               w[:, 64 * k:64 * (k + 1)], start=k == 0, stop=k == KD - 1)
                ins.then_inc(tensor_done, pe.used())
                for j in range(3):
                    pe.eng.wait_ge(scalar_done, pe.at("scalar", ("gqa square", j)))
                    nc.tensor.matmul(bank(4 + j), tab("ones64"), gq_sq[:, j, :], start=True, stop=True).then_inc(tensor_done, pe.mark(("gqa sum", j)))
                for j in range(3):
                    pe.eng.wait_ge(vector_done, pe.at("vector", ("gqa normed", j)))
                    nc.tensor.matmul(bank(j), tab("gqa_rot"), gq_n[:, j, :], start=True, stop=True).then_inc(tensor_done, pe.mark(("gqa rot", j)))
                pe.eng.wait_ge(vector_done, pe.at("vector", "gqa qk"))
                att_tensor(pe, "gqa", steps, gq_buf)
            pe.eng.wait_ge(vector_done, pe.at("vector", ("gqa", "group", 1)))
            out_tensor(pe, "gqa", gq_mixed_tiles, 8)

        def gqa_scalar(act, ready):
            norm_scalar(act, "gqa", x_tiles, xn_tiles, KD, ready)
            steps = gqa_steps()
            with act.loop(4, "gqa"):
                for j in range(3):
                    act.eng.wait_ge(tensor_done, act.at("tensor", ("gqa raw", j) if j < 2 else ("chunk", act.chunk)))
                    nc.scalar.copy(gq_raw[:, j, :], bank(j)).then_inc(scalar_done, act.mark())
                    nc.scalar.activation(gq_sq[:, j, :], bank(j), ACT.Square).then_inc(scalar_done, act.mark(("gqa square", j)))
                act.eng.wait_ge(vector_done, act.at("vector", "gqa mean"))
                nc.scalar.activation(gq_sq[:, :, :], gq_sq[:, :, :], ACT.Sqrt).then_inc(scalar_done, act.mark("gqa rstd"))
                att_scalar(act, "gqa", steps, gq_buf)
            act.chunk += 4

        def gqa_vector(dve):
            norm_vector(dve, "gqa", x_tiles, xn_tiles, KD, model_norm(9))
            first = dve.chunk
            steps = gqa_steps()
            with dve.loop(4, "gqa"):
                for j in range(3):
                    dve.eng.wait_ge(tensor_done, dve.at("tensor", ("gqa sum", j)))
                    nc.vector.tensor_scalar(gq_sq[:, j, :], bank(4 + j), 1.0 / 64, EPS, ALU.mult, ALU.add).then_inc(vector_done, dve.mark())
                    dve.eng.wait_ge(vector_done, dve.now())
                nc.vector.reciprocal(gq_sq[:, :, :], gq_sq[:, :, :]).then_inc(vector_done, dve.mark("gqa mean"))
                dve.eng.wait_ge(vector_done, dve.now())
                dve.eng.wait_ge(tensor_done, dve.at("tensor", ("chunk", first + 1)))
                nc.vector.tensor_copy(gq_v[:, :, :], bank(3)[:, 0:256].rearrange("p (i n) -> p i n", i=4)).then_inc(vector_done, dve.mark())
                dve.eng.wait_ge(scalar_done, dve.at("scalar", "gqa rstd"))
                for j in range(3):
                    gain = col("gqa_gk") if j == 2 else col("gqa_gq")
                    nc.vector.scalar_tensor_tensor(gq_n[:, j, :], gq_raw[:, j, :], gain, gq_sq[:, j, :], ALU.mult, ALU.mult).then_inc(vector_done, dve.mark(("gqa normed", j)))
                for j in range(3):
                    scale = 1.0 if j == 2 else 0.125
                    dve.eng.wait_ge(tensor_done, dve.at("tensor", ("gqa rot", j)))
                    nc.vector.scalar_tensor_tensor(gq_raw[:, j, :], gq_n[:, j, :], scale, tab("gqa_cos"), ALU.mult, ALU.mult).then_inc(vector_done, dve.mark())
                    nc.vector.scalar_tensor_tensor(gq_sq[:, j, :], bank(j), scale, tab("gqa_sin"), ALU.mult, ALU.mult).then_inc(vector_done, dve.mark())
                    dve.eng.wait_ge(vector_done, dve.now())
                    nc.vector.tensor_tensor(gq_qk[:, j, :], gq_raw[:, j, :], gq_sq[:, j, :], ALU.add).then_inc(vector_done, dve.mark("gqa qk" if j == 2 else None))

                def gqa_copy(dve, group):
                    return nc.vector.tensor_copy(gq_mixed[:, ds(dve.it * 2 + group, 1), :].rearrange("p a t -> p (a t)"), bank(6 + group))

                att_vector(dve, "gqa", steps, gq_buf, gqa_copy)
            dve.chunk += 2
            out_vector(dve, "gqa")

        MIXERS["gqa"] = {"sync": gqa_sync, "tensor": gqa_tensor, "scalar": gqa_scalar, "vector": gqa_vector}

        todo = stages or ["f0", "ab", "f1", "f2", "nsa", "f3", "n1", "m2", "f4", "gqa", "f5", "n2"]
        FFN = {"f0": (0, 0, 0.5), "f1": (1, 2, 0.5), "f2": (2, 3, 0.5), "f3": (3, 5, 0.5), "f4": (4, 8, 1.0), "f5": (5, 10, 1.0)}

        def ready_for(e, i):
            if i == 0:
                return vector_done, e.at("vector", "x")
            s = todo[i - 1]
            if s in FFN:
                return x_updated, KD * (FFN[s][0] + 1) + 2
            return vector_done, e.at("vector", (s, "copied") if s == "n1" else (s, "x", 1))

        def mixer_sync(sp, s, i):
            if i:
                sp.eng.wait_ge(*ready_for(sp, i))
            if s in tables_at:
                sp.eng.dma_start(tabbuf[s][:, 0:tables_at[s][1]], arrays["t_" + s]).then_inc(tables_loaded, 16)
            sp.base = sp.chunk
            MIXERS[s]["sync"](sp)

        def wait_tables(e, s):
            mixers = [m for m in todo if m in MIXERS]
            e.eng.wait_ge(tables_loaded, 16 * (mixers.index(s) + 1))

        if todo[-1] != "n2":
            todo = todo + ["end"]

        n_chunks = []
        block = ctx.enter_context(nc.Block())

        @block.sync
        def _(eng):
            sp = Engine(eng, None, counts, [counts["slot0"], counts["slot1"]])
            start_sync(sp)
            for i, s in enumerate(todo):
                if s in FFN:
                    ffn_sync(sp, s, FFN[s][0], i > 0 and todo[i - 1] in MIXERS)
                elif s in MIXERS:
                    mixer_sync(sp, s, i)
            end_sync(sp)
            n_chunks.append(sp.chunk)

        @block.tensor
        def _(eng):
            pe = Engine(eng, counts["tensor"], counts)
            eng.sem_inc(tensor_done, LEAD)
            eng.sem_inc(unit_used, 2)
            start_tensor(pe)
            for i, s in enumerate(todo):
                if s in FFN:
                    ffn_tensor(pe, s, FFN[s][0])
                elif s in MIXERS:
                    wait_tables(pe, s)
                    MIXERS[s]["tensor"](pe)
                elif s in ("n1", "n2"):
                    norm_tensor(pe, s, xn_tiles, KD)
            end_tensor(pe, ("n2", "normed", KD - 1) if todo[-1] == "n2" else "end")
            n_chunks.append(pe.chunk)

        @block.scalar
        def _(eng):
            act = Engine(eng, counts["scalar"], counts)
            eng.sem_inc(scalar_done, LEAD)
            for i, s in enumerate(todo):
                if s in FFN:
                    ffn_scalar(act, s, FFN[s][0], ready_for(act, i))
                elif s in MIXERS:
                    MIXERS[s]["scalar"](act, ready_for(act, i))
                elif s in ("n1", "n2"):
                    norm_scalar(act, s, x_tiles, xn_tiles, KD, ready_for(act, i))
            n_chunks.append(act.chunk)

        @block.vector
        def _(eng):
            dve = Engine(eng, counts["vector"], counts)
            eng.sem_inc(vector_done, LEAD)
            eng.sem_inc(unit_ready, 4)
            eng.sem_inc(hidden_ready, 2)
            eng.sem_inc(x_updated, 2)
            start_vector(dve)
            for i, s in enumerate(todo):
                if s in FFN:
                    ffn_vector(dve, s, *FFN[s])
                elif s in MIXERS:
                    wait_tables(dve, s)
                    MIXERS[s]["vector"](dve)
                elif s in ("n1", "n2"):
                    norm_vector(dve, s, x_tiles, xn_tiles, KD, model_norm(6 if s == "n1" else 11))
                    if s == "n1":
                        dve.eng.wait_ge(vector_done, dve.now())
                        nc.vector.tensor_copy(x[:, :, :], xn[:, :, :]).then_inc(vector_done, dve.mark((s, "copied")))
                elif s == "end":
                    dve.eng.wait_ge(vector_done, dve.now())
                    dve.eng.wait_ge(*ready_for(dve, i))
                    nc.vector.tensor_copy(xn[:, :, :], x[:, :, :]).then_inc(vector_done, dve.mark("end"))
            end_vector(dve)
            n_chunks.append(dve.chunk)

    assert len(set(n_chunks)) == 1, n_chunks
    return seen


def program(Bacc, shapes, columns_at, tables_at, stages=None):
    marks = {}
    while True:
        nc = Bacc("TRN2", target_bir_lowering=False, num_devices=1)
        arrays = {n: nc.dram_tensor(f"in_{n}", s, F32, kind="ExternalInput").ap() for n, s in shapes.items()}
        out = nc.dram_tensor("out_0", (T, D), F32, kind="ExternalOutput").ap()
        seen = build(nc, arrays, columns_at, tables_at, out, marks, stages)
        if seen == marks:
            return nc
        marks = seen


def prepare(inputs):
    tables = make_tables()
    weights, columns = lay_out(inputs)
    columns_at, _ = offsets(columns)
    tables_at = {stage: offsets(t) for stage, t in tables.items()}
    sent = {"x": inputs["x"][0], "columns": np.concatenate(list(columns.values()), 1)}
    sent.update(weights)
    sent.update({"t_" + stage: np.concatenate(list(t.values()), 1) for stage, t in tables.items()})
    return {n: np.ascontiguousarray(a) for n, a in sent.items()}, columns_at, tables_at


def kernel(**inputs):
    import concourse.bacc as _bacc
    from concourse.bass_utils import run_bass_kernel_spmd as _run

    inputs = {n: np.asarray(a) for n, a in inputs.items()}
    sent, columns_at, tables_at = prepare(inputs)
    nc = program(_bacc.Bacc, {n: a.shape for n, a in sent.items()}, columns_at, tables_at)
    r = _run(nc, [{f"in_{n}": a for n, a in sent.items()}], core_ids=[0])
    return r.results[0]["out_0"].reshape(1, T, D)
```

```python
from contextlib import ExitStack, contextmanager

import numpy as np

import concourse.bass as bass
from concourse import mybir

F32 = mybir.dt.float32
F32R = mybir.dt.float32r
ARENA = 26800
ACT = mybir.ActivationFunctionType
ALU = mybir.AluOpType
AX = mybir.AxisListType.X
ds = bass.ds

P = 128
T = 512
D = 1024
KD = D // P
D_FF = 2816
KF = D_FF // P
EPS = 1e-6
LEAD = 2048
SLOT = 4096
NSLOT = 2
UNIT = KF // 2 * P
NEG = -1e30
BIG = 1e30

DIL_SLOTS, DIL_GROUPS, DIL_CLASSES = 4, 3, 4
N_CMP = (T - 32) // 16 + 1
NSA_MASK = 3 * P + N_CMP


TABLES = {
    "all": ["ident", "ones"],
    "ab": ["future", "sel4"],
    "nsa": ["nsa_masks", "cmp_any"],
    "m2": ["dist0", "dist1", "dist2", "slopes", "mla_cos", "mla_sin", "mla_rot"],
    "gqa": ["gqa_cos", "gqa_sin", "gqa_rot", "ones64"],
}


def rope_tables(pos, dim):
    freqs = (np.float32(10000.0) ** (-np.arange(0, dim, 2, dtype=np.float32) / np.float32(dim))).astype(np.float32)
    ang = pos.astype(np.float32)[:, None] * freqs[None, :]
    return np.cos(ang).astype(np.float32).T, np.sin(ang).astype(np.float32).T


def rotation(width, starts, half):
    m = np.zeros((P, width), np.float32)
    for s in starts:
        for i in range(half):
            m[s + half + i, s + i] = -1.0
            m[s + i, s + half + i] = 1.0
    return m


def make_tables():
    q = np.arange(P)[:, None]
    k = np.arange(P)[None, :]
    pos = np.arange(T)
    t = {}
    t["ident"] = np.eye(P)
    t["ones"] = np.ones((P, P))
    t["ones64"] = (q // 64 == k // 64) * 1.0
    t["future"] = np.tile(np.where(q <= k, 0.0, BIG), (1, 4))
    causal, older = np.where(k <= q, 0.0, NEG), np.where(k > q, 0.0, NEG)
    masks = []
    for i in range(T // P):
        ok = (np.arange(N_CMP) * 16 + 31)[None, :] <= P * i + q
        masks += [causal, np.where(ok, 0.0, NEG), causal, older]
    t["nsa_masks"] = np.concatenate(masks, 1)
    t["cmp_any"] = (q >= 31) * 1.0
    near = []
    for c in range(DIL_CLASSES):
        u = (4 * k + np.arange(4)[:, None, None])
        dist = np.abs(4 * q[None] + c - u)
        near.append(np.where(dist <= 64, dist, 1e33).transpose(1, 0, 2).reshape(P, T))
    t["dist0"] = np.concatenate(near, 1)
    t["dist1"] = np.where(np.abs(q - k) <= 64, 4 * np.abs(q - k), 1e33)
    t["dist2"] = np.where((q - k) % 4 == 0, 4 * np.abs(q - k), 1e33)
    n = np.arange(1, DIL_SLOTS * DIL_GROUPS + 1, dtype=np.float32)
    t["slopes"] = np.tile(-np.exp2(np.float32(-8.0) * n / np.float32(12.0)), (P, 1))
    c, s = rope_tables(pos, 32)
    full = np.zeros((2, P, T), np.float32)
    full[0, :64] = 1.0
    full[0, 64:96], full[1, 64:96] = np.tile(c, (2, 1)), np.tile(s, (2, 1))
    t["mla_cos"], t["mla_sin"] = full
    cr, sr = rope_tables(pos // 64, 32)
    cc, sc = rope_tables(pos % 64, 32)
    t["gqa_cos"] = np.concatenate([cr, cr, cc, cc] * 2, 0)
    t["gqa_sin"] = np.concatenate([sr, sr, sc, sc] * 2, 0)
    t["mla_rot"] = rotation(96, [64], 16)
    t["gqa_rot"] = rotation(P, [0, 32, 64, 96], 16)
    t["sel4"] = np.concatenate([np.eye(4), np.zeros((P - 4, 4))], 0)
    t = {name: np.ascontiguousarray(a, np.float32) for name, a in t.items()}
    return {stage: {n: t[n] for n in names} for stage, names in TABLES.items()}


def offsets(parts):
    at, out = 0, {}
    for name, a in parts.items():
        out[name] = (at, a.shape[1])
        at += a.shape[1]
    return out, at


def m_tiles(w, width=P):
    k, m = w.shape
    return w.reshape(k // P, P, m // width, width).transpose(2, 1, 0, 3).reshape(m // width, P, -1)


def cols(w, at, width):
    return m_tiles(w[:, at:at + width], width)[0]


def twice(w, at, width):
    return m_tiles(np.concatenate([w[:, at:at + width]] * 2, 1))[0]


def column(v):
    return v.reshape(-1, P).T


def padded(v):
    v = v.reshape(v.shape[0], -1)
    out = np.zeros((P, v.shape[1]), v.dtype)
    out[:v.shape[0]] = v
    return out


def lay_out(i):
    w = {}
    gu, down = [], []
    for a, b in [(i["ffn1_w_gu"][0], i["ffn1_w_down"][0]), (i["ffn2_w_gu"][0], i["ffn2_w_down"][0]),
                 (i["ffn1_w_gu"][1], i["ffn1_w_down"][1]), (i["ffn2_w_gu"][1], i["ffn2_w_down"][1]),
                 (i["ffn_w_in_2"][0], i["ffn_w_out_2"][0]), (i["ffn_w_in_2"][1], i["ffn_w_out_2"][1])]:
        gu.append(np.concatenate([m_tiles(a[:, :D_FF]), m_tiles(a[:, D_FF:])], 2))
        down.append(m_tiles(b))
    w["gate_up"], w["down"] = np.concatenate(gu), np.concatenate(down)

    ab = i["ab_w_in"][0]
    w["ab_gates"] = np.concatenate([cols(ab, 3072, 4), cols(ab, 3076, 4)], 1)[None]
    rg, ml = [], []
    for t in range(4):
        pair = []
        for name in ("rg_w_r", "rg_w_i"):
            z = np.zeros((P, P), ab.dtype)
            z[:64, :64], z[64:, 64:] = i[name][0, 2 * t], i[name][0, 2 * t + 1]
            pair.append(z)
        rg.append(np.concatenate([cols(ab, P * t, P), *pair], 1))
        rg.append(padded_free(cols(ab, 512 + P * t, P), 1280))
        ml.append(np.concatenate([cols(ab, 1024 + P * t, P), cols(ab, 1536 + P * t, P)], 1))
        ml.append(np.concatenate([cols(ab, 2048 + P * t, P), cols(ab, 2560 + P * t, P)], 1))
    w["rg"], w["ml"] = np.stack(rg), np.stack(ml)
    w["ab_out"] = m_tiles(i["ab_w_out"][0])

    ns = i["nsa_w_in"][0]
    w["nsa_gates"] = cols(ns, 2560, 48)[None]
    w["nsa_w1"] = np.stack([i[n][0].reshape(16, P, 256).transpose(1, 0, 2).reshape(P, -1) for n in ("nsa_k_w1", "nsa_v_w1")])
    a, b = [], []
    for g in range(4):
        kv = [1024 + 256 * j + 64 * g for j in range(6)]
        a.append(np.concatenate([cols(ns, 256 * g, P), cols(ns, 256 * g + P, P), twice(ns, kv[2], 64), twice(ns, kv[4], 64)], 1))
        both = np.concatenate([ns[:, kv[3]:kv[3] + 64], ns[:, kv[5]:kv[5] + 64]], 1)
        b.append(np.concatenate([twice(ns, kv[0], 64), twice(ns, kv[1], 64), m_tiles(both)[0]], 1))
    w["nsa_a"], w["nsa_b"] = np.stack(a), np.stack(b)
    w["nsa_out"] = m_tiles(i["nsa_w_out"][0])

    z = i["w_in_ab_2"][0]
    w["mla_z"] = np.stack([np.concatenate([cols(z, P * t, P) for t in range(3)], 1),
                           padded_free(np.concatenate([cols(z, 384, P), cols(z, 512, P), cols(z, 576, 96)], 1), 3072)])
    uq, ukv = i["mla_w_uq_2"][0], i["mla_w_ukv_2"][0]
    w["mla_q"] = np.stack([np.concatenate([cols(uq[:, 2 * h + e], 0, 96) for e in range(2)], 1) for h in range(4)])
    w["mla_kv"] = np.stack([np.concatenate(
        [cols(ukv[:, 2 * h + e], 0, 64) for e in range(2)] +
        [m_tiles(np.concatenate([ukv[:, 2 * h, 64:], ukv[:, 2 * h + 1, 64:]], 1))[0]], 1) for h in range(4)])
    qk, v = [], []
    for s in range(2):
        for j in range(2):
            qk.append(np.concatenate([cols(z, 672 + 768 * j + 256 * g + P * s, P) for g in range(3)], 1))
        v.append(np.concatenate([z[:, 672 + 1536 + 256 * g + P * s:][:, :P] for g in range(3)], 1))
    w["dil_qk"] = np.stack(qk)
    w["dil_va"] = np.stack([cols(u, 0, 256) for u in v])
    w["dil_vb"] = np.stack([cols(u, 256, P) for u in v])
    w["ab2_out"] = m_tiles(i["w_out_ab_2"][0])

    gq, gkv = i["gqa_w_q_2"][0], i["gqa_w_kv_2"][0]
    w["gqa_qk"] = np.stack([np.concatenate([cols(gq, 256 * g, P), cols(gq, 256 * g + P, P), twice(gkv, 64 * g, 64)], 1) for g in range(4)])
    w["gqa_v"] = np.stack([cols(gkv, 256 + 64 * g, 64) for g in range(4)])
    w["gqa_out"] = m_tiles(i["gqa_w_o_2"][0])

    c = {}
    gains = [i["ffn1_norm"][0], i["mix_norm"][0], i["ffn2_norm"][0], i["ffn1_norm"][1], i["mix_norm"][1], i["ffn2_norm"][1],
             i["final_norm"], i["mix_norm_ab_2"][0], i["ffn_norm_2"][0], i["mix_norm_c_2"][0], i["ffn_norm_2"][1], i["final_norm_2"]]
    c["gains"] = np.concatenate([column(g) for g in gains], 1)
    taps = lambda a: a.reshape(4, -1, P).transpose(2, 1, 0).reshape(P, -1)
    c["rg_taps"] = taps(i["rg_conv_w"][0])
    c["rg_cb"], c["rg_br"], c["rg_bi"], c["rg_lam"] = (column(i[n][0]) for n in ("rg_conv_b", "rg_b_r", "rg_b_i", "rg_lambda"))
    c["ml_taps"] = taps(i["ml_conv_w"][0])
    c["ml_cb"], c["ml_norm"] = column(i["ml_conv_b"][0]), column(i["ml_norm"][0])
    c["ml_bi"], c["ml_bf"] = padded(i["ml_b_i"][0]), padded(i["ml_b_f"][0])
    c["nsa_pe"] = np.concatenate([i[n][0].reshape(16, P).T for n in ("nsa_pe_k", "nsa_pe_v")], 1)
    c["nsa_b1"] = np.concatenate([column(i[n][0]) for n in ("nsa_k_b1", "nsa_v_b1")], 1)
    k2 = i["nsa_k_w2"][0]
    c["nsa_k_w2"] = m_tiles(np.concatenate([k2, k2], 1))[0]
    c["nsa_v_w2"] = cols(i["nsa_v_w2"][0], 0, 64)
    c["nsa_bg"] = padded(i["nsa_b_gate"][0][None])
    c["mla_gq"], c["mla_gkv"] = column(i["mla_q_norm_2"][0]), column(i["mla_kv_norm_2"][0])
    c["gqa_gq"] = np.concatenate([i["gqa_q_norm_2"][0]] * 2)[:, None]
    c["gqa_gk"] = np.concatenate([i["gqa_k_norm_2"][0]] * 2)[:, None]
    return w, c


def padded_free(a, width):
    return np.concatenate([a, np.zeros((P, width - a.shape[1]), a.dtype)], 1)


class Count:

    def __init__(self, name, known, seen, by, lead):
        self.name, self.known, self.seen, self.by, self.lead = name, known, seen, by, lead
        self.count, self.loop = 0, None

    def mark(self, what=None):
        self.count += self.by
        if what is not None:
            assert (self.name, what) not in self.seen, what
            self.seen[self.name, what] = (self.count, self.loop)
        return self.by

    def per(self, loop):
        return self.known.get((self.name, "per", loop), (1, 1))

    def at(self, what, it, loop, back):
        assert not self.known or (self.name, what) in self.known, (self.name, what)
        count, within = self.known.get((self.name, what), (1, None))
        if within is None:
            return self.lead + count
        per, trips = self.per(within)
        if it is None or within != loop:
            return self.lead + count + per * (trips - 1)
        return it * per + (self.lead + count - back * per)


class Engine:

    def __init__(self, eng, own, counts, more=()):
        self.eng, self.own, self.counts = eng, own, counts
        self.raised = ([own] if own else []) + list(more)
        self.it = self.loop_tag = None
        self.chunk = 0

    def mark(self, what=None):
        return self.own.mark(what)

    def now(self):
        if self.it is None:
            return self.own.lead + self.own.count
        return self.it * self.own.per(self.loop_tag)[0] + (self.own.lead + self.own.count)

    def at(self, who, what, back=0):
        return self.counts[who].at(what, self.it, self.loop_tag, back)

    def slot(self):
        return self.chunk % NSLOT

    def loaded(self):
        self.chunk += 1
        return self.counts[f"slot{(self.chunk - 1) % NSLOT}"].mark(("chunk", self.chunk - 1))

    def chunk_loaded(self):
        return self.at(f"slot{self.slot()}", ("chunk", self.chunk))

    def used(self):
        self.chunk += 1
        return self.own.mark(("chunk", self.chunk - 1))

    @contextmanager
    def loop(self, trips, tag):
        base = {c.name: c.count for c in self.raised}
        with self.eng.Fori(0, trips) as it:
            self.it, self.loop_tag = it, tag
            for c in self.raised:
                c.loop = tag
            yield it
        for c in self.raised:
            per = c.count - base[c.name]
            c.seen[c.name, "per", tag] = (per, trips)
            c.count = base[c.name] + per * trips
            c.loop = None
        self.it = self.loop_tag = None


def build(nc, arrays, columns_at, tables_at, out, marks, stages=None):
    seen = {}
    with ExitStack() as ctx:
        sb = lambda name, n, parts=P: ctx.enter_context(nc.sbuf_tensor(name, [parts, n], F32))
        x = sb("x", KD * T)[:, :].rearrange("p (k t) -> p k t", k=KD)
        ring = sb("ring", NSLOT * SLOT)[:, :].rearrange("p (s n) -> p s n", s=NSLOT)
        colbuf = sb("colbuf", sum(n for _, n in columns_at.values()))
        tabbuf = {"all": sb("table_all", tables_at["all"][1])}
        rstd = sb("rstd", T)
        with ExitStack() as room:
            xn = room.enter_context(nc.sbuf_tensor("xn", [P, KD * T], F32))[:, :].rearrange("p (k t) -> p k t", k=KD)
            arena = room.enter_context(nc.sbuf_tensor("arena", [P, ARENA], F32))
            shared = room.enter_context(nc.sbuf_tensor("tables", [P, max(n for s, (_, n) in tables_at.items() if s != "all")], F32))
        tabbuf.update({stage: shared for stage in tables_at if stage != "all"})
        room = ctx.enter_context(ExitStack())
        fr = lambda name, n, k: room.enter_context(nc.sbuf_tensor(name, [P, n * k], F32R))[:, :].rearrange("p (k t) -> p k t", k=k)
        x_hi, x_lo = fr("x_hi", T, KD), fr("x_lo", T, KD)
        hid_hi, hid_lo = fr("hid_hi", T, KF), fr("hid_lo", T, KF)
        w_hi, w_lo = fr("w_hi", UNIT, 2), fr("w_lo", UNIT, 2)
        work = room.enter_context(nc.sbuf_tensor("work", [P, 4 * T], F32))[:, :].rearrange("p (k t) -> p k t", k=4)
        psum = ctx.enter_context(nc.psum_tensor("psum", [P, 8, T], F32))
        bank = lambda b: psum[:, b, :]

        def col(name, a=0, n=None):
            at, width = columns_at[name]
            return colbuf[:, at + a:at + a + (width - a if n is None else n)]

        def tab(name, a=0, n=None):
            stage = next(s for s, names in TABLES.items() if name in names)
            at, width = tables_at[stage][0][name]
            return tabbuf[stage][:, at + a:at + a + (width - a if n is None else n)]

        def dyn_col(name, it, step, a=0, n=1):
            at, _ = columns_at[name]
            return colbuf[:, ds(it * step + (at + a), n)]

        sem = lambda name: ctx.enter_context(nc.semaphore(name))
        tensor_done, scalar_done, vector_done = sem("tensor_done"), sem("scalar_done"), sem("vector_done")
        slot_loaded = [sem(f"slot{k}_loaded") for k in range(NSLOT)]
        consts_loaded, x_loaded, w1_loaded, stored = (sem(n) for n in ("consts_loaded", "x_loaded", "w1_loaded", "stored"))
        tables_loaded = sem("tables_loaded")
        unit_hi, unit_ready, unit_used, silu_ready, hidden_ready, x_updated = (
            sem(n) for n in ("unit_hi", "unit_ready", "unit_used", "silu_ready", "hidden_ready", "x_updated"))
        counts = {n: Count(n, marks, seen, 1, LEAD) for n in ("tensor", "scalar", "vector")}
        counts.update({n: Count(n, marks, seen, 16, 0) for n in ("slot0", "slot1")})

        carve_at = [0]

        def carve_reset(to=0):
            carve_at[0] = to

        def carve(n, *shape):
            a = arena[:, carve_at[0]:carve_at[0] + n * int(np.prod(shape or (1,)))]
            carve_at[0] += n * int(np.prod(shape or (1,)))
            assert carve_at[0] <= ARENA, carve_at[0]
            if shape:
                names = "abcd"[:len(shape) + 1]
                sizes = {c: s for c, s in zip(names, (n, *shape))}
                a = a.rearrange(f"p ({' '.join(names)}) -> p {' '.join(names)}", **sizes)
            return a


        def load(sp, src, n, trip=None):
            k = sp.chunk
            if k - NSLOT >= sp.base:
                sp.eng.wait_ge(tensor_done, sp.at("tensor", ("chunk", k - NSLOT)))
            if trip is not None and k - sp.first < NSLOT:
                sp.eng.wait_ge(tensor_done, sp.at("tensor", ("chunk", k - NSLOT + trip), back=1))
            sp.eng.dma_start(ring[:, k % NSLOT, 0:n], src).then_inc(slot_loaded[k % NSLOT], sp.loaded())

        def product(out, w, rhs, n, width=P, at=0, tile=None):
            for k in range(n):
                ins = nc.tensor.matmul(out, w[:, at + k * width:at + (k + 1) * width], rhs[k],
                                       start=k == 0, stop=k == n - 1)
            return ins

        xn_tiles = [xn[:, k, :] for k in range(KD)]
        ones, ident = tab("ones"), tab("ident")

        def start_sync(sp):
            sp.eng.dma_start(tabbuf["all"][:, :], arrays["t_all"]).then_inc(consts_loaded, 16)
            sp.eng.dma_start(colbuf[:, :], arrays["columns"]).then_inc(consts_loaded, 16)
            for i in range(4):
                sp.eng.dma_start(x_rows[:, i, :], arrays["x"][P * i:P * (i + 1), :]).then_inc(x_loaded, 16)

        x_rows = arena[:, 0:4 * D].rearrange("p (i n) -> p i n", i=4)
        all_consts = 16 * 2

        def start_tensor(pe):
            pe.eng.wait_ge(consts_loaded, all_consts)
            pe.eng.wait_ge(x_loaded, 16 * 4)
            for k in range(KD):
                for i in range(4):
                    ins = nc.tensor.transpose(bank(k)[:, P * i:P * (i + 1)], x_rows[:, i, P * k:P * (k + 1)], ident)
                ins.then_inc(tensor_done, pe.mark(("x", k)))

        def start_vector(dve):
            dve.eng.wait_ge(consts_loaded, all_consts)
            for k in range(KD):
                dve.eng.wait_ge(tensor_done, dve.at("tensor", ("x", k)))
                nc.vector.tensor_copy(x[:, k, :], bank(k)).then_inc(vector_done, dve.mark("x" if k == KD - 1 else None))

        def norm_scalar(act, tag, src, dst, n, ready):
            act.eng.wait_ge(*ready)
            for k in range(n):
                nc.scalar.activation(dst[k], src[k], ACT.Square).then_inc(scalar_done, act.mark((tag, "square", k)))
            act.eng.wait_ge(vector_done, act.at("vector", (tag, "mean")))
            nc.scalar.activation(rstd[:, :], rstd[:, :], ACT.Sqrt).then_inc(scalar_done, act.mark((tag, "rstd")))

        def norm_tensor(pe, tag, dst, n, b=0):
            for k in range(n):
                pe.eng.wait_ge(scalar_done, pe.at("scalar", (tag, "square", k)))
                ins = nc.tensor.matmul(bank(b), ones, dst[k], start=k == 0, stop=k == n - 1)
            ins.then_inc(tensor_done, pe.mark((tag, "sum")))

        def norm_vector(dve, tag, src, dst, n, gain, b=0):
            dve.eng.wait_ge(tensor_done, dve.at("tensor", (tag, "sum")))
            dve.eng.wait_ge(vector_done, dve.now())
            nc.vector.tensor_scalar(rstd[:, :], bank(b), 1.0 / (n * P), EPS, ALU.mult, ALU.add).then_inc(vector_done, dve.mark())
            dve.eng.wait_ge(vector_done, dve.now())
            nc.vector.reciprocal(rstd[:, :], rstd[:, :]).then_inc(vector_done, dve.mark((tag, "mean")))
            dve.eng.wait_ge(vector_done, dve.now())
            dve.eng.wait_ge(scalar_done, dve.at("scalar", (tag, "rstd")))
            for k in range(n):
                nc.vector.scalar_tensor_tensor(dst[k], src[k], gain(k), rstd[:, :], ALU.mult, ALU.mult).then_inc(vector_done, dve.mark((tag, "normed", k)))

        x_tiles = [x[:, k, :] for k in range(KD)]

        def model_norm(n):
            return lambda k: col("gains", n * KD + k, 1)

        UP, DOWN = 2 * KF, 2 * KD
        UNITS = UP + DOWN

        def place_of(h, j, ahead=0):
            return (h + (j + ahead) // 2, (j + ahead) % 2)

        def unit_size(up):
            return (KD if up else KF // 2) * P

        def ffn_slot(e, j):
            return (e.chunk + j) % 2

        def ffn_slot_loaded(e, tag, h, j):
            return h * 16 + (16 + e.at(f"slot{ffn_slot(e, j)}", ("base", tag)))

        def ffn_sync(sp, tag, n, after_mixer):
            if after_mixer:
                for k in (1, 2):
                    sp.eng.wait_ge(tensor_done, sp.at("tensor", ("chunk", sp.chunk - k)))
            for k in range(2):
                c = counts[f"slot{k}"]
                seen[c.name, ("base", tag)] = (c.count, None)
            with sp.eng.Fori(0, KF // 2) as it:
                for j in range(2):
                    sp.eng.wait_ge(unit_ready, it * 4 + (UNITS * n + 2 * j + 2))
                    sp.eng.dma_start(ring[:, ffn_slot(sp, j), 0:2 * unit_size(True)],
                                     arrays["gate_up"][ds(it * 2 + (KF * n + j), 1)].rearrange("a p n -> (a p) n")).then_inc(slot_loaded[ffn_slot(sp, j)], 16)
            with sp.eng.Fori(0, KD // 2) as it:
                for j in range(2):
                    sp.eng.wait_ge(unit_ready, it * 4 + (UNITS * n + UP + 2 * j + 2))
                    sp.eng.dma_start(ring[:, ffn_slot(sp, j), 0:2 * unit_size(False)],
                                     arrays["down"][ds(it * 2 + (KD * n + j), 1)].rearrange("a p n -> (a p) n")).then_inc(slot_loaded[ffn_slot(sp, j)], 16)
            for k in range(2):
                counts[f"slot{k}"].count += 16 * UNITS // 4
            sp.chunk += UNITS // 2

        def split_product(out, b, hi, lo, tiles, start, stop):
            for m, k in enumerate(tiles):
                wh, wl = w_hi[:, b, P * m:P * (m + 1)], w_lo[:, b, P * m:P * (m + 1)]
                nc.tensor.matmul(out, wh, hi[:, k, :], start=start and m == 0, stop=False)
                nc.tensor.matmul(out, wh, lo[:, k, :], start=False, stop=False)
                ins = nc.tensor.matmul(out, wl, hi[:, k, :], start=False, stop=stop and m == len(tiles) - 1)
            return ins

        def ffn_tensor(pe, tag, n):
            for k in range(KD):
                pe.eng.wait_ge(scalar_done, pe.at("scalar", (tag, "square", k)))
                nc.tensor.matmul(bank(7), ones, work[:, k % 4, :], start=k == 0, stop=k == KD - 1).then_inc(
                    tensor_done, pe.mark((tag, "sum") if k == KD - 1 else (tag, "square used", k)))
            pe.eng.wait_ge(vector_done, pe.at("vector", (tag, "normed")))
            with pe.eng.Fori(0, KF // 2) as it:
                for j in range(2):
                    pe.eng.wait_ge(hidden_ready, it * 2 + (KF * n + j + 1))
                    pe.eng.wait_ge(unit_ready, it * 4 + (UNITS * n + 2 * j + 5))
                    split_product(bank(2 * j), 0, x_hi, x_lo, range(KD), True, True).then_inc(unit_used, 1)
                    pe.eng.wait_ge(unit_ready, it * 4 + (UNITS * n + 2 * j + 6))
                    split_product(bank(2 * j + 1), 1, x_hi, x_lo, range(KD), True, True).then_inc(unit_used, 1)
            pe.eng.wait_ge(hidden_ready, KF * (n + 1) + 2)
            with pe.eng.Fori(0, KD // 2) as it:
                for j in range(2):
                    pe.eng.wait_ge(x_updated, it * 2 + (KD * n + j + 1))
                    pe.eng.wait_ge(unit_ready, it * 4 + (UNITS * n + UP + 2 * j + 5))
                    split_product(bank(4 + j), 0, hid_hi, hid_lo, range(KF // 2), True, False).then_inc(unit_used, 1)
                    pe.eng.wait_ge(unit_ready, it * 4 + (UNITS * n + UP + 2 * j + 6))
                    split_product(bank(4 + j), 1, hid_hi, hid_lo, range(KF // 2, KF), False, True).then_inc(unit_used, 1)
            pe.chunk += UNITS // 2

        def ffn_scalar(act, tag, n, ready):
            act.eng.wait_ge(*ready)
            for k in range(KD):
                if k >= 4:
                    act.eng.wait_ge(tensor_done, act.at("tensor", (tag, "square used", k - 4)))
                nc.scalar.activation(work[:, k % 4, :], x[:, k, :], ACT.Square).then_inc(scalar_done, act.mark((tag, "square", k)))

            def split_hi(h, j, up):
                for b in range(2):
                    if b == 0:
                        act.eng.wait_ge(slot_loaded[ffn_slot(act, j)], ffn_slot_loaded(act, tag, h, j))
                    act.eng.wait_ge(unit_used, h * 4 + (UNITS * n + 2 * j + b + 1))
                    nc.scalar.copy(w_hi[:, b, 0:unit_size(up)],
                                   ring[:, ffn_slot(act, j), unit_size(up) * b:unit_size(up) * (b + 1)]).then_inc(unit_hi, 1)
                    if b == 0:
                        yield

            def up_step(h, j, last=False):
                ahead = split_hi(*place_of(h, j, 1), up=not last)
                next(ahead)
                act.eng.wait_ge(unit_used, h * 4 + (UNITS * n + 2 * j + 3))
                act.eng.wait_ge(hidden_ready, h * 2 + (KF * n + j + 1))
                nc.scalar.activation(work[:, j, :], bank(2 * j), ACT.Silu).then_inc(silu_ready, 1)
                for _ in ahead:
                    pass

            for _ in split_hi(0, 0, True):
                pass
            act.eng.wait_ge(vector_done, act.at("vector", (tag, "mean")))
            nc.scalar.activation(rstd[:, :], rstd[:, :], ACT.Sqrt).then_inc(scalar_done, act.mark((tag, "rstd")))
            for k in range(KD):
                act.eng.wait_ge(vector_done, act.at("vector", (tag, "y", k)))
                nc.scalar.copy(x_hi[:, k, :], work[:, k % 4, :]).then_inc(scalar_done, act.mark((tag, "x_hi", k)))
            with act.eng.Fori(0, KF // 2 - 1) as it:
                for j in range(2):
                    up_step(it, j)
            up_step(KF // 2 - 1, 0)
            up_step(KF // 2 - 1, 1, last=True)
            with act.eng.Fori(0, KD // 2 - 1) as it:
                for j in range(2):
                    for _ in split_hi(*place_of(it + KF // 2, j, 1), up=False):
                        pass
            for _ in split_hi(KF // 2 + KD // 2 - 1, 1, up=False):
                pass
            act.chunk += UNITS // 2

        def ffn_vector(dve, tag, n, gain, scale):
            def split_lo(h, j, up):
                for b in range(2):
                    dve.eng.wait_ge(unit_hi, h * 4 + (UNITS * n + 2 * j + b + 1))
                    size = unit_size(up)
                    nc.vector.tensor_tensor(w_lo[:, b, 0:size], ring[:, ffn_slot(dve, j), size * b:size * (b + 1)],
                                            w_hi[:, b, 0:size].bitcast(F32), ALU.subtract).then_inc(unit_ready, 1)

            def up_step(h, j, last=False):
                split_lo(*place_of(h, j, 1), up=not last)
                dve.eng.wait_ge(silu_ready, h * 2 + (KF * n + j + 1))
                dve.eng.wait_ge(unit_used, h * 4 + (UNITS * n + 2 * j + 4))
                dve.eng.wait_ge(hidden_ready, h * 2 + (KF * n + j + 1))
                prod = work[:, 2 + j, :]
                tile = lambda t: (t[:, ds(h * 2 + j, 1), :]).rearrange("p a t -> p (a t)")
                nc.vector.tensor_tensor(prod, work[:, j, :], bank(2 * j + 1), ALU.mult).then_inc(vector_done, dve.mark())
                dve.eng.wait_ge(vector_done, dve.now())
                nc.vector.tensor_copy(tile(hid_hi), prod).then_inc(vector_done, dve.mark())
                dve.eng.wait_ge(vector_done, dve.now())
                nc.vector.tensor_tensor(tile(hid_lo), prod, tile(hid_hi).bitcast(F32), ALU.subtract).then_inc(hidden_ready, 1)

            def down_step(h, j, last=False):
                if not last:
                    split_lo(*place_of(h + KF // 2, j, 1), up=False)
                dve.eng.wait_ge(unit_used, h * 4 + (UNITS * n + UP + 2 * j + 4))
                tile = x[:, ds(h * 2 + j, 1), :].rearrange("p a t -> p (a t)")
                nc.vector.scalar_tensor_tensor(tile, bank(4 + j), scale, tile, ALU.mult, ALU.add).then_inc(x_updated, 1)

            dve.eng.wait_ge(tensor_done, dve.at("tensor", (tag, "sum")))
            nc.vector.tensor_scalar(rstd[:, :], bank(7), 1.0 / D, EPS, ALU.mult, ALU.add).then_inc(vector_done, dve.mark())
            dve.eng.wait_ge(vector_done, dve.now())
            nc.vector.reciprocal(rstd[:, :], rstd[:, :]).then_inc(vector_done, dve.mark((tag, "mean")))
            split_lo(0, 0, True)
            dve.eng.wait_ge(scalar_done, dve.at("scalar", (tag, "rstd")))
            for k in range(KD + 1):
                if k < KD:
                    if k >= 4:
                        dve.eng.wait_ge(vector_done, dve.at("vector", (tag, "x_lo", k - 4)))
                    nc.vector.scalar_tensor_tensor(work[:, k % 4, :], x[:, k, :], col("gains", gain * KD + k, 1), rstd[:, :],
                                                   ALU.mult, ALU.mult).then_inc(vector_done, dve.mark((tag, "y", k)))
                if k >= 1:
                    dve.eng.wait_ge(scalar_done, dve.at("scalar", (tag, "x_hi", k - 1)))
                    dve.eng.wait_ge(vector_done, dve.at("vector", (tag, "y", k - 1)))
                    nc.vector.tensor_tensor(x_lo[:, k - 1, :], work[:, (k - 1) % 4, :], x_hi[:, k - 1, :].bitcast(F32),
                                            ALU.subtract).then_inc(vector_done, dve.mark((tag, "normed") if k == KD else (tag, "x_lo", k - 1)))
            with dve.loop(KF // 2 - 1, (tag, "up")) as it:
                for j in range(2):
                    up_step(it, j)
            up_step(KF // 2 - 1, 0)
            up_step(KF // 2 - 1, 1, last=True)
            with dve.eng.Fori(0, KD // 2 - 1) as it:
                for j in range(2):
                    down_step(it, j)
            down_step(KD // 2 - 1, 0)
            down_step(KD // 2 - 1, 1, last=True)
            dve.chunk += UNITS // 2

        def out_sync(sp, tag, name, n):
            with sp.loop(KD // 2, (tag, "out")) as it:
                sp.first = sp.chunk
                for j in range(2):
                    load(sp, arrays[name][ds(it * 2 + j, 1)].rearrange("a p n -> (a p) n"), n * P, 2)

        def out_tensor(pe, tag, mixed, n):
            with pe.loop(KD // 2, (tag, "out")):
                for j in range(2):
                    pe.eng.wait_ge(slot_loaded[pe.slot()], pe.chunk_loaded())
                    w = ring[:, pe.slot(), :]
                    pe.eng.wait_ge(vector_done, pe.at("vector", (tag, "x", j), back=1))
                    product(bank(j), w, mixed, n).then_inc(tensor_done, pe.used())

        def out_vector(dve, tag):
            first = dve.chunk
            with dve.loop(KD // 2, (tag, "out")) as it:
                for j in range(2):
                    dve.eng.wait_ge(tensor_done, dve.at("tensor", ("chunk", first + j)))
                    tile = x[:, ds(it * 2 + j, 1), :].rearrange("p a t -> p (a t)")
                    nc.vector.tensor_tensor(tile, bank(j), tile, ALU.add).then_inc(vector_done, dve.mark((tag, "x", j)))
            dve.chunk += 2

        y_rows = arena[:, 0:4 * D].rearrange("p (i n) -> p i n", i=4)

        def end_tensor(pe, ready):
            pe.eng.wait_ge(vector_done, pe.at("vector", ready))
            for i in range(4):
                for h in range(2):
                    for k in range(4):
                        ins = nc.tensor.transpose(bank(2 * i + h)[:, P * k:P * (k + 1)],
                                                  xn[:, 4 * h + k, P * i:P * (i + 1)], ident)
                    ins.then_inc(tensor_done, pe.mark(("y", i, h)))

        def end_vector(dve):
            for i in range(4):
                for h in range(2):
                    dve.eng.wait_ge(tensor_done, dve.at("tensor", ("y", i, h)))
                    nc.vector.tensor_copy(y_rows[:, i, 512 * h:512 * (h + 1)], bank(2 * i + h)).then_inc(vector_done, dve.mark(("y", i, h)))

        def end_sync(sp):
            for i in range(4):
                sp.eng.wait_ge(vector_done, sp.at("vector", ("y", i, 1)))
                sp.eng.dma_start(out[P * i:P * (i + 1), :], y_rows[:, i, :]).then_inc(stored, 16)
            sp.eng.wait_ge(stored, 16 * 4)

        MIXERS = {}

        CH = 128
        NC_ = T // CH
        carve_reset()
        ab_mixed = carve(8, T)
        ab_mixed_tiles = [ab_mixed[:, k, :] for k in range(8)]
        rows = carve(14, T)
        ROW = {n: i for i, n in enumerate(["li", "f", "af", "lf", "b", "c", "M", "m", "sc", "wk", "one", "em", "t0", "t1"])}
        row = lambda n, a=0, w=T: rows[0:4, ROW[n], a:a + w]
        spread = carve(3, 4, T)
        rcol = carve(2, NC_, 4)
        lam = carve(12, 4)
        lamx = lambda i: lam[:, i, :]
        small0 = carve_at[0]
        rg = carve(10, T)
        RG = {n: i for i, n in enumerate(["conv", "r", "ig", "a", "t", "u", "gelu", "h", "v", "w"])}
        rgt = lambda n: rg[:, RG[n], :]
        carve_reset(small0)
        ml = carve(12, T)
        ML = {n: i for i, n in enumerate(["q", "k", "qs", "E", "P", "kw", "ho", "o", "den", "sq", "rs", "cq"])}
        mlt = lambda n: ml[:, ML[n], :]
        mv = carve(NC_, 2 * P)
        state = carve(3, 2 * P)

        def ab_sync(sp):
            load(sp, arrays["ab_gates"][0], 64)
            with sp.loop(4, "rg") as it:
                sp.first = sp.chunk
                for j, n in enumerate((1280, 1024)):
                    load(sp, arrays["rg"][ds(it * 2 + j, 1), :, 0:n].rearrange("a p n -> (a p) n"), n, 2)
            with sp.loop(4, "ml") as it:
                sp.first = sp.chunk
                for j in range(2):
                    load(sp, arrays["ml"][ds(it * 2 + j, 1)].rearrange("a p n -> (a p) n"), 2048, 2)
            out_sync(sp, "ab", "ab_out", 8)

        def ab_tensor(pe):
            norm_tensor(pe, "ab", xn_tiles, KD)
            pe.eng.wait_ge(vector_done, pe.at("vector", ("ab", "normed", KD - 1)))
            pe.eng.wait_ge(slot_loaded[pe.slot()], pe.chunk_loaded())
            w = ring[:, pe.slot(), :]
            product(bank(1)[0:4, :], w, xn_tiles, KD, width=4).then_inc(tensor_done, pe.mark("ml i"))
            product(bank(2)[0:4, :], w, xn_tiles, KD, width=4, at=32).then_inc(tensor_done, pe.used())
            pe.eng.wait_ge(scalar_done, pe.at("scalar", "ml wk"))
            for a, n in enumerate(("c", "wk")):
                for c in range(NC_):
                    ins = nc.tensor.transpose(bank(3)[:, (a * NC_ + c) * 4:(a * NC_ + c) * 4 + 4], row(n, c * CH, CH), ident[0:4, 0:4])
            ins.then_inc(tensor_done, pe.mark("ml cols"))
            with pe.loop(4, "rg"):
                pe.eng.wait_ge(vector_done, pe.at("vector", "rg mixed", back=1))
                pe.eng.wait_ge(slot_loaded[pe.slot()], pe.chunk_loaded())
                w = ring[:, pe.slot(), :]
                product(bank(4), w, xn_tiles, KD).then_inc(tensor_done, pe.mark("rg xa"))
                pe.eng.wait_ge(vector_done, pe.at("vector", "rg conv"))
                nc.tensor.matmul(bank(6), w[:, 1024:1152], rgt("conv"), start=True, stop=True).then_inc(tensor_done, pe.mark("rg r"))
                nc.tensor.matmul(bank(7), w[:, 1152:1280], rgt("conv"), start=True, stop=True).then_inc(tensor_done, pe.used())
                pe.eng.wait_ge(slot_loaded[pe.slot()], pe.chunk_loaded())
                w = ring[:, pe.slot(), :]
                product(bank(5), w, xn_tiles, KD).then_inc(tensor_done, pe.used())
            pe.eng.wait_ge(vector_done, pe.at("vector", "rg mixed"))
            pe.eng.wait_ge(vector_done, pe.at("vector", "ml rows"))
            with pe.loop(4, "ml") as it:
                pe.eng.wait_ge(vector_done, pe.at("vector", "ml mixed", back=1))
                pe.eng.wait_ge(slot_loaded[pe.slot()], pe.chunk_loaded())
                w = ring[:, pe.slot(), :]
                product(bank(0), w, xn_tiles, KD).then_inc(tensor_done, pe.mark("ml q"))
                product(bank(1), w, xn_tiles, KD, at=1024).then_inc(tensor_done, pe.used())
                pe.eng.wait_ge(slot_loaded[pe.slot()], pe.chunk_loaded())
                w = ring[:, pe.slot(), :]
                for i in range(NC_):
                    for k in range(KD):
                        ins = nc.tensor.matmul(bank(2)[:, P * i:P * (i + 1)], xn[:, k, P * i:P * (i + 1)],
                                               w[:, P * k:P * (k + 1)], start=k == 0, stop=k == KD - 1)
                ins.then_inc(tensor_done, pe.mark("ml v"))
                product(bank(3), w, xn_tiles, KD, at=1024).then_inc(tensor_done, pe.used())
                nc.tensor.matmul(bank(4), ones[0:4, :], spread[0:4, 0, ds(it, 1), :].rearrange("p a t -> p (a t)"), start=True, stop=False)
                nc.tensor.matmul(bank(4), ident, tab("future"), start=False, stop=True).then_inc(tensor_done, pe.mark("ml M"))
                nc.tensor.matmul(bank(5), ones[0:4, :], spread[0:4, 1, ds(it, 1), :].rearrange("p a t -> p (a t)"), start=True, stop=True).then_inc(tensor_done, pe.mark("ml sc"))
                nc.tensor.matmul(bank(6), ones[0:4, :], spread[0:4, 2, ds(it, 1), :].rearrange("p a t -> p (a t)"), start=True, stop=True).then_inc(tensor_done, pe.mark("ml em"))
                pe.eng.wait_ge(scalar_done, pe.at("scalar", "ml qk silu"))
                for c in range(NC_):
                    ins = nc.tensor.matmul(bank(7)[:, c * CH:(c + 1) * CH], mlt("k")[:, c * CH:(c + 1) * CH],
                                           mlt("q")[:, c * CH:(c + 1) * CH], start=True, stop=True)
                ins.then_inc(tensor_done, pe.mark("ml s"))
                for c in range(NC_ - 1):
                    ins = nc.tensor.transpose(bank(0)[:, c * CH:(c + 1) * CH], mlt("k")[:, c * CH:(c + 1) * CH], ident)
                ins.then_inc(tensor_done, pe.mark("ml kT"))
                pe.eng.wait_ge(vector_done, pe.at("vector", "ml v"))
                pe.eng.wait_ge(vector_done, pe.at("vector", "ml kw"))
                for c in range(NC_ - 1):
                    ins = nc.tensor.matmul(bank(1 + c // 2)[:, 256 * (c % 2):256 * (c % 2) + 256],
                                           mlt("kw")[:, c * CH:(c + 1) * CH], mv[:, c, :], start=True, stop=True)
                ins.then_inc(tensor_done, pe.mark("ml state"))
                pe.eng.wait_ge(vector_done, pe.at("vector", "ml P"))
                pe.eng.wait_ge(vector_done, pe.at("vector", "ml states"))
                for c in range(NC_):
                    at = slice(c * CH, (c + 1) * CH)
                    nc.tensor.matmul(bank(4)[:, at], mv[:, c, 0:P], mlt("P")[:, at], start=True, stop=c == 0)
                    if c:
                        nc.tensor.matmul(bank(4)[:, at], state[:, c - 1, 0:P], mlt("qs")[:, at], start=False, stop=True)
                for c in range(NC_):
                    at = slice(c * CH, (c + 1) * CH)
                    ins = nc.tensor.matmul(bank(7)[:, at], ones, mlt("P")[:, at], start=True, stop=c == 0)
                    if c:
                        ins = nc.tensor.matmul(bank(7)[:, at], state[:, c - 1, P:2 * P], mlt("qs")[:, at], start=False, stop=True)
                ins.then_inc(tensor_done, pe.mark("ml den"))
                pe.eng.wait_ge(scalar_done, pe.at("scalar", "ml sq"))
                nc.tensor.matmul(bank(0), ones, mlt("sq"), start=True, stop=True).then_inc(tensor_done, pe.mark("ml ss"))
            pe.eng.wait_ge(vector_done, pe.at("vector", "ml mixed"))
            out_tensor(pe, "ab", ab_mixed_tiles, 8)

        def ab_scalar(act, ready):
            norm_scalar(act, "ab", x_tiles, xn_tiles, KD, ready)
            act.eng.wait_ge(vector_done, act.at("vector", "rg |lam|"))
            nc.scalar.activation(lamx(1), lamx(0), ACT.Exp, scale=-1.0).then_inc(scalar_done, act.mark("rg exp lam"))
            act.eng.wait_ge(vector_done, act.at("vector", "ml |f|"))
            nc.scalar.activation(row("t0"), row("af"), ACT.Exp, scale=-1.0).then_inc(scalar_done, act.mark())
            act.eng.wait_ge(scalar_done, act.now())
            nc.scalar.activation(row("t1"), row("t0"), ACT.Ln, bias=1.0).then_inc(scalar_done, act.mark("ml ln"))
            act.eng.wait_ge(vector_done, act.at("vector", "ml m"))
            nc.scalar.activation(row("sc"), row("t0"), ACT.Exp).then_inc(scalar_done, act.mark("ml sc"))
            nc.scalar.activation(row("em"), row("m"), ACT.Exp, scale=-1.0).then_inc(scalar_done, act.mark("ml em"))
            nc.scalar.activation(row("wk"), row("t1"), ACT.Exp).then_inc(scalar_done, act.mark("ml wk"))
            with act.loop(4, "rg") as it:
                act.eng.wait_ge(tensor_done, act.at("tensor", "rg r"))
                nc.scalar.activation(rgt("r"), bank(6), ACT.Sigmoid, bias=dyn_col("rg_br", it, 1)).then_inc(scalar_done, act.mark())
                act.eng.wait_ge(tensor_done, act.at("tensor", ("chunk", act.chunk + 1)))
                nc.scalar.activation(rgt("ig"), bank(7), ACT.Sigmoid, bias=dyn_col("rg_bi", it, 1)).then_inc(scalar_done, act.mark("rg ig"))
                act.eng.wait_ge(scalar_done, act.now())
                nc.scalar.activation(rgt("a"), rgt("r"), ACT.Exp, scale=lam[:, 11, ds(it, 1)]).then_inc(scalar_done, act.mark("rg a"))
                nc.scalar.activation(rgt("t"), rgt("r"), ACT.Tanh, scale=lam[:, 11, ds(it, 1)]).then_inc(scalar_done, act.mark("rg t"))
                act.eng.wait_ge(vector_done, act.at("vector", "rg u2"))
                nc.scalar.activation(rgt("u"), rgt("u"), ACT.Sqrt).then_inc(scalar_done, act.mark("rg sqrt"))
                act.eng.wait_ge(tensor_done, act.at("tensor", ("chunk", act.chunk + 2)))
                nc.scalar.activation(rgt("gelu"), bank(5), ACT.Gelu_apprx_tanh).then_inc(scalar_done, act.mark("rg gelu"))
            with act.loop(4, "ml") as it:
                act.eng.wait_ge(vector_done, act.at("vector", "ml qk conv"))
                nc.scalar.activation(mlt("q"), mlt("qs"), ACT.Silu).then_inc(scalar_done, act.mark())
                nc.scalar.activation(mlt("k"), mlt("cq"), ACT.Silu).then_inc(scalar_done, act.mark("ml qk silu"))
                act.eng.wait_ge(tensor_done, act.at("tensor", ("chunk", act.chunk + 4)))
                nc.scalar.activation(mlt("o"), bank(3), ACT.Sigmoid).then_inc(scalar_done, act.mark("ml o"))
                act.eng.wait_ge(tensor_done, act.at("tensor", "ml M"))
                for c in range(NC_):
                    at = slice(c * CH, (c + 1) * CH)
                    nc.scalar.activation(mlt("E")[:, at], bank(4)[:, at], ACT.Exp, scale=-1.0,
                                                  bias=rcol[:, 0, c, ds(it, 1)]).then_inc(scalar_done, act.mark("ml E" if c == NC_ - 1 else None))
                act.eng.wait_ge(tensor_done, act.at("tensor", "ml den"))
                nc.scalar.activation(mlt("den"), bank(7), ACT.Abs).then_inc(scalar_done, act.mark("ml |den|"))
                act.eng.wait_ge(vector_done, act.at("vector", "ml h"))
                nc.scalar.activation(mlt("sq"), mlt("ho"), ACT.Square).then_inc(scalar_done, act.mark("ml sq"))
                act.eng.wait_ge(vector_done, act.at("vector", "ml mean"))
                nc.scalar.activation(mlt("rs"), mlt("rs"), ACT.Sqrt).then_inc(scalar_done, act.mark("ml rstd"))
            act.chunk += 7

        def conv4(dve, out, src, taps, bias):
            nc.vector.tensor_scalar(out, src, taps(3), bias, ALU.mult, ALU.add).then_inc(vector_done, dve.mark())
            dve.eng.wait_ge(vector_done, dve.now())
            for j in (1, 2, 3):
                ins = nc.vector.scalar_tensor_tensor(out[:, j:T], src[:, 0:T - j], taps(3 - j), out[:, j:T], ALU.mult, ALU.add)
                if j < 3:
                    ins.then_inc(vector_done, dve.mark())
                    dve.eng.wait_ge(vector_done, dve.now())
            return ins

        def ab_vector(dve):
            norm_vector(dve, "ab", x_tiles, xn_tiles, KD, model_norm(1))
            first = dve.chunk
            la = col("rg_lam")
            nc.vector.scalar_tensor_tensor(lamx(0), la, -1.0, la, ALU.mult, ALU.max).then_inc(vector_done, dve.mark("rg |lam|"))
            dve.eng.wait_ge(vector_done, dve.now())
            dve.eng.wait_ge(scalar_done, dve.at("scalar", "rg exp lam"))
            nc.vector.tensor_scalar(lamx(2), lamx(1), 2.0, None, ALU.add).then_inc(vector_done, dve.mark())
            dve.eng.wait_ge(vector_done, dve.now())
            nc.vector.reciprocal(lamx(2), lamx(2)).then_inc(vector_done, dve.mark())
            dve.eng.wait_ge(vector_done, dve.now())
            nc.vector.tensor_tensor(lamx(3), lamx(1), lamx(2), ALU.mult).then_inc(vector_done, dve.mark())
            dve.eng.wait_ge(vector_done, dve.now())
            nc.vector.tensor_tensor(lamx(4), lamx(3), lamx(3), ALU.mult).then_inc(vector_done, dve.mark())
            dve.eng.wait_ge(vector_done, dve.now())
            nc.vector.tensor_scalar(lamx(5), lamx(4), 1.0 / 17, None, ALU.mult).then_inc(vector_done, dve.mark())
            dve.eng.wait_ge(vector_done, dve.now())
            for n in (15, 13, 11, 9, 7, 5, 3):
                nc.vector.scalar_tensor_tensor(lamx(5), lamx(5), 1.0 / n, lamx(4), ALU.add, ALU.mult).then_inc(vector_done, dve.mark())
                dve.eng.wait_ge(vector_done, dve.now())
            nc.vector.scalar_tensor_tensor(lamx(5), lamx(5), 1.0, lamx(3), ALU.add, ALU.mult).then_inc(vector_done, dve.mark())
            dve.eng.wait_ge(vector_done, dve.now())
            nc.vector.tensor_scalar(lamx(6), la, -1.0, 0.0, ALU.mult, ALU.max).then_inc(vector_done, dve.mark())
            dve.eng.wait_ge(vector_done, dve.now())
            nc.vector.scalar_tensor_tensor(lamx(7), lamx(5), 2.0, lamx(6), ALU.mult, ALU.add).then_inc(vector_done, dve.mark())
            dve.eng.wait_ge(vector_done, dve.now())
            nc.vector.tensor_scalar(lamx(11), lamx(7), -8.0, None, ALU.mult).then_inc(vector_done, dve.mark())
            dve.eng.wait_ge(vector_done, dve.now())
            dve.eng.wait_ge(tensor_done, dve.at("tensor", "ml i"))
            nc.vector.tensor_scalar(row("li"), bank(1)[0:4, :], col("ml_bi")[0:4, :], None, ALU.add).then_inc(vector_done, dve.mark())
            dve.eng.wait_ge(tensor_done, dve.at("tensor", ("chunk", first)))
            nc.vector.tensor_scalar(row("f"), bank(2)[0:4, :], col("ml_bf")[0:4, :], None, ALU.add).then_inc(vector_done, dve.mark())
            dve.eng.wait_ge(vector_done, dve.now())
            nc.vector.scalar_tensor_tensor(row("af"), row("f"), -1.0, row("f"), ALU.mult, ALU.max).then_inc(vector_done, dve.mark("ml |f|"))
            nc.vector.memset(row("one"), 1.0).then_inc(vector_done, dve.mark())
            dve.eng.wait_ge(scalar_done, dve.at("scalar", "ml ln"))
            nc.vector.scalar_tensor_tensor(row("lf"), row("f"), 0.0, row("t1"), ALU.min, ALU.subtract).then_inc(vector_done, dve.mark())
            dve.eng.wait_ge(vector_done, dve.now())
            for c in range(NC_):
                ins = nc.vector.tensor_tensor_scan(row("b", c * CH, CH), row("one", c * CH, CH), row("lf", c * CH, CH), 0.0, ALU.mult, ALU.add)
                ins.then_inc(vector_done, dve.mark())
            dve.eng.wait_ge(vector_done, dve.now())
            nc.vector.tensor_tensor(row("c"), row("li"), row("b"), ALU.subtract).then_inc(vector_done, dve.mark())
            dve.eng.wait_ge(vector_done, dve.now())
            for c in range(NC_):
                m0 = NEG if c == 0 else row("m", c * CH - 1, 1)
                nc.vector.tensor_tensor_scan(row("M", c * CH, CH), row("c", c * CH, CH), row("c", c * CH, CH), m0, ALU.max, ALU.max).then_inc(vector_done, dve.mark())
                dve.eng.wait_ge(vector_done, dve.now())
                nc.vector.tensor_tensor(row("m", c * CH, CH), row("M", c * CH, CH), row("b", c * CH, CH), ALU.add).then_inc(vector_done, dve.mark())
                nc.vector.tensor_scalar(row("t0", c * CH, CH), row("M", c * CH, CH), -1.0, m0, ALU.mult, ALU.add).then_inc(vector_done, dve.mark())
                nc.vector.tensor_scalar(row("t1", c * CH, CH), row("c", c * CH, CH), row("M", (c + 1) * CH - 1, 1), None, ALU.subtract).then_inc(vector_done, dve.mark("ml m" if c == NC_ - 1 else None))
                dve.eng.wait_ge(vector_done, dve.now())
            dve.eng.wait_ge(scalar_done, dve.at("scalar", "ml wk"))
            for a, n in enumerate(("M", "sc", "em")):
                for h in range(4):
                    nc.vector.tensor_scalar(spread[0:4, a, h, :], row(n), tab("sel4", h, 1)[0:4, :], None, ALU.mult).then_inc(vector_done, dve.mark())
            dve.eng.wait_ge(tensor_done, dve.at("tensor", "ml cols"))
            nc.vector.tensor_copy(rcol[:, :, :, :], bank(3)[:, 0:2 * NC_ * 4].rearrange("p (a c h) -> p a c h", a=2, c=NC_)).then_inc(vector_done, dve.mark("ml rows"))
            with dve.loop(4, "rg") as it:
                dve.eng.wait_ge(tensor_done, dve.at("tensor", "rg xa"))
                conv4(dve, rgt("conv"), bank(4), lambda j: dyn_col("rg_taps", it, 4, j), dyn_col("rg_cb", it, 1)).then_inc(vector_done, dve.mark("rg conv"))
                dve.eng.wait_ge(scalar_done, dve.at("scalar", "rg t"))
                nc.vector.tensor_tensor(rgt("v"), rgt("a"), rgt("a"), ALU.mult).then_inc(vector_done, dve.mark())
                dve.eng.wait_ge(vector_done, dve.now())
                nc.vector.scalar_tensor_tensor(rgt("w"), rgt("v"), 1.0, rgt("t"), ALU.add, ALU.mult).then_inc(vector_done, dve.mark())
                dve.eng.wait_ge(vector_done, dve.now())
                nc.vector.tensor_scalar(rgt("u"), rgt("w"), -1.0, 0.0, ALU.mult, ALU.max).then_inc(vector_done, dve.mark("rg u2"))
                dve.eng.wait_ge(vector_done, dve.now())
                nc.vector.tensor_tensor(rgt("v"), rgt("ig"), rgt("conv"), ALU.mult).then_inc(vector_done, dve.mark())
                dve.eng.wait_ge(vector_done, dve.now())
                dve.eng.wait_ge(scalar_done, dve.at("scalar", "rg sqrt"))
                nc.vector.tensor_tensor(rgt("w"), rgt("v"), rgt("u"), ALU.mult).then_inc(vector_done, dve.mark())
                dve.eng.wait_ge(vector_done, dve.now())
                nc.vector.tensor_tensor_scan(rgt("h"), rgt("a"), rgt("w"), 0.0, ALU.mult, ALU.add).then_inc(vector_done, dve.mark())
                dve.eng.wait_ge(vector_done, dve.now())
                dve.eng.wait_ge(scalar_done, dve.at("scalar", "rg gelu"))
                nc.vector.tensor_tensor(ab_mixed[:, ds(it, 1), :].rearrange("p a t -> p (a t)"), rgt("gelu"), rgt("h"), ALU.mult).then_inc(vector_done, dve.mark("rg mixed"))
            for c in range(NC_):
                nc.vector.memset(mv[:, c, P:2 * P], 1.0).then_inc(vector_done, dve.mark())
            scale = float(P) ** -0.5
            with dve.loop(4, "ml") as it:
                dve.eng.wait_ge(tensor_done, dve.at("tensor", "ml q"))
                conv4(dve, mlt("qs"), bank(0), lambda j: dyn_col("ml_taps", it, 4, j), dyn_col("ml_cb", it, 1)).then_inc(vector_done, dve.mark())
                dve.eng.wait_ge(tensor_done, dve.at("tensor", ("chunk", first + 3)))
                conv4(dve, mlt("cq"), bank(1), lambda j: dyn_col("ml_taps", it, 4, 16 + j), dyn_col("ml_cb", it, 1, 4)).then_inc(vector_done, dve.mark("ml qk conv"))
                dve.eng.wait_ge(tensor_done, dve.at("tensor", "ml v"))
                nc.vector.tensor_copy(mv[:, :, 0:P], bank(2).rearrange("p (c n) -> p c n", c=NC_)).then_inc(vector_done, dve.mark("ml v"))
                dve.eng.wait_ge(tensor_done, dve.at("tensor", "ml kT"))
                for c in range(NC_ - 1):
                    nc.vector.tensor_scalar(mlt("kw")[:, c * CH:(c + 1) * CH], bank(0)[:, c * CH:(c + 1) * CH],
                                                     rcol[:, 1, c, ds(it, 1)], None, ALU.mult).then_inc(vector_done, dve.mark("ml kw" if c == NC_ - 2 else None))
                dve.eng.wait_ge(scalar_done, dve.at("scalar", "ml E"))
                dve.eng.wait_ge(tensor_done, dve.at("tensor", "ml s"))
                nc.vector.scalar_tensor_tensor(mlt("P"), bank(7), scale, mlt("E"), ALU.mult, ALU.mult).then_inc(vector_done, dve.mark("ml P"))
                dve.eng.wait_ge(tensor_done, dve.at("tensor", "ml sc"))
                nc.vector.scalar_tensor_tensor(mlt("qs"), mlt("q"), scale, bank(5), ALU.mult, ALU.mult).then_inc(vector_done, dve.mark())
                dve.eng.wait_ge(tensor_done, dve.at("tensor", "ml state"))
                nc.vector.tensor_copy(mlt("rs")[:, 0:4], bank(5)[:, CH - 1:T:CH]).then_inc(vector_done, dve.mark())
                nc.vector.tensor_copy(state[:, 0, :], bank(1)[:, 0:256]).then_inc(vector_done, dve.mark())
                dve.eng.wait_ge(vector_done, dve.now())
                for c in (1, 2):
                    nc.vector.scalar_tensor_tensor(state[:, c, :], state[:, c - 1, :], mlt("rs")[:, c:c + 1],
                                                             bank(1 + c // 2)[:, 256 * (c % 2):256 * (c % 2) + 256], ALU.mult, ALU.add).then_inc(vector_done, dve.mark("ml states" if c == 2 else None))
                    dve.eng.wait_ge(vector_done, dve.now())
                dve.eng.wait_ge(scalar_done, dve.at("scalar", "ml |den|"))
                nc.vector.tensor_tensor(mlt("den"), mlt("den"), bank(6), ALU.max).then_inc(vector_done, dve.mark())
                dve.eng.wait_ge(vector_done, dve.now())
                nc.vector.reciprocal(mlt("den"), mlt("den")).then_inc(vector_done, dve.mark())
                dve.eng.wait_ge(vector_done, dve.now())
                nc.vector.tensor_tensor(mlt("ho"), mlt("den"), bank(4), ALU.mult).then_inc(vector_done, dve.mark("ml h"))
                dve.eng.wait_ge(vector_done, dve.now())
                dve.eng.wait_ge(tensor_done, dve.at("tensor", "ml ss"))
                nc.vector.tensor_scalar(mlt("rs"), bank(0), 1.0 / P, EPS, ALU.mult, ALU.add).then_inc(vector_done, dve.mark())
                dve.eng.wait_ge(vector_done, dve.now())
                nc.vector.reciprocal(mlt("rs"), mlt("rs")).then_inc(vector_done, dve.mark("ml mean"))
                dve.eng.wait_ge(vector_done, dve.now())
                dve.eng.wait_ge(scalar_done, dve.at("scalar", "ml rstd"))
                nc.vector.scalar_tensor_tensor(mlt("den"), mlt("ho"), dyn_col("ml_norm", it, 1), mlt("rs"), ALU.mult, ALU.mult).then_inc(vector_done, dve.mark())
                dve.eng.wait_ge(vector_done, dve.now())
                nc.vector.tensor_tensor(ab_mixed[:, ds(it + 4, 1), :].rearrange("p a t -> p (a t)"), mlt("den"), mlt("o"), ALU.mult).then_inc(vector_done, dve.mark("ml mixed"))
            dve.chunk += 5
            out_vector(dve, "ab")

        MIXERS["ab"] = {"sync": ab_sync, "tensor": ab_tensor, "scalar": ab_scalar, "vector": ab_vector}

        class Step:

            def __init__(self, scores, masks, parts, values, out, group, gates=None, any_key=None):
                self.scores, self.masks, self.parts, self.values, self.out = scores, masks, parts, values, out
                self.group, self.gates, self.any_key = group, gates, any_key

        def att_carve():
            return carve(2, 2 * T), carve(2, 2 * T), carve(2, 12)

        def area(n):
            return psum[:, 2 * (n % 2):2 * (n % 2) + 2, :].rearrange("p b t -> p (b t)")

        def place(step, m):
            first = len(step.values) // 2
            return m if m < first else 4 + m - first

        def turned_blocks(step, b):
            runs = []
            for m, (_, keys, _) in enumerate(step.values):
                at = place(step, m)
                if at // 4 == b:
                    if runs and runs[-1][2] == keys:
                        runs[-1] = (runs[-1][0], at + 1, keys)
                    else:
                        runs.append((at, at + 1, keys))
            return runs

        def att_tensor(pe, tag, steps, buf):
            p, pT, _ = buf
            turned = psum[:, 4:6, :].rearrange("p b t -> p (b t)")
            last = len(steps) - 1

            def scores(n):
                if n >= 2:
                    pe.eng.wait_ge(scalar_done, pe.at("scalar", (tag, "exp", n - 2)))
                for q, k, at in steps[n].scores:
                    ins = nc.tensor.matmul(area(n)[:, at:at + k.free_size()], q, k, start=True, stop=True)
                ins.then_inc(tensor_done, pe.mark((tag, "scores", n)))

            def turn(n):
                pe.eng.wait_ge(vector_done, pe.at("vector", (tag, "p", n)))
                for m, (at, keys, _) in enumerate(steps[n].values):
                    ins = nc.tensor.transpose(turned[0:keys, P * place(steps[n], m):P * place(steps[n], m) + P], p[:, n % 2, at:at + keys], ident)
                ins.then_inc(tensor_done, pe.mark((tag, "turn", n)))

            def values(n):
                b, parts, where = steps[n].out
                for m, (_, keys, v) in enumerate(steps[n].values):
                    ins = nc.tensor.matmul(bank(b)[parts, where], v, pT[0:keys, n % 2, P * place(steps[n], m):P * place(steps[n], m) + P],
                                           start=m == 0, stop=m == len(steps[n].values) - 1)
                ins.then_inc(tensor_done, pe.mark((tag, "values", n)))

            scores(0)
            scores(1)
            for n in range(last + 2):
                if n + 2 <= last:
                    scores(n + 2)
                if n >= 1:
                    pe.eng.wait_ge(vector_done, pe.at("vector", (tag, "turned", n - 1)))
                    pe.eng.wait_ge(scalar_done, pe.at("scalar", (tag, "turned", n - 1)))
                if n <= last:
                    turn(n)
                if n >= 1:
                    values(n - 1)

        def att_scalar(act, tag, steps, buf, mixed):
            p, pT, stats = buf
            last = len(steps) - 1

            def exps(n):
                act.eng.wait_ge(vector_done, act.at("vector", (tag, "max", n)))
                for m, (a, b) in enumerate(steps[n].parts):
                    nc.scalar.activation(p[:, n % 2, a:b], area(n)[:, a:b], ACT.Exp, bias=stats[:, n % 2, m:m + 1],
                                         accum_out=stats[:, n % 2, 4 + m:5 + m]).then_inc(
                        scalar_done, act.mark((tag, "exp", n) if m == len(steps[n].parts) - 1 else None))

            def copy_turned(n):
                act.eng.wait_ge(tensor_done, act.at("tensor", (tag, "turn", n)))
                if n >= 2:
                    act.eng.wait_ge(tensor_done, act.at("tensor", (tag, "values", n - 2)))
                other = turned_blocks(steps[n], 1)
                for i, (a, b, keys) in enumerate(other):
                    src = psum[0:keys, 4:6, :].rearrange("p b t -> p (b t)")[:, P * a:P * b]
                    nc.scalar.copy(pT[0:keys, n % 2, P * a:P * b], src).then_inc(
                        scalar_done, act.mark((tag, "turned", n) if i == len(other) - 1 else None))

            exps(0)
            exps(1)
            for n in range(last + 2):
                if n <= last:
                    copy_turned(n)
                if n + 2 <= last:
                    exps(n + 2)
                if n >= 1 and (n == last + 1 or steps[n].group != steps[n - 1].group):
                    group = steps[n - 1].group
                    act.eng.wait_ge(tensor_done, act.at("tensor", (tag, "values", n - 1)))
                    to = mixed(group)
                    nc.scalar.copy(to, bank(steps[n - 1].out[0]) if len(to.shape) == 2 else in_order(bank(steps[n - 1].out[0]))).then_inc(
                        scalar_done, act.mark((tag, "mixed", group)))

        def att_vector(dve, tag, steps, buf):
            p, pT, stats = buf
            last = len(steps) - 1

            def maxima(n):
                step = steps[n]
                dve.eng.wait_ge(tensor_done, dve.at("tensor", (tag, "scores", n)))
                for mask in step.masks:
                    mask(dve, area(n)).then_inc(vector_done, dve.mark())
                if step.masks:
                    dve.eng.wait_ge(vector_done, dve.now())
                for m, (a, b) in enumerate(step.parts):
                    nc.vector.tensor_reduce(stats[:, n % 2, m:m + 1], area(n)[:, a:b], AX, ALU.max, negate=True).then_inc(
                        vector_done, dve.mark((tag, "max", n) if m == len(step.parts) - 1 else None))

            def weigh(n):
                step = steps[n]
                k = len(step.parts)
                r = stats[:, n % 2, 8:8 + k]
                dve.eng.wait_ge(scalar_done, dve.at("scalar", (tag, "exp", n)))
                nc.vector.reciprocal(r, stats[:, n % 2, 4:4 + k]).then_inc(vector_done, dve.mark())
                dve.eng.wait_ge(vector_done, dve.now())
                if step.gates is not None:
                    nc.vector.tensor_tensor(r, r, step.gates(dve), ALU.mult).then_inc(vector_done, dve.mark())
                    dve.eng.wait_ge(vector_done, dve.now())
                if step.any_key is not None:
                    nc.vector.tensor_tensor(r[:, 0:1], r[:, 0:1], step.any_key, ALU.mult).then_inc(vector_done, dve.mark())
                    dve.eng.wait_ge(vector_done, dve.now())
                for m, (a, b) in enumerate(step.parts):
                    nc.vector.tensor_scalar(p[:, n % 2, a:b], p[:, n % 2, a:b], r[:, m:m + 1], None, ALU.mult).then_inc(
                        vector_done, dve.mark((tag, "p", n) if m == k - 1 else None))

            def copy_turned(n):
                dve.eng.wait_ge(tensor_done, dve.at("tensor", (tag, "turn", n)))
                if n >= 2:
                    dve.eng.wait_ge(tensor_done, dve.at("tensor", (tag, "values", n - 2)))
                mine = turned_blocks(steps[n], 0)
                for i, (a, b, keys) in enumerate(mine):
                    src = psum[0:keys, 4:6, :].rearrange("p b t -> p (b t)")[:, P * a:P * b]
                    nc.vector.tensor_copy(pT[0:keys, n % 2, P * a:P * b], src).then_inc(
                        vector_done, dve.mark((tag, "turned", n) if i == len(mine) - 1 else None))

            maxima(0)
            maxima(1)
            weigh(0)
            for n in range(last + 1):
                if n + 2 <= last:
                    maxima(n + 2)
                copy_turned(n)
                if n + 1 <= last:
                    weigh(n + 1)

        carve_reset()
        ns_mixed = carve(8, T)
        ns_mixed_tiles = [ns_mixed[:, k, :] for k in range(8)]
        ns_w1 = carve(2, SLOT)
        ns_gates = carve(4, 48)
        ns_q = carve(4, T)
        ns_ks, ns_kw = carve(T), carve(T)
        ns_c = carve(2, T)
        ns_v = carve(4, P)
        ns_h = carve(4, 32)
        ns_b1 = carve(4)
        ns_kc = carve(32)
        ns_vc = carve(64)
        att_buf = att_carve()

        def ns_steps():
            steps = []
            for h in range(4):
                half = slice(64 * (h % 2), 64 * (h % 2) + 64)
                for i in range(4):
                    q = ns_q[:, h, P * i:P * (i + 1)]
                    lo = max(0, i - 2)
                    wide, win, at_win = P * (i + 1), P * (i + 1 - lo), T + N_CMP
                    scores = [(q, ns_ks[:, 0:wide], T - wide), (q, ns_kc[:, 0:N_CMP], T), (q, ns_kw[:, P * i:P * (i + 1)], at_win)]
                    if i > 0:
                        scores.append((q, ns_kw[:, P * lo:P * i], at_win + P))
                    masked = P + N_CMP + P + (P if i >= 2 else 0)

                    def mask(dve, s, i=i, n=masked):
                        return nc.vector.tensor_tensor(s[:, T - P:T - P + n], s[:, T - P:T - P + n], tab("nsa_masks", NSA_MASK * i, n), ALU.add)

                    values = [(T - wide + P * j, P, ns_v[:, j, 0:64]) for j in range(i + 1)] + [(at_win, P, ns_v[:, i, 64:128])]
                    values += [(at_win + P + P * j, P, ns_v[:, lo + j, 64:128]) for j in range(i - lo)] + [(T, N_CMP, ns_vc[0:N_CMP, :])]
                    gates = lambda dve, i=i, h=h: ns_gates[:, i, ds(dve.it * 12 + 3 * h, 3)]
                    steps.append(Step(scores, [mask], [(T, T + N_CMP), (T - wide, T), (at_win, at_win + win)], values,
                                      (6 + h // 2, half, slice(P * i, P * (i + 1))), h // 2, gates, tab("cmp_any") if i == 0 else None))
            return steps

        def nsa_sync(sp):
            load(sp, arrays["nsa_gates"][0], 384)
            sp.eng.wait_ge(tensor_done, sp.at("tensor", ("nsa", "sum")))
            for a in range(2):
                sp.eng.dma_start(ns_w1[:, a, :], arrays["nsa_w1"][a]).then_inc(w1_loaded, 16)
            with sp.loop(4, "nsa") as it:
                sp.first = sp.chunk
                load(sp, arrays["nsa_a"][ds(it, 1)].rearrange("a p n -> (a p) n"), 4096, 2)
                load(sp, arrays["nsa_b"][ds(it, 1)].rearrange("a p n -> (a p) n"), 3072, 2)
            out_sync(sp, "nsa", "nsa_out", 8)

        def nsa_tensor(pe):
            norm_tensor(pe, "nsa", xn_tiles, KD)
            pe.eng.wait_ge(vector_done, pe.at("vector", ("nsa", "normed", KD - 1)))
            pe.eng.wait_ge(slot_loaded[pe.slot()], pe.chunk_loaded())
            w = ring[:, pe.slot(), :]
            for i in range(4):
                for k in range(KD):
                    nc.tensor.matmul(bank(1)[:, 48 * i:48 * i + 48], xn[:, k, P * i:P * (i + 1)], w[:, 48 * k:48 * k + 48],
                                     start=k == 0, stop=False)
                ins = nc.tensor.matmul(bank(1)[:, 48 * i:48 * i + 48], ones[0:1, :], col("nsa_bg")[0:1, :], start=False, stop=True)
            ins.then_inc(tensor_done, pe.used())
            pe.eng.wait_ge(w1_loaded, 16 * 2)
            for a in range(2):
                for m in range(2):
                    for l in range(16):
                        ins = nc.tensor.matmul(bank(2)[:, 2 * a + m:2 * a + m + 1], ns_w1[:, a, 256 * l + P * m:256 * l + P * m + P],
                                               col("nsa_pe", 16 * a + l, 1), start=l == 0, stop=l == 15)
            ins.then_inc(tensor_done, pe.mark("nsa pe"))
            pe.eng.wait_ge(vector_done, pe.at("vector", "nsa b1"))
            pe.eng.wait_ge(scalar_done, pe.at("scalar", "nsa gates"))
            steps = ns_steps()
            with pe.loop(4, "nsa"):
                pe.eng.wait_ge(scalar_done, pe.at("scalar", ("nsa", "mixed", 1), back=1))
                pe.eng.wait_ge(slot_loaded[pe.slot()], pe.chunk_loaded())
                w = ring[:, pe.slot(), :]
                for j in range(2):
                    product(bank(j), w, xn_tiles, KD, at=1024 * j).then_inc(tensor_done, pe.mark(("nsa q", j)))
                product(bank(2), w, xn_tiles, KD, at=2048).then_inc(tensor_done, pe.mark("nsa ks"))
                product(bank(3), w, xn_tiles, KD, at=3072).then_inc(tensor_done, pe.used())
                pe.eng.wait_ge(slot_loaded[pe.slot()], pe.chunk_loaded())
                w = ring[:, pe.slot(), :]
                product(bank(4), w, xn_tiles, KD).then_inc(tensor_done, pe.mark("nsa kc"))
                product(bank(5), w, xn_tiles, KD, at=1024).then_inc(tensor_done, pe.mark("nsa vc"))
                for i in range(4):
                    for k in range(KD):
                        ins = nc.tensor.matmul(bank(6)[:, P * i:P * (i + 1)], xn[:, k, P * i:P * (i + 1)],
                                               w[:, 2048 + P * k:2048 + P * (k + 1)], start=k == 0, stop=k == KD - 1)
                ins.then_inc(tensor_done, pe.used())
                pe.eng.wait_ge(vector_done, pe.at("vector", "nsa c"))
                for a in range(2):
                    for m in range(2):
                        for l in range(16):
                            ins = nc.tensor.matmul(bank(7)[:, 32 * (2 * a + m):32 * (2 * a + m) + N_CMP],
                                                   ns_w1[:, a, 256 * l + P * m:256 * l + P * m + P],
                                                   ns_c[:, a, 2 * l:2 * l + 16 * (N_CMP - 1) + 1:16], start=l == 0, stop=l == 15)
                ins.then_inc(tensor_done, pe.mark("nsa h"))
                pe.eng.wait_ge(scalar_done, pe.at("scalar", "nsa h"))
                for m in range(2):
                    ins = nc.tensor.matmul(bank(4)[:, 0:N_CMP], col("nsa_k_w2", P * m, P), ns_h[:, m, 0:N_CMP], start=m == 0, stop=m == 1)
                for m in range(2):
                    ins = nc.tensor.matmul(bank(5)[0:N_CMP, 0:64], ns_h[:, 2 + m, 0:N_CMP], col("nsa_v_w2", 64 * m, 64), start=m == 0, stop=m == 1)
                ins.then_inc(tensor_done, pe.mark("nsa kvc"))
                pe.eng.wait_ge(scalar_done, pe.at("scalar", "nsa kw"))
                pe.eng.wait_ge(vector_done, pe.at("vector", "nsa kvc"))
                att_tensor(pe, "nsa", steps, att_buf)
            pe.eng.wait_ge(scalar_done, pe.at("scalar", ("nsa", "mixed", 1)))
            out_tensor(pe, "nsa", ns_mixed_tiles, 8)

        def nsa_scalar(act, ready):
            def nsa_mixed(group):
                return ns_mixed[:, ds(act.it * 2 + group, 1), :].rearrange("p a t -> p (a t)")

            norm_scalar(act, "nsa", x_tiles, xn_tiles, KD, ready)
            act.eng.wait_ge(tensor_done, act.at("tensor", ("chunk", act.chunk)))
            nc.scalar.activation(ns_gates[:, :, :], bank(1)[:, 0:192].rearrange("p (i n) -> p i n", i=4), ACT.Sigmoid).then_inc(scalar_done, act.mark("nsa gates"))
            steps = ns_steps()
            with act.loop(4, "nsa"):
                for h in range(4):
                    half = slice(64 * (h % 2), 64 * (h % 2) + 64)
                    act.eng.wait_ge(tensor_done, act.at("tensor", ("nsa q", h // 2)))
                    nc.scalar.mul(ns_q[half, h, :], bank(h // 2)[half, :], 0.125).then_inc(scalar_done, act.mark())
                act.eng.wait_ge(tensor_done, act.at("tensor", "nsa ks"))
                nc.scalar.copy(ns_ks, bank(2)).then_inc(scalar_done, act.mark())
                act.eng.wait_ge(tensor_done, act.at("tensor", ("chunk", act.chunk + 1)))
                nc.scalar.copy(ns_kw, bank(3)).then_inc(scalar_done, act.mark("nsa kw"))
                act.eng.wait_ge(tensor_done, act.at("tensor", "nsa h"))
                for j in range(4):
                    nc.scalar.activation(ns_h[:, j, 0:N_CMP], bank(7)[:, 32 * j:32 * j + N_CMP], ACT.Gelu_apprx_tanh,
                                                  bias=ns_b1[:, j:j + 1]).then_inc(scalar_done, act.mark("nsa h" if j == 3 else None))
                att_scalar(act, "nsa", steps, att_buf, nsa_mixed)
            act.chunk += 5

        def nsa_vector(dve):
            norm_vector(dve, "nsa", x_tiles, xn_tiles, KD, model_norm(4))
            first = dve.chunk
            dve.eng.wait_ge(tensor_done, dve.at("tensor", "nsa pe"))
            nc.vector.tensor_tensor(ns_b1, bank(2)[:, 0:4], col("nsa_b1"), ALU.add).then_inc(vector_done, dve.mark("nsa b1"))
            for h in range(4):
                other = slice(64 - 64 * (h % 2), 128 - 64 * (h % 2))
                nc.vector.memset(ns_q[other, h, :], 0.0).then_inc(vector_done, dve.mark())
            nc.vector.memset(ns_c[64:128, :, T - 1:T], 0.0).then_inc(vector_done, dve.mark())
            steps = ns_steps()

            with dve.loop(4, "nsa"):
                for a, n in enumerate(("nsa kc", "nsa vc")):
                    dve.eng.wait_ge(tensor_done, dve.at("tensor", n))
                    nc.vector.tensor_copy(ns_c[0:64, a, :], bank(4 + a)[0:64, :]).then_inc(vector_done, dve.mark())
                    nc.vector.tensor_copy(ns_c[64:128, a, 0:T - 1], bank(4 + a)[64:128, 1:T]).then_inc(vector_done, dve.mark("nsa c" if a == 1 else None))
                dve.eng.wait_ge(tensor_done, dve.at("tensor", ("chunk", first + 2)))
                nc.vector.tensor_copy(ns_v[:, :, :], bank(6).rearrange("p (i n) -> p i n", i=4)).then_inc(vector_done, dve.mark())
                dve.eng.wait_ge(tensor_done, dve.at("tensor", "nsa kvc"))
                nc.vector.tensor_copy(ns_kc[:, 0:N_CMP], bank(4)[:, 0:N_CMP]).then_inc(vector_done, dve.mark())
                nc.vector.tensor_copy(ns_vc[0:N_CMP, :], bank(5)[0:N_CMP, 0:64]).then_inc(vector_done, dve.mark("nsa kvc"))
                att_vector(dve, "nsa", steps, att_buf)
            dve.chunk += 3
            out_vector(dve, "nsa")

        MIXERS["nsa"] = {"sync": nsa_sync, "tensor": nsa_tensor, "scalar": nsa_scalar, "vector": nsa_vector}

        carve_reset()
        m2_mixed = carve(6, T)
        m2_mixed_tiles = [m2_mixed[:, k, :] for k in range(6)]
        lat = carve(6, T)
        lat_n = carve(5, T)
        m2_t = carve(2, T)
        mla_q, mla_k = carve(2, T), carve(2, T)
        mla_v = carve(4, P)
        m2_buf = att_carve()
        carve_reset(6 * T)
        dil_q, dil_k = carve(2, 3, T), carve(3, T)
        dil_v = carve(4, 384)
        dil_buf = att_carve()
        MLA_SCALE = float(96) ** -0.5
        by_class = lambda ap: ap.rearrange("p (q c) -> p c q", c=4)
        in_order = lambda ap: ap.rearrange("p (c q) -> p c q", c=4)

        def mla_steps():
            steps = []
            for h in range(2):
                for i in range(4):
                    steps.append(Step([(mla_q[0:96, h, P * i:P * (i + 1)], mla_k[0:96, h, :], 0)], [], [(0, T)],
                                      [(P * j, P, mla_v[:, j, 64 * h:64 * h + 64]) for j in range(4)],
                                      (6, slice(64 * h, 64 * h + 64), slice(P * i, P * (i + 1))), 0))
            return steps

        def dil_steps():
            steps = []
            for s in range(2):
                for c in range(DIL_CLASSES):
                    own = slice(P * c, P * (c + 1))
                    scores = [(dil_q[:, s, 0, own], dil_k[:, 0, :], 0)]
                    scores += [(dil_q[:, s, g, own], dil_k[:, g, own], T + P * (g - 1)) for g in (1, 2)]

                    def bias(g, a, n, table, s=s):
                        def put(dve, area):
                            slope = tab("slopes")[:, ds(dve.it * 2 + (4 * g + s), 1)]
                            return nc.vector.scalar_tensor_tensor(area[:, a:a + n], table, slope, area[:, a:a + n], ALU.mult, ALU.add)
                        return put

                    masks = [bias(0, 0, T, tab("dist0", T * c, T)), bias(1, T, P, tab("dist1")), bias(2, T + P, P, tab("dist2"))]
                    values = [(P * j, P, dil_v[:, j, 64 * s:64 * s + 64]) for j in range(4)]
                    values += [(T + P * (g - 1), P, dil_v[:, c, P * g + 64 * s:P * g + 64 * s + 64]) for g in (1, 2)]
                    steps.append(Step(scores, masks, [(0, T + 2 * P)], values, (6, slice(64 * s, 64 * s + 64), own), 0))
            return steps

        def m2_sync(sp):
            load(sp, arrays["mla_z"][0], 3072)
            load(sp, arrays["mla_z"][1][:, 0:2816], 2816)
            with sp.loop(4, "mla") as it:
                sp.first = sp.chunk
                load(sp, arrays["mla_q"][ds(it, 1)].rearrange("a p n -> (a p) n"), 576, 2)
                load(sp, arrays["mla_kv"][ds(it, 1)].rearrange("a p n -> (a p) n"), 512, 2)
            with sp.loop(2, "dil") as it:
                sp.first = sp.chunk
                for j in range(2):
                    load(sp, arrays["dil_qk"][ds(it * 2 + j, 1)].rearrange("a p n -> (a p) n"), 3072, 4)
                load(sp, arrays["dil_va"][ds(it, 1)].rearrange("a p n -> (a p) n"), 2048, 4)
                load(sp, arrays["dil_vb"][ds(it, 1)].rearrange("a p n -> (a p) n"), 1024, 4)
            out_sync(sp, "m2", "ab2_out", 6)

        lat_q = [lat[:, k, :] for k in range(3)]
        lat_kv = [lat[:, 3 + k, :] for k in range(2)]
        lat_qn = [lat_n[:, k, :] for k in range(3)]
        lat_kvn = [lat_n[:, 3 + k, :] for k in range(2)]

        def m2_tensor(pe):
            norm_tensor(pe, "m2", xn_tiles, KD)
            pe.eng.wait_ge(vector_done, pe.at("vector", ("m2", "normed", KD - 1)))
            pe.eng.wait_ge(slot_loaded[pe.slot()], pe.chunk_loaded())
            w = ring[:, pe.slot(), :]
            for j in range(3):
                ins = product(bank(j), w, xn_tiles, KD, at=1024 * j)
                if j < 2:
                    ins.then_inc(tensor_done, pe.mark(("m2 z", j)))
            ins.then_inc(tensor_done, pe.used())
            pe.eng.wait_ge(slot_loaded[pe.slot()], pe.chunk_loaded())
            w = ring[:, pe.slot(), :]
            for j in range(2):
                product(bank(3 + j), w, xn_tiles, KD, at=1024 * j).then_inc(tensor_done, pe.mark(("m2 z", 3 + j)))
            product(bank(5)[0:96, :], w, xn_tiles, KD, width=96, at=2048).then_inc(tensor_done, pe.used())
            norm_tensor(pe, "mla gq", lat_qn, 3, b=6)
            norm_tensor(pe, "mla gkv", lat_kvn, 2, b=7)
            pe.eng.wait_ge(vector_done, pe.at("vector", "m2 z"))
            nc.tensor.matmul(bank(0)[0:96, :], tab("mla_rot")[0:96, :], lat[0:96, 5, :], start=True, stop=True).then_inc(tensor_done, pe.mark("mla rot k"))
            pe.eng.wait_ge(vector_done, pe.at("vector", "mla k rope"))
            pe.eng.wait_ge(vector_done, pe.at("vector", ("mla gkv", "normed", 1)))
            steps = mla_steps()
            with pe.loop(4, "mla"):
                pe.eng.wait_ge(scalar_done, pe.at("scalar", ("mla", "mixed", 0), back=1))
                pe.eng.wait_ge(slot_loaded[pe.slot()], pe.chunk_loaded())
                w = ring[:, pe.slot(), :]
                product(bank(0)[0:96, :], w, lat_qn, 3, width=96).then_inc(tensor_done, pe.mark(("mla q", 0)))
                product(bank(1)[0:96, :], w, lat_qn, 3, width=96, at=288).then_inc(tensor_done, pe.used())
                pe.eng.wait_ge(slot_loaded[pe.slot()], pe.chunk_loaded())
                w = ring[:, pe.slot(), :]
                for h in range(2):
                    product(bank(2 + h)[0:64, :], w, lat_kvn, 2, width=64, at=128 * h).then_inc(tensor_done, pe.mark(("mla k", h)))
                for i in range(4):
                    for k in range(2):
                        ins = nc.tensor.matmul(bank(4)[:, P * i:P * (i + 1)], lat_kvn[k][:, P * i:P * (i + 1)],
                                               w[:, 256 + P * k:256 + P * (k + 1)], start=k == 0, stop=k == 1)
                ins.then_inc(tensor_done, pe.used())
                for h in range(2):
                    pe.eng.wait_ge(scalar_done, pe.at("scalar", ("mla raw", h)))
                    nc.tensor.matmul(bank(5 + h)[0:96, :], tab("mla_rot")[0:96, :], m2_t[0:96, h, :], start=True, stop=True).then_inc(tensor_done, pe.mark(("mla rot", h)))
                pe.eng.wait_ge(scalar_done, pe.at("scalar", ("mla k", 1)))
                pe.eng.wait_ge(vector_done, pe.at("vector", ("mla q", 1)))
                att_tensor(pe, "mla", steps, m2_buf)
            pe.eng.wait_ge(scalar_done, pe.at("scalar", ("mla", "mixed", 0)))
            steps = dil_steps()
            with pe.loop(2, "dil"):
                pe.eng.wait_ge(scalar_done, pe.at("scalar", ("dil", "mixed", 0), back=1))
                for n in range(2):
                    pe.eng.wait_ge(slot_loaded[pe.slot()], pe.chunk_loaded())
                    w = ring[:, pe.slot(), :]
                    for j in range(3):
                        ins = product(bank(3 * n + j), w, xn_tiles, KD, at=1024 * j)
                        if j < 2:
                            ins.then_inc(tensor_done, pe.mark(("dil qk", 3 * n + j)))
                    ins.then_inc(tensor_done, pe.used())
                pe.eng.wait_ge(slot_loaded[pe.slot()], pe.chunk_loaded())
                w = ring[:, pe.slot(), :]
                for c in range(4):
                    for k in range(KD):
                        ins = nc.tensor.matmul(bank(6 + c // 2)[:, 256 * (c % 2):256 * (c % 2) + 256], by_class(xn[:, k, :])[:, c, :],
                                               w[:, 256 * k:256 * (k + 1)], start=k == 0, stop=k == KD - 1)
                ins.then_inc(tensor_done, pe.used())
                pe.eng.wait_ge(slot_loaded[pe.slot()], pe.chunk_loaded())
                w = ring[:, pe.slot(), :]
                pe.eng.wait_ge(scalar_done, pe.at("scalar", "dil q"))
                for c in range(4):
                    for k in range(KD):
                        ins = nc.tensor.matmul(bank(0)[:, P * c:P * (c + 1)], by_class(xn[:, k, :])[:, c, :],
                                               w[:, P * k:P * (k + 1)], start=k == 0, stop=k == KD - 1)
                ins.then_inc(tensor_done, pe.used())
                pe.eng.wait_ge(vector_done, pe.at("vector", "dil v"))
                pe.eng.wait_ge(scalar_done, pe.at("scalar", "dil q"))
                att_tensor(pe, "dil", steps, dil_buf)
            pe.eng.wait_ge(scalar_done, pe.at("scalar", ("dil", "mixed", 0)))
            out_tensor(pe, "m2", m2_mixed_tiles, 6)

        def m2_scalar(act, ready):
            def mla_mixed(group):
                return m2_mixed[:, ds(act.it, 1), :].rearrange("p a t -> p (a t)")

            def dil_mixed(group):
                return m2_mixed[:, ds(act.it + 4, 1), :].rearrange("p a (q c) -> p (a c) q", c=4)

            norm_scalar(act, "m2", x_tiles, xn_tiles, KD, ready)
            latents = (vector_done, act.at("vector", "m2 z"))
            norm_scalar(act, "mla gq", lat_q, lat_qn, 3, latents)
            norm_scalar(act, "mla gkv", lat_kv, lat_kvn, 2, latents)
            steps = mla_steps()
            with act.loop(4, "mla"):
                act.eng.wait_ge(tensor_done, act.at("tensor", ("mla q", 0)))
                nc.scalar.copy(m2_t[0:96, 0, :], bank(0)[0:96, :]).then_inc(scalar_done, act.mark(("mla raw", 0)))
                act.eng.wait_ge(tensor_done, act.at("tensor", ("chunk", act.chunk + 2)))
                nc.scalar.copy(m2_t[0:96, 1, :], bank(1)[0:96, :]).then_inc(scalar_done, act.mark(("mla raw", 1)))
                for h in range(2):
                    act.eng.wait_ge(tensor_done, act.at("tensor", ("mla k", h)))
                    nc.scalar.copy(mla_k[0:64, h, :], bank(2 + h)[0:64, :]).then_inc(scalar_done, act.mark(("mla k", h)))
                att_scalar(act, "mla", steps, m2_buf, mla_mixed)
            steps = dil_steps()
            with act.loop(2, "dil"):
                for j in range(3):
                    act.eng.wait_ge(tensor_done, act.at("tensor", ("dil qk", j) if j < 2 else ("chunk", act.chunk + 4)))
                    for s in range(2):
                        half = slice(64 * s, 64 * s + 64)
                        nc.scalar.mul(in_order(dil_q[half, s, j, :]), by_class(bank(j)[half, :]), 0.125).then_inc(
                            scalar_done, act.mark("dil q" if j == 2 and s == 1 else None))
                att_scalar(act, "dil", steps, dil_buf, dil_mixed)
            act.chunk += 10

        def m2_vector(dve):
            norm_vector(dve, "m2", x_tiles, xn_tiles, KD, model_norm(7))
            first = dve.chunk
            for j in range(6):
                dve.eng.wait_ge(tensor_done, dve.at("tensor", ("chunk", first) if j == 2 else ("chunk", first + 1) if j == 5 else ("m2 z", j)))
                n = 96 if j == 5 else P
                nc.vector.tensor_copy(lat[0:n, j, :], bank(j)[0:n, :]).then_inc(vector_done, dve.mark("m2 z" if j == 5 else None))
            norm_vector(dve, "mla gq", lat_q, lat_qn, 3, lambda k: col("mla_gq", k, 1), b=6)
            norm_vector(dve, "mla gkv", lat_kv, lat_kvn, 2, lambda k: col("mla_gkv", k, 1), b=7)
            dve.eng.wait_ge(tensor_done, dve.at("tensor", "mla rot k"))
            at = slice(64, 96)
            nc.vector.tensor_tensor(m2_t[at, 0, :], lat[at, 5, :], tab("mla_cos")[at, :], ALU.mult).then_inc(vector_done, dve.mark())
            nc.vector.tensor_tensor(m2_t[at, 1, :], tab("mla_sin")[at, :], bank(0)[at, :], ALU.mult).then_inc(vector_done, dve.mark())
            dve.eng.wait_ge(vector_done, dve.now())
            for h in range(2):
                nc.vector.tensor_tensor(mla_k[at, h, :], m2_t[at, 0, :], m2_t[at, 1, :], ALU.add).then_inc(vector_done, dve.mark("mla k rope" if h else None))
            steps = mla_steps()
            with dve.loop(4, "mla"):
                for h in range(2):
                    dve.eng.wait_ge(tensor_done, dve.at("tensor", ("mla rot", h)))
                    nc.vector.scalar_tensor_tensor(mla_q[0:96, h, :], m2_t[0:96, h, :], MLA_SCALE, tab("mla_cos")[0:96, :], ALU.mult, ALU.mult).then_inc(vector_done, dve.mark())
                    dve.eng.wait_ge(vector_done, dve.now())
                    nc.vector.scalar_tensor_tensor(m2_t[0:96, h, :], bank(5 + h)[0:96, :], MLA_SCALE, tab("mla_sin")[0:96, :], ALU.mult, ALU.mult).then_inc(vector_done, dve.mark())
                    dve.eng.wait_ge(vector_done, dve.now())
                    nc.vector.tensor_tensor(mla_q[0:96, h, :], mla_q[0:96, h, :], m2_t[0:96, h, :], ALU.add).then_inc(vector_done, dve.mark())
                dve.eng.wait_ge(tensor_done, dve.at("tensor", ("chunk", first + 3)))
                nc.vector.tensor_copy(mla_v[:, :, :], bank(4).rearrange("p (i n) -> p i n", i=4)).then_inc(vector_done, dve.mark(("mla q", 1)))

                att_vector(dve, "mla", steps, m2_buf)
            steps = dil_steps()
            for s in range(2):
                nc.vector.memset(dil_q[64 - 64 * s:128 - 64 * s, s, :, :], 0.0).then_inc(vector_done, dve.mark())
            with dve.loop(2, "dil"):
                for j in range(3):
                    dve.eng.wait_ge(tensor_done, dve.at("tensor", ("dil qk", 3 + j) if j < 2 else ("chunk", first + 5)))
                    nc.vector.tensor_copy(in_order(dil_k[:, j, :]), by_class(bank(3 + j))).then_inc(vector_done, dve.mark())
                dve.eng.wait_ge(tensor_done, dve.at("tensor", ("chunk", first + 6)))
                for b in range(2):
                    nc.vector.tensor_copy(dil_v[:, 2 * b:2 * b + 2, 0:256], bank(6 + b).rearrange("p (c n) -> p c n", c=2)).then_inc(vector_done, dve.mark())
                dve.eng.wait_ge(tensor_done, dve.at("tensor", ("chunk", first + 7)))
                nc.vector.tensor_copy(dil_v[:, :, 256:384], bank(0).rearrange("p (c n) -> p c n", c=4)).then_inc(vector_done, dve.mark("dil v"))

                att_vector(dve, "dil", steps, dil_buf)
            dve.chunk += 8
            out_vector(dve, "m2")

        MIXERS["m2"] = {"sync": m2_sync, "tensor": m2_tensor, "scalar": m2_scalar, "vector": m2_vector}

        carve_reset()
        gq_mixed = carve(8, T)
        gq_mixed_tiles = [gq_mixed[:, k, :] for k in range(8)]
        gq_raw, gq_sq, gq_n = carve(3, T), carve(3, T), carve(3, T)
        gq_q = carve(4, T)
        gq_k = carve(T)
        gq_v = carve(4, 64)
        gq_buf = att_carve()

        def gqa_steps():
            steps = []
            for h in range(4):
                half = slice(64 * (h % 2), 64 * (h % 2) + 64)
                for i in range(4):
                    steps.append(Step([(gq_q[:, h, P * i:P * (i + 1)], gq_k, 0)], [], [(0, T)],
                                      [(P * j, P, gq_v[:, j, :]) for j in range(4)],
                                      (6 + h // 2, half, slice(P * i, P * (i + 1))), h // 2))
            return steps

        def gqa_sync(sp):
            with sp.loop(4, "gqa") as it:
                sp.first = sp.chunk
                load(sp, arrays["gqa_qk"][ds(it, 1)].rearrange("a p n -> (a p) n"), 3072, 2)
                load(sp, arrays["gqa_v"][ds(it, 1)].rearrange("a p n -> (a p) n"), 512, 2)
            out_sync(sp, "gqa", "gqa_out", 8)

        def gqa_tensor(pe):
            norm_tensor(pe, "gqa", xn_tiles, KD)
            pe.eng.wait_ge(vector_done, pe.at("vector", ("gqa", "normed", KD - 1)))
            steps = gqa_steps()
            with pe.loop(4, "gqa"):
                pe.eng.wait_ge(scalar_done, pe.at("scalar", ("gqa", "mixed", 1), back=1))
                pe.eng.wait_ge(slot_loaded[pe.slot()], pe.chunk_loaded())
                w = ring[:, pe.slot(), :]
                for j in range(2):
                    product(bank(j), w, xn_tiles, KD, at=1024 * j).then_inc(tensor_done, pe.mark(("gqa raw", j)))
                product(bank(2), w, xn_tiles, KD, at=2048).then_inc(tensor_done, pe.used())
                pe.eng.wait_ge(slot_loaded[pe.slot()], pe.chunk_loaded())
                w = ring[:, pe.slot(), :]
                for i in range(4):
                    for k in range(KD):
                        ins = nc.tensor.matmul(bank(3)[:, 64 * i:64 * (i + 1)], xn[:, k, P * i:P * (i + 1)],
                                               w[:, 64 * k:64 * (k + 1)], start=k == 0, stop=k == KD - 1)
                ins.then_inc(tensor_done, pe.used())
                for j in range(3):
                    pe.eng.wait_ge(scalar_done, pe.at("scalar", ("gqa square", j)))
                    nc.tensor.matmul(bank(4 + j), tab("ones64"), gq_sq[:, j, :], start=True, stop=True).then_inc(tensor_done, pe.mark(("gqa sum", j)))
                for j in range(3):
                    pe.eng.wait_ge(vector_done, pe.at("vector", ("gqa normed", j)))
                    nc.tensor.matmul(bank(j), tab("gqa_rot"), gq_n[:, j, :], start=True, stop=True).then_inc(tensor_done, pe.mark(("gqa rot", j)))
                pe.eng.wait_ge(vector_done, pe.at("vector", "gqa qk"))
                att_tensor(pe, "gqa", steps, gq_buf)
            pe.eng.wait_ge(scalar_done, pe.at("scalar", ("gqa", "mixed", 1)))
            out_tensor(pe, "gqa", gq_mixed_tiles, 8)

        def gqa_scalar(act, ready):
            def gqa_mixed(group):
                return gq_mixed[:, ds(act.it * 2 + group, 1), :].rearrange("p a t -> p (a t)")

            norm_scalar(act, "gqa", x_tiles, xn_tiles, KD, ready)
            steps = gqa_steps()
            with act.loop(4, "gqa"):
                for j in range(3):
                    act.eng.wait_ge(tensor_done, act.at("tensor", ("gqa raw", j) if j < 2 else ("chunk", act.chunk)))
                    nc.scalar.copy(gq_raw[:, j, :], bank(j)).then_inc(scalar_done, act.mark())
                    nc.scalar.activation(gq_sq[:, j, :], bank(j), ACT.Square).then_inc(scalar_done, act.mark(("gqa square", j)))
                act.eng.wait_ge(vector_done, act.at("vector", "gqa mean"))
                nc.scalar.activation(gq_sq[:, :, :], gq_sq[:, :, :], ACT.Sqrt).then_inc(scalar_done, act.mark("gqa rstd"))
                att_scalar(act, "gqa", steps, gq_buf, gqa_mixed)
            act.chunk += 4

        def gqa_vector(dve):
            norm_vector(dve, "gqa", x_tiles, xn_tiles, KD, model_norm(9))
            for h in range(4):
                other = slice(64 - 64 * (h % 2), 128 - 64 * (h % 2))
                nc.vector.memset(gq_q[other, h, :], 0.0).then_inc(vector_done, dve.mark())
            first = dve.chunk
            steps = gqa_steps()
            with dve.loop(4, "gqa"):
                for j in range(3):
                    dve.eng.wait_ge(tensor_done, dve.at("tensor", ("gqa sum", j)))
                    nc.vector.tensor_scalar(gq_sq[:, j, :], bank(4 + j), 1.0 / 64, EPS, ALU.mult, ALU.add).then_inc(vector_done, dve.mark())
                    dve.eng.wait_ge(vector_done, dve.now())
                nc.vector.reciprocal(gq_sq[:, :, :], gq_sq[:, :, :]).then_inc(vector_done, dve.mark("gqa mean"))
                dve.eng.wait_ge(vector_done, dve.now())
                dve.eng.wait_ge(tensor_done, dve.at("tensor", ("chunk", first + 1)))
                nc.vector.tensor_copy(gq_v[:, :, :], bank(3)[:, 0:256].rearrange("p (i n) -> p i n", i=4)).then_inc(vector_done, dve.mark())
                dve.eng.wait_ge(scalar_done, dve.at("scalar", "gqa rstd"))
                for j in range(3):
                    gain = col("gqa_gk") if j == 2 else col("gqa_gq")
                    nc.vector.scalar_tensor_tensor(gq_n[:, j, :], gq_raw[:, j, :], gain, gq_sq[:, j, :], ALU.mult, ALU.mult).then_inc(vector_done, dve.mark(("gqa normed", j)))
                for j in range(3):
                    scale = 1.0 if j == 2 else 0.125
                    dve.eng.wait_ge(tensor_done, dve.at("tensor", ("gqa rot", j)))
                    nc.vector.scalar_tensor_tensor(gq_raw[:, j, :], gq_n[:, j, :], scale, tab("gqa_cos"), ALU.mult, ALU.mult).then_inc(vector_done, dve.mark())
                    nc.vector.scalar_tensor_tensor(gq_sq[:, j, :], bank(j), scale, tab("gqa_sin"), ALU.mult, ALU.mult).then_inc(vector_done, dve.mark())
                    dve.eng.wait_ge(vector_done, dve.now())
                    if j == 2:
                        nc.vector.tensor_tensor(gq_k, gq_raw[:, j, :], gq_sq[:, j, :], ALU.add).then_inc(vector_done, dve.mark("gqa qk"))
                    else:
                        for half, h in ((slice(0, 64), 2 * j), (slice(64, 128), 2 * j + 1)):
                            nc.vector.tensor_tensor(gq_q[half, h, :], gq_raw[half, j, :], gq_sq[half, j, :], ALU.add).then_inc(vector_done, dve.mark())

                att_vector(dve, "gqa", steps, gq_buf)
            dve.chunk += 2
            out_vector(dve, "gqa")

        MIXERS["gqa"] = {"sync": gqa_sync, "tensor": gqa_tensor, "scalar": gqa_scalar, "vector": gqa_vector}

        todo = stages or ["f0", "ab", "f1", "f2", "nsa", "f3", "n1", "m2", "f4", "gqa", "f5", "n2"]
        FFN = {"f0": (0, 0, 0.5), "f1": (1, 2, 0.5), "f2": (2, 3, 0.5), "f3": (3, 5, 0.5), "f4": (4, 8, 1.0), "f5": (5, 10, 1.0)}

        def ready_for(e, i):
            if i == 0:
                return vector_done, e.at("vector", "x")
            s = todo[i - 1]
            if s in FFN:
                return x_updated, KD * (FFN[s][0] + 1) + 2
            return vector_done, e.at("vector", (s, "copied") if s == "n1" else (s, "x", 1))

        def mixer_sync(sp, s, i):
            if i:
                sp.eng.wait_ge(*ready_for(sp, i))
            if s in tables_at:
                sp.eng.dma_start(tabbuf[s][:, 0:tables_at[s][1]], arrays["t_" + s]).then_inc(tables_loaded, 16)
            sp.base = sp.chunk
            MIXERS[s]["sync"](sp)

        def wait_tables(e, s):
            mixers = [m for m in todo if m in MIXERS]
            e.eng.wait_ge(tables_loaded, 16 * (mixers.index(s) + 1))

        if todo[-1] != "n2":
            todo = todo + ["end"]

        n_chunks = []
        block = ctx.enter_context(nc.Block())

        @block.sync
        def _(eng):
            sp = Engine(eng, None, counts, [counts["slot0"], counts["slot1"]])
            start_sync(sp)
            for i, s in enumerate(todo):
                if s in FFN:
                    ffn_sync(sp, s, FFN[s][0], i > 0 and todo[i - 1] in MIXERS)
                elif s in MIXERS:
                    mixer_sync(sp, s, i)
            end_sync(sp)
            n_chunks.append(sp.chunk)

        @block.tensor
        def _(eng):
            pe = Engine(eng, counts["tensor"], counts)
            eng.sem_inc(tensor_done, LEAD)
            eng.sem_inc(unit_used, 2)
            start_tensor(pe)
            for i, s in enumerate(todo):
                if s in FFN:
                    ffn_tensor(pe, s, FFN[s][0])
                elif s in MIXERS:
                    wait_tables(pe, s)
                    MIXERS[s]["tensor"](pe)
                elif s in ("n1", "n2"):
                    norm_tensor(pe, s, xn_tiles, KD)
            end_tensor(pe, ("n2", "normed", KD - 1) if todo[-1] == "n2" else "end")
            n_chunks.append(pe.chunk)

        @block.scalar
        def _(eng):
            act = Engine(eng, counts["scalar"], counts)
            eng.sem_inc(scalar_done, LEAD)
            for i, s in enumerate(todo):
                if s in FFN:
                    ffn_scalar(act, s, FFN[s][0], ready_for(act, i))
                elif s in MIXERS:
                    MIXERS[s]["scalar"](act, ready_for(act, i))
                elif s in ("n1", "n2"):
                    norm_scalar(act, s, x_tiles, xn_tiles, KD, ready_for(act, i))
            n_chunks.append(act.chunk)

        @block.vector
        def _(eng):
            dve = Engine(eng, counts["vector"], counts)
            eng.sem_inc(vector_done, LEAD)
            eng.sem_inc(unit_ready, 4)
            eng.sem_inc(hidden_ready, 2)
            eng.sem_inc(x_updated, 2)
            start_vector(dve)
            for i, s in enumerate(todo):
                if s in FFN:
                    ffn_vector(dve, s, *FFN[s])
                elif s in MIXERS:
                    wait_tables(dve, s)
                    MIXERS[s]["vector"](dve)
                elif s in ("n1", "n2"):
                    norm_vector(dve, s, x_tiles, xn_tiles, KD, model_norm(6 if s == "n1" else 11))
                    if s == "n1":
                        dve.eng.wait_ge(vector_done, dve.now())
                        nc.vector.tensor_copy(x[:, :, :], xn[:, :, :]).then_inc(vector_done, dve.mark((s, "copied")))
                elif s == "end":
                    dve.eng.wait_ge(vector_done, dve.now())
                    dve.eng.wait_ge(*ready_for(dve, i))
                    nc.vector.tensor_copy(xn[:, :, :], x[:, :, :]).then_inc(vector_done, dve.mark("end"))
            end_vector(dve)
            n_chunks.append(dve.chunk)

    assert len(set(n_chunks)) == 1, n_chunks
    return seen


def program(Bacc, shapes, columns_at, tables_at, stages=None):
    marks = {}
    while True:
        nc = Bacc("TRN2", target_bir_lowering=False, num_devices=1)
        arrays = {n: nc.dram_tensor(f"in_{n}", s, F32, kind="ExternalInput").ap() for n, s in shapes.items()}
        out = nc.dram_tensor("out_0", (T, D), F32, kind="ExternalOutput").ap()
        seen = build(nc, arrays, columns_at, tables_at, out, marks, stages)
        if seen == marks:
            return nc
        marks = seen


def prepare(inputs):
    tables = make_tables()
    weights, columns = lay_out(inputs)
    columns_at, _ = offsets(columns)
    tables_at = {stage: offsets(t) for stage, t in tables.items()}
    sent = {"x": inputs["x"][0], "columns": np.concatenate(list(columns.values()), 1)}
    sent.update(weights)
    sent.update({"t_" + stage: np.concatenate(list(t.values()), 1) for stage, t in tables.items()})
    return {n: np.ascontiguousarray(a) for n, a in sent.items()}, columns_at, tables_at


def kernel(**inputs):
    import concourse.bacc as _bacc
    from concourse.bass_utils import run_bass_kernel_spmd as _run

    inputs = {n: np.asarray(a) for n, a in inputs.items()}
    sent, columns_at, tables_at = prepare(inputs)
    nc = program(_bacc.Bacc, {n: a.shape for n, a in sent.items()}, columns_at, tables_at)
    r = _run(nc, [{f"in_{n}": a for n, a in sent.items()}], core_ids=[0])
    return r.results[0]["out_0"].reshape(1, T, D)
```

```python
from contextlib import ExitStack, contextmanager

import numpy as np

import concourse.bass as bass
from concourse import mybir

F32 = mybir.dt.float32
F32R = mybir.dt.float32r
ARENA = 26800
ACT = mybir.ActivationFunctionType
ALU = mybir.AluOpType
AX = mybir.AxisListType.X
ds = bass.ds

P = 128
T = 512
D = 1024
KD = D // P
D_FF = 2816
KF = D_FF // P
EPS = 1e-6
LEAD = 2048
SLOT = 4096
NSLOT = 2
UNIT = KF // 2 * P
NEG = -1e30
BIG = 1e30

DIL_SLOTS, DIL_GROUPS, DIL_CLASSES = 4, 3, 4
N_CMP = (T - 32) // 16 + 1
NSA_MASK = 3 * P + N_CMP


TABLES = {
    "all": ["ident", "ones"],
    "ab": ["future", "sel4"],
    "nsa": ["nsa_masks", "cmp_any"],
    "m2": ["dist0", "dist1", "dist2", "slopes", "mla_cos", "mla_sin", "mla_rot"],
    "gqa": ["gqa_cos", "gqa_sin", "gqa_rot", "ones64"],
}


def rope_tables(pos, dim):
    freqs = (np.float32(10000.0) ** (-np.arange(0, dim, 2, dtype=np.float32) / np.float32(dim))).astype(np.float32)
    ang = pos.astype(np.float32)[:, None] * freqs[None, :]
    return np.cos(ang).astype(np.float32).T, np.sin(ang).astype(np.float32).T


def rotation(width, starts, half):
    m = np.zeros((P, width), np.float32)
    for s in starts:
        for i in range(half):
            m[s + half + i, s + i] = -1.0
            m[s + i, s + half + i] = 1.0
    return m


def make_tables():
    q = np.arange(P)[:, None]
    k = np.arange(P)[None, :]
    pos = np.arange(T)
    t = {}
    t["ident"] = np.eye(P)
    t["ones"] = np.ones((P, P))
    t["ones64"] = (q // 64 == k // 64) * 1.0
    t["future"] = np.tile(np.where(q <= k, 0.0, BIG), (1, 4))
    causal, older = np.where(k <= q, 0.0, NEG), np.where(k > q, 0.0, NEG)
    masks = []
    for i in range(T // P):
        ok = (np.arange(N_CMP) * 16 + 31)[None, :] <= P * i + q
        masks += [causal, np.where(ok, 0.0, NEG), causal, older]
    t["nsa_masks"] = np.concatenate(masks, 1)
    t["cmp_any"] = (q >= 31) * 1.0
    near = []
    for c in range(DIL_CLASSES):
        u = (4 * k + np.arange(4)[:, None, None])
        dist = np.abs(4 * q[None] + c - u)
        near.append(np.where(dist <= 64, dist, 1e33).transpose(1, 0, 2).reshape(P, T))
    t["dist0"] = np.concatenate(near, 1)
    t["dist1"] = np.where(np.abs(q - k) <= 64, 4 * np.abs(q - k), 1e33)
    t["dist2"] = np.where((q - k) % 4 == 0, 4 * np.abs(q - k), 1e33)
    n = np.arange(1, DIL_SLOTS * DIL_GROUPS + 1, dtype=np.float32)
    t["slopes"] = np.tile(-np.exp2(np.float32(-8.0) * n / np.float32(12.0)), (P, 1))
    c, s = rope_tables(pos, 32)
    full = np.zeros((2, P, T), np.float32)
    full[0, :64] = 1.0
    full[0, 64:96], full[1, 64:96] = np.tile(c, (2, 1)), np.tile(s, (2, 1))
    t["mla_cos"], t["mla_sin"] = full
    cr, sr = rope_tables(pos // 64, 32)
    cc, sc = rope_tables(pos % 64, 32)
    t["gqa_cos"] = np.concatenate([cr, cr, cc, cc] * 2, 0)
    t["gqa_sin"] = np.concatenate([sr, sr, sc, sc] * 2, 0)
    t["mla_rot"] = rotation(96, [64], 16)
    t["gqa_rot"] = rotation(P, [0, 32, 64, 96], 16)
    t["sel4"] = np.concatenate([np.eye(4), np.zeros((P - 4, 4))], 0)
    t = {name: np.ascontiguousarray(a, np.float32) for name, a in t.items()}
    return {stage: {n: t[n] for n in names} for stage, names in TABLES.items()}


def offsets(parts):
    at, out = 0, {}
    for name, a in parts.items():
        out[name] = (at, a.shape[1])
        at += a.shape[1]
    return out, at


def m_tiles(w, width=P):
    k, m = w.shape
    return w.reshape(k // P, P, m // width, width).transpose(2, 1, 0, 3).reshape(m // width, P, -1)


def cols(w, at, width):
    return m_tiles(w[:, at:at + width], width)[0]


def twice(w, at, width):
    return m_tiles(np.concatenate([w[:, at:at + width]] * 2, 1))[0]


def column(v):
    return v.reshape(-1, P).T


def padded(v):
    v = v.reshape(v.shape[0], -1)
    out = np.zeros((P, v.shape[1]), v.dtype)
    out[:v.shape[0]] = v
    return out


def lay_out(i):
    w = {}
    gu, down = [], []
    for a, b in [(i["ffn1_w_gu"][0], i["ffn1_w_down"][0]), (i["ffn2_w_gu"][0], i["ffn2_w_down"][0]),
                 (i["ffn1_w_gu"][1], i["ffn1_w_down"][1]), (i["ffn2_w_gu"][1], i["ffn2_w_down"][1]),
                 (i["ffn_w_in_2"][0], i["ffn_w_out_2"][0]), (i["ffn_w_in_2"][1], i["ffn_w_out_2"][1])]:
        gu.append(np.concatenate([m_tiles(a[:, :D_FF]), m_tiles(a[:, D_FF:])], 2))
        down.append(m_tiles(b))
    w["gate_up"], w["down"] = np.concatenate(gu), np.concatenate(down)

    ab = i["ab_w_in"][0]
    gates = np.zeros((1024, 36), ab.dtype)
    gates[:, 0:4], gates[:, 32:36] = ab[:, 3072:3076], ab[:, 3076:3080]
    w["ab_gates"] = cols(gates, 0, 36)[None]
    rg, ml = [], []
    for t in range(4):
        pair = []
        for name in ("rg_w_r", "rg_w_i"):
            z = np.zeros((P, P), ab.dtype)
            z[:64, :64], z[64:, 64:] = i[name][0, 2 * t], i[name][0, 2 * t + 1]
            pair.append(z)
        rg.append(padded_free(cols(ab, P * t, P), 1280))
        rg.append(np.concatenate([cols(ab, 512 + P * t, P), *pair], 1))
        ml.append(np.concatenate([cols(ab, 1024 + P * t, P), cols(ab, 1536 + P * t, P)], 1))
        ml.append(np.concatenate([cols(ab, 2048 + P * t, P), cols(ab, 2560 + P * t, P)], 1))
    w["rg"], w["ml"] = np.stack(rg), np.stack(ml)
    w["ab_out"] = m_tiles(i["ab_w_out"][0])

    ns = i["nsa_w_in"][0]
    w["nsa_gates"] = cols(ns, 2560, 48)[None]
    w["nsa_w1"] = np.stack([i[n][0].reshape(16, P, 256).transpose(1, 0, 2).reshape(P, -1) for n in ("nsa_k_w1", "nsa_v_w1")])
    tile = lambda j, t: cols(ns, 1024 + 256 * j + P * t, P)
    w["nsa_c"] = np.concatenate([tile(0, 0), tile(1, 0), tile(0, 1), tile(1, 1)], 1)[None]
    w["nsa_k"] = np.concatenate([tile(2, 0), tile(4, 0), tile(2, 1), tile(4, 1)], 1)[None]
    w["nsa_q"] = np.stack([np.concatenate([cols(ns, 256 * g, P), cols(ns, 256 * g + P, P)], 1) for g in range(4)])
    w["nsa_v"] = np.stack([m_tiles(np.concatenate([ns[:, 1792 + 64 * g:][:, :64], ns[:, 2304 + 64 * g:][:, :64]], 1))[0] for g in range(4)])
    w["nsa_out"] = m_tiles(i["nsa_w_out"][0])

    z = i["w_in_ab_2"][0]
    w["mla_z"] = np.stack([np.concatenate([cols(z, P * t, P) for t in range(3)], 1),
                           padded_free(np.concatenate([cols(z, 384, P), cols(z, 512, P), cols(z, 576, 96)], 1), 3072)])
    uq, ukv = i["mla_w_uq_2"][0], i["mla_w_ukv_2"][0]
    w["mla_q"] = np.stack([np.concatenate([cols(uq[:, 2 * h + e], 0, 96) for e in range(2)], 1) for h in range(4)])
    w["mla_kv"] = np.stack([np.concatenate(
        [cols(ukv[:, 2 * h + e], 0, 64) for e in range(2)] +
        [m_tiles(np.concatenate([ukv[:, 2 * h, 64:], ukv[:, 2 * h + 1, 64:]], 1))[0]], 1) for h in range(4)])
    qk, v = [], []
    for s in range(2):
        for j in range(2):
            qk.append(np.concatenate([cols(z, 672 + 768 * j + 256 * g + P * s, P) for g in range(3)], 1))
        v.append(np.concatenate([z[:, 672 + 1536 + 256 * g + P * s:][:, :P] for g in range(3)], 1))
    w["dil_qk"] = np.stack(qk)
    w["dil_va"] = np.stack([cols(u, 0, 256) for u in v])
    w["dil_vb"] = np.stack([cols(u, 256, P) for u in v])
    w["ab2_out"] = m_tiles(i["w_out_ab_2"][0])

    gq, gkv = i["gqa_w_q_2"][0], i["gqa_w_kv_2"][0]
    w["gqa_k"], w["gqa_v"] = m_tiles(gkv[:, 0:256]).transpose(1, 0, 2).reshape(1, P, -1), cols(gkv, 256, 256)[None]
    w["gqa_q"] = m_tiles(gq)
    w["gqa_out"] = m_tiles(i["gqa_w_o_2"][0])

    c = {}
    gains = [i["ffn1_norm"][0], i["mix_norm"][0], i["ffn2_norm"][0], i["ffn1_norm"][1], i["mix_norm"][1], i["ffn2_norm"][1],
             i["final_norm"], i["mix_norm_ab_2"][0], i["ffn_norm_2"][0], i["mix_norm_c_2"][0], i["ffn_norm_2"][1], i["final_norm_2"]]
    c["gains"] = np.concatenate([column(g) for g in gains], 1)
    taps = lambda a: a.reshape(4, -1, P).transpose(2, 1, 0).reshape(P, -1)
    c["rg_taps"] = taps(i["rg_conv_w"][0])
    c["rg_cb"], c["rg_br"], c["rg_bi"], c["rg_lam"] = (column(i[n][0]) for n in ("rg_conv_b", "rg_b_r", "rg_b_i", "rg_lambda"))
    c["ml_taps"] = taps(i["ml_conv_w"][0])
    c["ml_cb"], c["ml_norm"] = column(i["ml_conv_b"][0]), column(i["ml_norm"][0])
    c["ml_bi"], c["ml_bf"] = padded(i["ml_b_i"][0]), np.roll(padded(i["ml_b_f"][0]), 32, 0)
    c["nsa_pe"] = np.concatenate([i[n][0].reshape(16, P).T for n in ("nsa_pe_k", "nsa_pe_v")], 1)
    c["nsa_b1"] = np.concatenate([column(i[n][0]) for n in ("nsa_k_b1", "nsa_v_b1")], 1)
    k2 = i["nsa_k_w2"][0]
    c["nsa_k_w2"] = m_tiles(np.concatenate([k2, k2], 1))[0]
    c["nsa_v_w2"] = cols(i["nsa_v_w2"][0], 0, 64)
    c["nsa_bg"] = padded(i["nsa_b_gate"][0][None])
    c["mla_gq"], c["mla_gkv"] = column(i["mla_q_norm_2"][0]), column(i["mla_kv_norm_2"][0])
    c["gqa_gq"] = np.concatenate([i["gqa_q_norm_2"][0]] * 2)[:, None]
    c["gqa_gk"] = np.concatenate([i["gqa_k_norm_2"][0]] * 2)[:, None]
    return w, c


def padded_free(a, width):
    return np.concatenate([a, np.zeros((P, width - a.shape[1]), a.dtype)], 1)


class Count:

    def __init__(self, name, known, seen, by, lead):
        self.name, self.known, self.seen, self.by, self.lead = name, known, seen, by, lead
        self.count, self.loop = 0, None

    def mark(self, what=None):
        self.count += self.by
        if what is not None:
            assert (self.name, what) not in self.seen, what
            self.seen[self.name, what] = (self.count, self.loop)
        return self.by

    def per(self, loop):
        return self.known.get((self.name, "per", loop), (1, 1))

    def at(self, what, it, loop, back):
        assert not self.known or (self.name, what) in self.known, (self.name, what)
        count, within = self.known.get((self.name, what), (1, None))
        if within is None:
            return self.lead + count
        per, trips = self.per(within)
        if it is None or within != loop:
            return self.lead + count + per * (trips - 1)
        return it * per + (self.lead + count - back * per)


class Engine:

    def __init__(self, eng, own, counts, more=()):
        self.eng, self.own, self.counts = eng, own, counts
        self.raised = ([own] if own else []) + list(more)
        self.it = self.loop_tag = None
        self.chunk = 0

    def mark(self, what=None):
        return self.own.mark(what)

    def now(self):
        if self.it is None:
            return self.own.lead + self.own.count
        return self.it * self.own.per(self.loop_tag)[0] + (self.own.lead + self.own.count)

    def at(self, who, what, back=0):
        return self.counts[who].at(what, self.it, self.loop_tag, back)

    def slot(self):
        return self.chunk % NSLOT

    def loaded(self):
        self.chunk += 1
        return self.counts[f"slot{(self.chunk - 1) % NSLOT}"].mark(("chunk", self.chunk - 1))

    def chunk_loaded(self):
        return self.at(f"slot{self.slot()}", ("chunk", self.chunk))

    def used(self):
        self.chunk += 1
        return self.own.mark(("chunk", self.chunk - 1))

    @contextmanager
    def loop(self, trips, tag):
        base = {c.name: c.count for c in self.raised}
        with self.eng.Fori(0, trips) as it:
            self.it, self.loop_tag = it, tag
            for c in self.raised:
                c.loop = tag
            yield it
        for c in self.raised:
            per = c.count - base[c.name]
            c.seen[c.name, "per", tag] = (per, trips)
            c.count = base[c.name] + per * trips
            c.loop = None
        self.it = self.loop_tag = None


def build(nc, arrays, columns_at, tables_at, out, marks, stages=None):
    seen = {}
    with ExitStack() as ctx:
        sb = lambda name, n, parts=P: ctx.enter_context(nc.sbuf_tensor(name, [parts, n], F32))
        x = sb("x", KD * T)[:, :].rearrange("p (k t) -> p k t", k=KD)
        ring = sb("ring", NSLOT * SLOT)[:, :].rearrange("p (s n) -> p s n", s=NSLOT)
        colbuf = sb("colbuf", sum(n for _, n in columns_at.values()))
        tabbuf = {"all": sb("table_all", tables_at["all"][1])}
        rstd = sb("rstd", T)
        warm = sb("warm", 1)
        with ExitStack() as room:
            xn = room.enter_context(nc.sbuf_tensor("xn", [P, KD * T], F32))[:, :].rearrange("p (k t) -> p k t", k=KD)
            arena = room.enter_context(nc.sbuf_tensor("arena", [P, ARENA], F32))
            shared = room.enter_context(nc.sbuf_tensor("tables", [P, max(n for s, (_, n) in tables_at.items() if s != "all")], F32))
        tabbuf.update({stage: shared for stage in tables_at if stage != "all"})
        room = ctx.enter_context(ExitStack())
        fr = lambda name, n, k: room.enter_context(nc.sbuf_tensor(name, [P, n * k], F32R))[:, :].rearrange("p (k t) -> p k t", k=k)
        x_hi, x_lo = fr("x_hi", T, KD), fr("x_lo", T, KD)
        hid_hi, hid_lo = fr("hid_hi", T, KF), fr("hid_lo", T, KF)
        w_hi, w_lo = fr("w_hi", UNIT, 2), fr("w_lo", UNIT, 2)
        work = room.enter_context(nc.sbuf_tensor("work", [P, 4 * T], F32))[:, :].rearrange("p (k t) -> p k t", k=4)
        psum = ctx.enter_context(nc.psum_tensor("psum", [P, 8, T], F32))
        bank = lambda b: psum[:, b, :]

        def col(name, a=0, n=None):
            at, width = columns_at[name]
            return colbuf[:, at + a:at + a + (width - a if n is None else n)]

        def tab(name, a=0, n=None):
            stage = next(s for s, names in TABLES.items() if name in names)
            at, width = tables_at[stage][0][name]
            return tabbuf[stage][:, at + a:at + a + (width - a if n is None else n)]

        def dyn_col(name, it, step, a=0, n=1):
            at, _ = columns_at[name]
            return colbuf[:, ds(it * step + (at + a), n)]

        sem = lambda name: ctx.enter_context(nc.semaphore(name))
        tensor_done, scalar_done, vector_done = sem("tensor_done"), sem("scalar_done"), sem("vector_done")
        slot_loaded = [sem(f"slot{k}_loaded") for k in range(NSLOT)]
        consts_loaded, x_loaded, w1_loaded, stored = (sem(n) for n in ("consts_loaded", "x_loaded", "w1_loaded", "stored"))
        tables_loaded = sem("tables_loaded")
        unit_hi, unit_ready, unit_used, silu_ready, hidden_ready, x_updated = (
            sem(n) for n in ("unit_hi", "unit_ready", "unit_used", "silu_ready", "hidden_ready", "x_updated"))
        squared, summed = sem("squared"), sem("summed")
        counts = {n: Count(n, marks, seen, 1, LEAD) for n in ("tensor", "scalar", "vector")}
        counts.update({n: Count(n, marks, seen, 16, 0) for n in ("slot0", "slot1")})

        carve_at = [0]

        def carve_reset(to=0):
            carve_at[0] = to

        def carve(n, *shape):
            a = arena[:, carve_at[0]:carve_at[0] + n * int(np.prod(shape or (1,)))]
            carve_at[0] += n * int(np.prod(shape or (1,)))
            assert carve_at[0] <= ARENA, carve_at[0]
            if shape:
                names = "abcd"[:len(shape) + 1]
                sizes = {c: s for c, s in zip(names, (n, *shape))}
                a = a.rearrange(f"p ({' '.join(names)}) -> p {' '.join(names)}", **sizes)
            return a


        def load(sp, src, n, trip=None):
            k = sp.chunk
            if k - NSLOT >= sp.base:
                sp.eng.wait_ge(tensor_done, sp.at("tensor", ("chunk", k - NSLOT)))
            if trip is not None and k - sp.first < NSLOT:
                sp.eng.wait_ge(tensor_done, sp.at("tensor", ("chunk", k - NSLOT + trip), back=1))
            sp.eng.dma_start(ring[:, k % NSLOT, 0:n], src).then_inc(slot_loaded[k % NSLOT], sp.loaded())

        def product(out, w, rhs, n, width=P, at=0, wait=None):
            for k in range(n):
                if wait is not None:
                    wait(k)
                ins = nc.tensor.matmul(out, w[:, at + k * width:at + (k + 1) * width], rhs[k],
                                       start=k == 0, stop=k == n - 1)
            return ins

        def normed(pe, tag):
            return lambda k: pe.eng.wait_ge(vector_done, pe.at("vector", (tag, "normed", k)))

        xn_tiles = [xn[:, k, :] for k in range(KD)]
        ones, ident = tab("ones"), tab("ident")

        def start_sync(sp):
            sp.eng.dma_start(tabbuf["all"][:, :], arrays["t_all"]).then_inc(consts_loaded, 16)
            sp.eng.dma_start(colbuf[:, :], arrays["columns"]).then_inc(consts_loaded, 16)
            for i in range(4):
                sp.eng.dma_start(x_rows[:, i, :], arrays["x"][P * i:P * (i + 1), :]).then_inc(x_loaded, 16)

        x_rows = arena[:, 0:4 * D].rearrange("p (i n) -> p i n", i=4)
        all_consts = 16 * 2

        def start_tensor(pe):
            pe.eng.wait_ge(consts_loaded, all_consts)
            pe.eng.wait_ge(x_loaded, 16 * 4)
            for k in range(KD):
                for i in range(4):
                    ins = nc.tensor.transpose(bank(k)[:, P * i:P * (i + 1)], x_rows[:, i, P * k:P * (k + 1)], ident)
                ins.then_inc(tensor_done, pe.mark(("x", k)))

        def start_vector(dve):
            dve.eng.wait_ge(consts_loaded, all_consts)
            for k in range(KD):
                dve.eng.wait_ge(tensor_done, dve.at("tensor", ("x", k)))
                nc.vector.tensor_copy(x[:, k, :], bank(k)).then_inc(vector_done, dve.mark("x" if k == KD - 1 else None))

        def root(act, tag):
            act.eng.wait_ge(scalar_done, act.now())
            nc.scalar.activation(warm[:, :], ones[:, 0:1], ACT.Sqrt).then_inc(scalar_done, act.mark())
            act.eng.wait_ge(vector_done, act.at("vector", (tag, "mean")))
            nc.scalar.activation(rstd[:, :], rstd[:, :], ACT.Sqrt).then_inc(scalar_done, act.mark((tag, "rstd")))

        def norm_scalar(act, tag, src, dst, n, ready, after=None):
            tiled = tag == "m2" and "n1" in todo
            if not tiled:
                act.eng.wait_ge(*ready)
            if after is None:
                for k in range(n):
                    if tiled:
                        act.eng.wait_ge(vector_done, act.at("vector", ("n1", "normed", k)))
                    nc.scalar.activation(dst[k], src[k], ACT.Square).then_inc(scalar_done, act.mark((tag, "square", k)))
            root(act, tag)

        def norm_tensor(pe, tag, dst, n, b=0, after=None):
            if after is not None:
                pe.eng.wait_ge(summed, KD * after)
                ins = nc.tensor.matmul(bank(b), ones, rstd[:, :], start=True, stop=True)
            else:
                for k in range(n):
                    pe.eng.wait_ge(scalar_done, pe.at("scalar", (tag, "square", k)))
                    ins = nc.tensor.matmul(bank(b), ones, dst[k], start=k == 0, stop=k == n - 1)
            ins.then_inc(tensor_done, pe.mark((tag, "sum")))

        def mean(dve, tag, b, n):
            dve.eng.wait_ge(tensor_done, dve.at("tensor", (tag, "sum")))
            dve.eng.wait_ge(vector_done, dve.now())
            nc.vector.tensor_scalar(rstd[:, :], bank(b), 1.0 / n, EPS, ALU.mult, ALU.add).then_inc(vector_done, dve.mark())
            dve.eng.wait_ge(vector_done, dve.now())
            nc.vector.reciprocal(rstd[:, :], rstd[:, :]).then_inc(vector_done, dve.mark((tag, "mean")))

        def norm_vector(dve, tag, src, dst, n, gain, b=0):
            mean(dve, tag, b, n * P)
            dve.eng.wait_ge(vector_done, dve.now())
            dve.eng.wait_ge(scalar_done, dve.at("scalar", (tag, "rstd")))
            for k in range(n):
                nc.vector.scalar_tensor_tensor(dst[k], src[k], gain(k), rstd[:, :], ALU.mult, ALU.mult).then_inc(vector_done, dve.mark((tag, "normed", k)))

        def square_tile(act, no, it, j, buf, updated):
            act.eng.wait_ge(*updated)
            nc.scalar.activation(buf, x[:, ds(it * 2 + j, 1), :].rearrange("p a t -> p (a t)"), ACT.Square).then_inc(squared, 1)

        def sum_start(dve):
            dve.eng.wait_ge(vector_done, dve.now())
            nc.vector.memset(rstd[:, :], 0.0).then_inc(vector_done, dve.mark())
            dve.eng.wait_ge(vector_done, dve.now())

        def sum_tile(dve, no, it, j, buf):
            dve.eng.wait_ge(squared, it * 2 + (KD * no + j + 1))
            if no + j > 0:
                dve.eng.wait_ge(summed, it * 2 + (KD * no + j))
            nc.vector.tensor_tensor(rstd[:, :], rstd[:, :], buf, ALU.add).then_inc(summed, 1)

        x_tiles = [x[:, k, :] for k in range(KD)]

        def model_norm(n):
            return lambda k: col("gains", n * KD + k, 1)

        UP, DOWN = 2 * KF, 2 * KD
        UNITS = UP + DOWN

        def place_of(h, j, ahead=0):
            return (h + (j + ahead) // 2, (j + ahead) % 2)

        def unit_size(up):
            return (KD if up else KF // 2) * P

        def ffn_slot(e, j):
            return (e.chunk + j) % 2

        def ffn_slot_loaded(e, tag, h, j):
            return h * 16 + (16 + e.at(f"slot{ffn_slot(e, j)}", ("base", tag)))

        def ffn_sync(sp, tag, n, after_mixer):
            if after_mixer:
                for k in (1, 2):
                    sp.eng.wait_ge(tensor_done, sp.at("tensor", ("chunk", sp.chunk - k)))
            for k in range(2):
                c = counts[f"slot{k}"]
                seen[c.name, ("base", tag)] = (c.count, None)
            with sp.eng.Fori(0, KF // 2) as it:
                for j in range(2):
                    sp.eng.wait_ge(unit_ready, it * 4 + (UNITS * n + 2 * j + 2))
                    sp.eng.dma_start(ring[:, ffn_slot(sp, j), 0:2 * unit_size(True)],
                                     arrays["gate_up"][ds(it * 2 + (KF * n + j), 1)].rearrange("a p n -> (a p) n")).then_inc(slot_loaded[ffn_slot(sp, j)], 16)
            with sp.eng.Fori(0, KD // 2) as it:
                for j in range(2):
                    sp.eng.wait_ge(unit_ready, it * 4 + (UNITS * n + UP + 2 * j + 2))
                    sp.eng.dma_start(ring[:, ffn_slot(sp, j), 0:2 * unit_size(False)],
                                     arrays["down"][ds(it * 2 + (KD * n + j), 1)].rearrange("a p n -> (a p) n")).then_inc(slot_loaded[ffn_slot(sp, j)], 16)
            for k in range(2):
                counts[f"slot{k}"].count += 16 * UNITS // 4
            sp.chunk += UNITS // 2

        def split_product(out, b, hi, lo, tiles, start, stop, wait=None):
            for m, k in enumerate(tiles):
                if wait is not None:
                    wait(k)
                wh, wl = w_hi[:, b, P * m:P * (m + 1)], w_lo[:, b, P * m:P * (m + 1)]
                nc.tensor.matmul(out, wh, hi[:, k, :], start=start and m == 0, stop=False)
                nc.tensor.matmul(out, wh, lo[:, k, :], start=False, stop=False)
                ins = nc.tensor.matmul(out, wl, hi[:, k, :], start=False, stop=stop and m == len(tiles) - 1)
            return ins

        def ffn_tensor(pe, tag, n):
            def normed(k):
                pe.eng.wait_ge(vector_done, pe.at("vector", (tag, "x_lo", k)))

            if after_of[tag] is not None:
                norm_tensor(pe, tag, None, KD, b=7, after=after_of[tag])
            else:
                for k in range(KD):
                    pe.eng.wait_ge(scalar_done, pe.at("scalar", (tag, "square", k)))
                    nc.tensor.matmul(bank(7), ones, work[:, k % 4, :], start=k == 0, stop=k == KD - 1).then_inc(
                        tensor_done, pe.mark((tag, "sum") if k == KD - 1 else (tag, "square used", k)))
            with pe.eng.Fori(0, KF // 2) as it:
                for j in range(2):
                    pe.eng.wait_ge(hidden_ready, it * 2 + (KF * n + j + 1))
                    pe.eng.wait_ge(unit_ready, it * 4 + (UNITS * n + 2 * j + 5))
                    split_product(bank(2 * j), 0, x_hi, x_lo, range(KD), True, True, normed if j == 0 else None).then_inc(unit_used, 1)
                    pe.eng.wait_ge(unit_ready, it * 4 + (UNITS * n + 2 * j + 6))
                    split_product(bank(2 * j + 1), 1, x_hi, x_lo, range(KD), True, True).then_inc(unit_used, 1)
            pe.eng.wait_ge(hidden_ready, KF * n + KF // 2 + 2)
            with pe.eng.Fori(0, KD // 2) as it:
                for j in range(2):
                    pe.eng.wait_ge(x_updated, it * 2 + (KD * stage_no[tag] + j + 1))
                    pe.eng.wait_ge(unit_ready, it * 4 + (UNITS * n + UP + 2 * j + 5))
                    split_product(bank(4 + j), 0, hid_hi, hid_lo, range(KF // 2), True, False).then_inc(unit_used, 1)
                    pe.eng.wait_ge(hidden_ready, KF * (n + 1) + 2)
                    pe.eng.wait_ge(unit_ready, it * 4 + (UNITS * n + UP + 2 * j + 6))
                    split_product(bank(4 + j), 1, hid_hi, hid_lo, range(KF // 2, KF), False, True).then_inc(unit_used, 1)
            pe.chunk += UNITS // 2

        def ffn_scalar(act, tag, n, ready):
            act.eng.wait_ge(*ready)
            for k in range(KD if after_of[tag] is None else 0):
                if k >= 4:
                    act.eng.wait_ge(tensor_done, act.at("tensor", (tag, "square used", k - 4)))
                nc.scalar.activation(work[:, k % 4, :], x[:, k, :], ACT.Square).then_inc(scalar_done, act.mark((tag, "square", k)))

            def split_hi(h, j, up):
                for b in range(2):
                    if b == 0:
                        act.eng.wait_ge(slot_loaded[ffn_slot(act, j)], ffn_slot_loaded(act, tag, h, j))
                    act.eng.wait_ge(unit_used, h * 4 + (UNITS * n + 2 * j + b + 1))
                    nc.scalar.copy(w_hi[:, b, 0:unit_size(up)],
                                   ring[:, ffn_slot(act, j), unit_size(up) * b:unit_size(up) * (b + 1)]).then_inc(unit_hi, 1)
                    if b == 0:
                        yield

            def up_step(h, j, last=False):
                ahead = split_hi(*place_of(h, j, 1), up=not last)
                next(ahead)
                act.eng.wait_ge(unit_used, h * 4 + (UNITS * n + 2 * j + 3))
                act.eng.wait_ge(hidden_ready, h * 2 + (KF * n + j + 1))
                nc.scalar.activation(work[:, j, :], bank(2 * j), ACT.Silu).then_inc(silu_ready, 1)
                for _ in ahead:
                    pass

            def square_down(h, j):
                square_tile(act, stage_no[tag], h, j, work[:, j, :], (x_updated, h * 2 + (KD * stage_no[tag] + j + 3)))

            for _ in split_hi(0, 0, True):
                pass
            root(act, tag)
            for k in range(KD):
                act.eng.wait_ge(vector_done, act.at("vector", (tag, "y", k)))
                nc.scalar.copy(x_hi[:, k, :], work[:, k % 4, :]).then_inc(scalar_done, act.mark((tag, "x_hi", k)))
            with act.eng.Fori(0, KF // 2 - 1) as it:
                for j in range(2):
                    up_step(it, j)
            up_step(KF // 2 - 1, 0)
            up_step(KF // 2 - 1, 1, last=True)
            with act.eng.Fori(0, KD // 2 - 1) as it:
                for j in range(2):
                    for _ in split_hi(*place_of(it + KF // 2, j, 1), up=False):
                        pass
                    square_down(it, j)
            for _ in split_hi(KF // 2 + KD // 2 - 1, 1, up=False):
                pass
            for j in range(2):
                square_down(KD // 2 - 1, j)
            act.chunk += UNITS // 2

        def ffn_vector(dve, tag, n, gain, scale):
            def split_lo(h, j, up):
                for b in range(2):
                    dve.eng.wait_ge(unit_hi, h * 4 + (UNITS * n + 2 * j + b + 1))
                    size = unit_size(up)
                    nc.vector.tensor_tensor(w_lo[:, b, 0:size], ring[:, ffn_slot(dve, j), size * b:size * (b + 1)],
                                            w_hi[:, b, 0:size].bitcast(F32), ALU.subtract).then_inc(unit_ready, 1)

            def up_step(h, j, last=False):
                split_lo(*place_of(h, j, 1), up=not last)
                dve.eng.wait_ge(silu_ready, h * 2 + (KF * n + j + 1))
                dve.eng.wait_ge(unit_used, h * 4 + (UNITS * n + 2 * j + 4))
                dve.eng.wait_ge(hidden_ready, h * 2 + (KF * n + j + 1))
                prod = work[:, 2 + j, :]
                tile = lambda t: (t[:, ds(h * 2 + j, 1), :]).rearrange("p a t -> p (a t)")
                nc.vector.tensor_tensor(prod, work[:, j, :], bank(2 * j + 1), ALU.mult).then_inc(vector_done, dve.mark())
                dve.eng.wait_ge(vector_done, dve.now())
                nc.vector.tensor_copy(tile(hid_hi), prod).then_inc(vector_done, dve.mark())
                dve.eng.wait_ge(vector_done, dve.now())
                nc.vector.tensor_tensor(tile(hid_lo), prod, tile(hid_hi).bitcast(F32), ALU.subtract).then_inc(hidden_ready, 1)

            def down_step(h, j, last=False):
                if not last:
                    split_lo(*place_of(h + KF // 2, j, 1), up=False)
                dve.eng.wait_ge(unit_used, h * 4 + (UNITS * n + UP + 2 * j + 4))
                tile = x[:, ds(h * 2 + j, 1), :].rearrange("p a t -> p (a t)")
                nc.vector.scalar_tensor_tensor(tile, bank(4 + j), scale, tile, ALU.mult, ALU.add).then_inc(x_updated, 1)
                sum_tile(dve, stage_no[tag], h, j, work[:, j, :])

            mean(dve, tag, 7, D)
            split_lo(0, 0, True)
            dve.eng.wait_ge(scalar_done, dve.at("scalar", (tag, "rstd")))
            for k in range(KD + 1):
                if k < KD:
                    if k >= 4:
                        dve.eng.wait_ge(vector_done, dve.at("vector", (tag, "x_lo", k - 4)))
                    nc.vector.scalar_tensor_tensor(work[:, k % 4, :], x[:, k, :], col("gains", gain * KD + k, 1), rstd[:, :],
                                                   ALU.mult, ALU.mult).then_inc(vector_done, dve.mark((tag, "y", k)))
                if k >= 1:
                    dve.eng.wait_ge(scalar_done, dve.at("scalar", (tag, "x_hi", k - 1)))
                    dve.eng.wait_ge(vector_done, dve.at("vector", (tag, "y", k - 1)))
                    nc.vector.tensor_tensor(x_lo[:, k - 1, :], work[:, (k - 1) % 4, :], x_hi[:, k - 1, :].bitcast(F32),
                                            ALU.subtract).then_inc(vector_done, dve.mark((tag, "x_lo", k - 1)))
            with dve.loop(KF // 2 - 1, (tag, "up")) as it:
                for j in range(2):
                    up_step(it, j)
            up_step(KF // 2 - 1, 0)
            up_step(KF // 2 - 1, 1, last=True)
            sum_start(dve)
            with dve.eng.Fori(0, KD // 2 - 1) as it:
                for j in range(2):
                    down_step(it, j)
            down_step(KD // 2 - 1, 0)
            down_step(KD // 2 - 1, 1, last=True)
            dve.chunk += UNITS // 2

        def out_sync(sp, tag, name, n):
            with sp.loop(KD // 2, (tag, "out")) as it:
                sp.first = sp.chunk
                for j in range(2):
                    load(sp, arrays[name][ds(it * 2 + j, 1)].rearrange("a p n -> (a p) n"), n * P, 2)

        def out_tensor(pe, tag, mixed, n, last=None):
            wait = lambda k: pe.eng.wait_ge(*last) if last is not None and k == n - 1 else None
            with pe.loop(KD // 2, (tag, "out")) as it:
                for j in range(2):
                    pe.eng.wait_ge(slot_loaded[pe.slot()], pe.chunk_loaded())
                    w = ring[:, pe.slot(), :]
                    pe.eng.wait_ge(x_updated, it * 2 + (KD * stage_no[tag] + j + 1))
                    product(bank(j), w, mixed, n, wait=wait if j == 0 else None).then_inc(tensor_done, pe.used())

        def out_scalar(act, tag):
            with act.loop(KD // 2, (tag, "out")) as it:
                for j in range(2):
                    square_tile(act, stage_no[tag], it, j, xn[:, j, :], (x_updated, it * 2 + (KD * stage_no[tag] + j + 3)))
            act.chunk += 2

        def out_vector(dve, tag):
            first = dve.chunk
            sum_start(dve)
            with dve.loop(KD // 2, (tag, "out")) as it:
                for j in range(2):
                    dve.eng.wait_ge(tensor_done, dve.at("tensor", ("chunk", first + j)))
                    tile = x[:, ds(it * 2 + j, 1), :].rearrange("p a t -> p (a t)")
                    nc.vector.tensor_tensor(tile, bank(j), tile, ALU.add).then_inc(x_updated, 1)
                    sum_tile(dve, stage_no[tag], it, j, xn[:, j, :])
            dve.chunk += 2

        y_rows = arena[:, 0:4 * D].rearrange("p (i n) -> p i n", i=4)

        def end_tensor(pe, ready):
            pe.eng.wait_ge(vector_done, pe.at("vector", ready))
            for i in range(4):
                for h in range(2):
                    for k in range(4):
                        ins = nc.tensor.transpose(bank(2 * i + h)[:, P * k:P * (k + 1)],
                                                  xn[:, 4 * h + k, P * i:P * (i + 1)], ident)
                    ins.then_inc(tensor_done, pe.mark(("y", i, h)))

        def end_vector(dve):
            for i in range(4):
                for h in range(2):
                    dve.eng.wait_ge(tensor_done, dve.at("tensor", ("y", i, h)))
                    nc.vector.tensor_copy(y_rows[:, i, 512 * h:512 * (h + 1)], bank(2 * i + h)).then_inc(vector_done, dve.mark(("y", i, h)))

        def end_sync(sp):
            for i in range(4):
                sp.eng.wait_ge(vector_done, sp.at("vector", ("y", i, 1)))
                sp.eng.dma_start(out[P * i:P * (i + 1), :], y_rows[:, i, :]).then_inc(stored, 16)
            sp.eng.wait_ge(stored, 16 * 4)

        MIXERS = {}

        CH = 128
        NC_ = T // CH
        carve_reset()
        ab_mixed = carve(9, T)
        ab_mixed_tiles = [ab_mixed[:, k, :] for k in (0, 1, 2, 3, 5, 6, 7, 8)]
        rows = carve(14, T)
        ROW = {n: i for i, n in enumerate(["li", "f", "af", "lf", "b", "c", "M", "m", "sc", "wk", "one", "em", "t0", "t1"])}
        row = lambda n, a=0, w=T: rows[0:4, ROW[n], a:a + w]
        spread = carve(3, 4, T)
        rcol = carve(2, NC_, 4)
        lam = carve(12, 4)
        lamx = lambda i: lam[:, i, :]
        small0 = carve_at[0]
        rg = carve(10, T)
        RG = {n: i for i, n in enumerate(["conv", "r", "ig", "a", "t", "u", "gelu", "h", "v", "w"])}
        rgt = lambda n: rg[:, RG[n], :]
        carve_reset(small0)
        ml = carve(12, T)
        ML = {n: i for i, n in enumerate(["q", "k", "qs", "E", "P", "kw", "ho", "o", "den", "sq", "rs", "cq"])}
        mlt = lambda n: ml[:, ML[n], :]
        mv = carve(NC_, 2 * P)
        state = carve(3, 2 * P)

        def ab_sync(sp):
            load(sp, arrays["ab_gates"][0], KD * 36)
            with sp.loop(4, "rg") as it:
                sp.first = sp.chunk
                for j, n in enumerate((1024, 1280)):
                    load(sp, arrays["rg"][ds(it * 2 + j, 1), :, 0:n].rearrange("a p n -> (a p) n"), n, 2)
            with sp.loop(4, "ml") as it:
                sp.first = sp.chunk
                for j in range(2):
                    load(sp, arrays["ml"][ds(it * 2 + j, 1)].rearrange("a p n -> (a p) n"), 2048, 2)
            out_sync(sp, "ab", "ab_out", 8)

        def ab_tensor(pe):
            norm_tensor(pe, "ab", xn_tiles, KD, after=after_of["ab"])
            pe.eng.wait_ge(slot_loaded[pe.slot()], pe.chunk_loaded())
            w = ring[:, pe.slot(), :]
            product(bank(1)[0:36, :], w, xn_tiles, KD, width=36, wait=normed(pe, "ab")).then_inc(tensor_done, pe.used())
            with pe.loop(4, "rg"):
                pe.eng.wait_ge(slot_loaded[pe.slot()], pe.chunk_loaded())
                product(bank(4), ring[:, pe.slot(), :], xn_tiles, KD).then_inc(tensor_done, pe.used())
                pe.eng.wait_ge(slot_loaded[pe.slot()], pe.chunk_loaded())
                w = ring[:, pe.slot(), :]
                pe.eng.wait_ge(scalar_done, pe.at("scalar", "rg gelu", back=1))
                product(bank(5), w, xn_tiles, KD).then_inc(tensor_done, pe.mark("rg ga"))
                pe.eng.wait_ge(scalar_done, pe.at("scalar", "rg ig", back=1))
                pe.eng.wait_ge(vector_done, pe.at("vector", "rg conv"))
                nc.tensor.matmul(bank(6), w[:, 1024:1152], rgt("conv"), start=True, stop=True).then_inc(tensor_done, pe.mark("rg r"))
                nc.tensor.matmul(bank(7), w[:, 1152:1280], rgt("conv"), start=True, stop=True).then_inc(tensor_done, pe.used())
            pe.eng.wait_ge(scalar_done, pe.at("scalar", "ml wk"))
            for a, n in enumerate(("c", "wk")):
                for c in range(NC_):
                    ins = nc.tensor.transpose(bank(3)[:, (a * NC_ + c) * 4:(a * NC_ + c) * 4 + 4], row(n, c * CH, CH), ident[0:4, 0:4])
            ins.then_inc(tensor_done, pe.mark("ml cols"))

            def squares_sum(name):
                nc.tensor.matmul(bank(6), ones, mlt("sq"), start=True, stop=True).then_inc(tensor_done, pe.mark(name))

            with pe.loop(4, "ml") as it:
                pe.eng.wait_ge(slot_loaded[pe.slot()], pe.chunk_loaded())
                w = ring[:, pe.slot(), :]
                product(bank(0), w, xn_tiles, KD).then_inc(tensor_done, pe.mark("ml q"))
                product(bank(1), w, xn_tiles, KD, at=1024).then_inc(tensor_done, pe.used())
                pe.eng.wait_ge(vector_done, pe.at("vector", "ml begin"))
                pe.eng.wait_ge(scalar_done, pe.at("scalar", "ml sq", back=1))
                squares_sum("ml ss")
                pe.eng.wait_ge(slot_loaded[pe.slot()], pe.chunk_loaded())
                w = ring[:, pe.slot(), :]
                for i in range(NC_):
                    for k in range(KD):
                        ins = nc.tensor.matmul(bank(2)[:, P * i:P * (i + 1)], xn[:, k, P * i:P * (i + 1)],
                                               w[:, P * k:P * (k + 1)], start=k == 0, stop=k == KD - 1)
                ins.then_inc(tensor_done, pe.mark("ml v"))
                pe.eng.wait_ge(vector_done, pe.at("vector", "ml rows"))
                pe.eng.wait_ge(scalar_done, pe.at("scalar", "ml o", back=1))
                product(bank(3), w, xn_tiles, KD, at=1024).then_inc(tensor_done, pe.used())
                pe.eng.wait_ge(vector_done, pe.at("vector", "ml h", back=1))
                nc.tensor.matmul(bank(4), ones[0:4, :], spread[0:4, 0, ds(it, 1), :].rearrange("p a t -> p (a t)"), start=True, stop=False)
                nc.tensor.matmul(bank(4), ident, tab("future"), start=False, stop=True).then_inc(tensor_done, pe.mark("ml M"))
                nc.tensor.matmul(bank(5), ones[0:4, :], spread[0:4, 1, ds(it, 1), :].rearrange("p a t -> p (a t)"), start=True, stop=True).then_inc(tensor_done, pe.mark("ml sc"))
                pe.eng.wait_ge(vector_done, pe.at("vector", "ml mean"))
                nc.tensor.matmul(bank(6), ones[0:4, :], spread[0:4, 2, ds(it, 1), :].rearrange("p a t -> p (a t)"), start=True, stop=True).then_inc(tensor_done, pe.mark("ml em"))
                pe.eng.wait_ge(scalar_done, pe.at("scalar", "ml qk silu"))
                for c in range(NC_):
                    ins = nc.tensor.matmul(bank(7)[:, c * CH:(c + 1) * CH], mlt("k")[:, c * CH:(c + 1) * CH],
                                           mlt("q")[:, c * CH:(c + 1) * CH], start=True, stop=True)
                ins.then_inc(tensor_done, pe.mark("ml s"))
                for c in range(NC_ - 1):
                    ins = nc.tensor.transpose(bank(0)[:, c * CH:(c + 1) * CH], mlt("k")[:, c * CH:(c + 1) * CH], ident)
                ins.then_inc(tensor_done, pe.mark("ml kT"))
                pe.eng.wait_ge(vector_done, pe.at("vector", "ml v"))
                pe.eng.wait_ge(vector_done, pe.at("vector", "ml kw"))
                for c in range(NC_ - 1):
                    ins = nc.tensor.matmul(bank(1 + c // 2)[:, 256 * (c % 2):256 * (c % 2) + 256],
                                           mlt("kw")[:, c * CH:(c + 1) * CH], mv[:, c, :], start=True, stop=True)
                ins.then_inc(tensor_done, pe.mark("ml state"))
                pe.eng.wait_ge(vector_done, pe.at("vector", "ml P"))
                pe.eng.wait_ge(vector_done, pe.at("vector", "ml states"))
                for c in range(NC_):
                    at = slice(c * CH, (c + 1) * CH)
                    nc.tensor.matmul(bank(4)[:, at], mv[:, c, 0:P], mlt("P")[:, at], start=True, stop=c == 0)
                    if c:
                        nc.tensor.matmul(bank(4)[:, at], state[:, c - 1, 0:P], mlt("qs")[:, at], start=False, stop=True)
                for c in range(NC_):
                    at = slice(c * CH, (c + 1) * CH)
                    ins = nc.tensor.matmul(bank(7)[:, at], ones, mlt("P")[:, at], start=True, stop=c == 0)
                    if c:
                        ins = nc.tensor.matmul(bank(7)[:, at], state[:, c - 1, P:2 * P], mlt("qs")[:, at], start=False, stop=True)
                ins.then_inc(tensor_done, pe.mark("ml den"))
            pe.eng.wait_ge(scalar_done, pe.at("scalar", "ml sq"))
            squares_sum("ml last ss")
            out_tensor(pe, "ab", ab_mixed_tiles, 8, last=(vector_done, pe.at("vector", "ml last mixed")))

        def ab_scalar(act, ready):
            norm_scalar(act, "ab", x_tiles, xn_tiles, KD, ready, after=after_of["ab"])
            act.eng.wait_ge(vector_done, act.at("vector", "rg |lam|"))
            nc.scalar.activation(lamx(1), lamx(0), ACT.Exp, scale=-1.0).then_inc(scalar_done, act.mark("rg exp lam"))
            act.eng.wait_ge(vector_done, act.at("vector", "ml |f|"))
            nc.scalar.activation(row("t0"), row("af"), ACT.Exp, scale=-1.0).then_inc(scalar_done, act.mark())
            act.eng.wait_ge(scalar_done, act.now())
            nc.scalar.activation(row("t1"), row("t0"), ACT.Ln, bias=1.0).then_inc(scalar_done, act.mark("ml ln"))
            act.eng.wait_ge(vector_done, act.at("vector", "ml m"))
            nc.scalar.activation(row("sc"), row("t0"), ACT.Exp).then_inc(scalar_done, act.mark("ml sc"))
            nc.scalar.activation(row("em"), row("m"), ACT.Exp, scale=-1.0).then_inc(scalar_done, act.mark("ml em"))
            nc.scalar.activation(row("wk"), row("t1"), ACT.Exp).then_inc(scalar_done, act.mark("ml wk"))
            with act.loop(4, "rg") as it:
                act.eng.wait_ge(tensor_done, act.at("tensor", "rg ga"))
                act.eng.wait_ge(vector_done, act.at("vector", "rg mixed", back=1))
                nc.scalar.activation(rgt("gelu"), bank(5), ACT.Gelu_apprx_tanh).then_inc(scalar_done, act.mark("rg gelu"))
                act.eng.wait_ge(tensor_done, act.at("tensor", "rg r"))
                nc.scalar.activation(rgt("r"), bank(6), ACT.Sigmoid, bias=dyn_col("rg_br", it, 1)).then_inc(scalar_done, act.mark())
                act.eng.wait_ge(tensor_done, act.at("tensor", ("chunk", act.chunk + 2)))
                nc.scalar.activation(rgt("ig"), bank(7), ACT.Sigmoid, bias=dyn_col("rg_bi", it, 1)).then_inc(scalar_done, act.mark("rg ig"))
                act.eng.wait_ge(scalar_done, act.now())
                nc.scalar.activation(rgt("a"), rgt("r"), ACT.Exp, scale=lam[:, 11, ds(it, 1)]).then_inc(scalar_done, act.mark("rg a"))
                nc.scalar.activation(rgt("t"), rgt("r"), ACT.Tanh, scale=lam[:, 11, ds(it, 1)]).then_inc(scalar_done, act.mark("rg t"))
                act.eng.wait_ge(vector_done, act.at("vector", "rg u2"))
                nc.scalar.activation(rgt("u"), rgt("u"), ACT.Sqrt).then_inc(scalar_done, act.mark("rg sqrt"))

            def head_root(pre):
                act.eng.wait_ge(vector_done, act.at("vector", pre + "mean"))
                nc.scalar.activation(mlt("rs"), mlt("rs"), ACT.Sqrt).then_inc(scalar_done, act.mark(pre + "rstd"))

            with act.loop(4, "ml") as it:
                act.eng.wait_ge(vector_done, act.at("vector", "ml qk conv"))
                nc.scalar.activation(mlt("q"), mlt("qs"), ACT.Silu).then_inc(scalar_done, act.mark())
                nc.scalar.activation(mlt("k"), mlt("cq"), ACT.Silu).then_inc(scalar_done, act.mark("ml qk silu"))
                head_root("ml ")
                act.eng.wait_ge(tensor_done, act.at("tensor", ("chunk", act.chunk + 4)))
                act.eng.wait_ge(vector_done, act.at("vector", "ml mixed"))
                nc.scalar.activation(mlt("o"), bank(3), ACT.Sigmoid).then_inc(scalar_done, act.mark("ml o"))
                act.eng.wait_ge(tensor_done, act.at("tensor", "ml M"))
                for c in range(NC_):
                    at = slice(c * CH, (c + 1) * CH)
                    nc.scalar.activation(mlt("E")[:, at], bank(4)[:, at], ACT.Exp, scale=-1.0,
                                                  bias=rcol[:, 0, c, ds(it, 1)]).then_inc(scalar_done, act.mark("ml E" if c == NC_ - 1 else None))
                act.eng.wait_ge(tensor_done, act.at("tensor", "ml den"))
                nc.scalar.activation(mlt("den"), bank(7), ACT.Abs).then_inc(scalar_done, act.mark("ml |den|"))
                act.eng.wait_ge(vector_done, act.at("vector", "ml h"))
                nc.scalar.activation(mlt("sq"), mlt("ho"), ACT.Square).then_inc(scalar_done, act.mark("ml sq"))
            head_root("ml last ")
            act.chunk += 5
            out_scalar(act, "ab")

        def conv4(dve, out, src, taps, bias):
            nc.vector.tensor_scalar(out, src, taps(3), bias, ALU.mult, ALU.add).then_inc(vector_done, dve.mark())
            dve.eng.wait_ge(vector_done, dve.now())
            for j in (1, 2, 3):
                ins = nc.vector.scalar_tensor_tensor(out[:, j:T], src[:, 0:T - j], taps(3 - j), out[:, j:T], ALU.mult, ALU.add)
                if j < 3:
                    ins.then_inc(vector_done, dve.mark())
                    dve.eng.wait_ge(vector_done, dve.now())
            return ins

        def ab_vector(dve):
            norm_vector(dve, "ab", x_tiles, xn_tiles, KD, model_norm(1))
            first = dve.chunk
            la = col("rg_lam")
            nc.vector.scalar_tensor_tensor(lamx(0), la, -1.0, la, ALU.mult, ALU.max).then_inc(vector_done, dve.mark("rg |lam|"))
            dve.eng.wait_ge(vector_done, dve.now())
            dve.eng.wait_ge(scalar_done, dve.at("scalar", "rg exp lam"))
            nc.vector.tensor_scalar(lamx(2), lamx(1), 2.0, None, ALU.add).then_inc(vector_done, dve.mark())
            dve.eng.wait_ge(vector_done, dve.now())
            nc.vector.reciprocal(lamx(2), lamx(2)).then_inc(vector_done, dve.mark())
            dve.eng.wait_ge(vector_done, dve.now())
            nc.vector.tensor_tensor(lamx(3), lamx(1), lamx(2), ALU.mult).then_inc(vector_done, dve.mark())
            dve.eng.wait_ge(vector_done, dve.now())
            nc.vector.tensor_tensor(lamx(4), lamx(3), lamx(3), ALU.mult).then_inc(vector_done, dve.mark())
            dve.eng.wait_ge(vector_done, dve.now())
            nc.vector.tensor_scalar(lamx(5), lamx(4), 1.0 / 17, None, ALU.mult).then_inc(vector_done, dve.mark())
            dve.eng.wait_ge(vector_done, dve.now())
            for n in (15, 13, 11, 9, 7, 5, 3):
                nc.vector.scalar_tensor_tensor(lamx(5), lamx(5), 1.0 / n, lamx(4), ALU.add, ALU.mult).then_inc(vector_done, dve.mark())
                dve.eng.wait_ge(vector_done, dve.now())
            nc.vector.scalar_tensor_tensor(lamx(5), lamx(5), 1.0, lamx(3), ALU.add, ALU.mult).then_inc(vector_done, dve.mark())
            dve.eng.wait_ge(vector_done, dve.now())
            nc.vector.tensor_scalar(lamx(6), la, -1.0, 0.0, ALU.mult, ALU.max).then_inc(vector_done, dve.mark())
            dve.eng.wait_ge(vector_done, dve.now())
            nc.vector.scalar_tensor_tensor(lamx(7), lamx(5), 2.0, lamx(6), ALU.mult, ALU.add).then_inc(vector_done, dve.mark())
            dve.eng.wait_ge(vector_done, dve.now())
            nc.vector.tensor_scalar(lamx(11), lamx(7), -8.0, None, ALU.mult).then_inc(vector_done, dve.mark())
            dve.eng.wait_ge(vector_done, dve.now())
            dve.eng.wait_ge(tensor_done, dve.at("tensor", ("chunk", first)))
            nc.vector.tensor_scalar(row("li"), bank(1)[0:4, :], col("ml_bi")[0:4, :], None, ALU.add).then_inc(vector_done, dve.mark())
            nc.vector.tensor_scalar(row("f"), bank(1)[32:36, :], col("ml_bf")[32:36, :], None, ALU.add).then_inc(vector_done, dve.mark())
            dve.eng.wait_ge(vector_done, dve.now())
            nc.vector.scalar_tensor_tensor(row("af"), row("f"), -1.0, row("f"), ALU.mult, ALU.max).then_inc(vector_done, dve.mark("ml |f|"))
            nc.vector.memset(row("one"), 1.0).then_inc(vector_done, dve.mark())
            dve.eng.wait_ge(scalar_done, dve.at("scalar", "ml ln"))
            nc.vector.scalar_tensor_tensor(row("lf"), row("f"), 0.0, row("t1"), ALU.min, ALU.subtract).then_inc(vector_done, dve.mark())
            dve.eng.wait_ge(vector_done, dve.now())
            for c in range(NC_):
                ins = nc.vector.tensor_tensor_scan(row("b", c * CH, CH), row("one", c * CH, CH), row("lf", c * CH, CH), 0.0, ALU.mult, ALU.add)
                ins.then_inc(vector_done, dve.mark())
            dve.eng.wait_ge(vector_done, dve.now())
            nc.vector.tensor_tensor(row("c"), row("li"), row("b"), ALU.subtract).then_inc(vector_done, dve.mark())
            dve.eng.wait_ge(vector_done, dve.now())
            for c in range(NC_):
                m0 = NEG if c == 0 else row("m", c * CH - 1, 1)
                nc.vector.tensor_tensor_scan(row("M", c * CH, CH), row("c", c * CH, CH), row("c", c * CH, CH), m0, ALU.max, ALU.max).then_inc(vector_done, dve.mark())
                dve.eng.wait_ge(vector_done, dve.now())
                nc.vector.tensor_tensor(row("m", c * CH, CH), row("M", c * CH, CH), row("b", c * CH, CH), ALU.add).then_inc(vector_done, dve.mark())
                nc.vector.tensor_scalar(row("t0", c * CH, CH), row("M", c * CH, CH), -1.0, m0, ALU.mult, ALU.add).then_inc(vector_done, dve.mark())
                nc.vector.tensor_scalar(row("t1", c * CH, CH), row("c", c * CH, CH), row("M", (c + 1) * CH - 1, 1), None, ALU.subtract).then_inc(vector_done, dve.mark("ml m" if c == NC_ - 1 else None))
                dve.eng.wait_ge(vector_done, dve.now())
            dve.eng.wait_ge(scalar_done, dve.at("scalar", "ml wk"))
            for a, n in enumerate(("M", "sc", "em")):
                for h in range(4):
                    nc.vector.tensor_scalar(spread[0:4, a, h, :], row(n), tab("sel4", h, 1)[0:4, :], None, ALU.mult).then_inc(vector_done, dve.mark())
            with dve.loop(4, "rg") as it:
                dve.eng.wait_ge(tensor_done, dve.at("tensor", ("chunk", first + 1)))
                conv4(dve, rgt("conv"), bank(4), lambda j: dyn_col("rg_taps", it, 4, j), dyn_col("rg_cb", it, 1)).then_inc(vector_done, dve.mark("rg conv"))
                dve.eng.wait_ge(scalar_done, dve.at("scalar", "rg t"))
                nc.vector.tensor_tensor(rgt("v"), rgt("a"), rgt("a"), ALU.mult).then_inc(vector_done, dve.mark())
                dve.eng.wait_ge(vector_done, dve.now())
                nc.vector.scalar_tensor_tensor(rgt("w"), rgt("v"), 1.0, rgt("t"), ALU.add, ALU.mult).then_inc(vector_done, dve.mark())
                dve.eng.wait_ge(vector_done, dve.now())
                nc.vector.tensor_scalar(rgt("u"), rgt("w"), -1.0, 0.0, ALU.mult, ALU.max).then_inc(vector_done, dve.mark("rg u2"))
                dve.eng.wait_ge(vector_done, dve.now())
                nc.vector.tensor_tensor(rgt("v"), rgt("ig"), rgt("conv"), ALU.mult).then_inc(vector_done, dve.mark())
                dve.eng.wait_ge(vector_done, dve.now())
                dve.eng.wait_ge(scalar_done, dve.at("scalar", "rg sqrt"))
                nc.vector.tensor_tensor(rgt("w"), rgt("v"), rgt("u"), ALU.mult).then_inc(vector_done, dve.mark())
                dve.eng.wait_ge(vector_done, dve.now())
                nc.vector.tensor_tensor_scan(rgt("h"), rgt("a"), rgt("w"), 0.0, ALU.mult, ALU.add).then_inc(vector_done, dve.mark())
                dve.eng.wait_ge(vector_done, dve.now())
                dve.eng.wait_ge(scalar_done, dve.at("scalar", "rg gelu"))
                nc.vector.tensor_tensor(ab_mixed[:, ds(it, 1), :].rearrange("p a t -> p (a t)"), rgt("gelu"), rgt("h"), ALU.mult).then_inc(vector_done, dve.mark("rg mixed"))
            dve.eng.wait_ge(tensor_done, dve.at("tensor", "ml cols"))
            nc.vector.tensor_copy(rcol[:, :, :, :], bank(3)[:, 0:2 * NC_ * 4].rearrange("p (a c h) -> p a c h", a=2, c=NC_)).then_inc(vector_done, dve.mark("ml rows"))
            dve.eng.wait_ge(vector_done, dve.now())
            for c in range(NC_):
                nc.vector.memset(mv[:, c, P:2 * P], 1.0).then_inc(vector_done, dve.mark())
            for name in ("ho", "o", "sq"):
                nc.vector.memset(mlt(name), 1.0).then_inc(vector_done, dve.mark("ml begin" if name == "sq" else None))
            scale = float(P) ** -0.5

            def tail(pre, gain, mixed):
                dve.eng.wait_ge(vector_done, dve.now())
                dve.eng.wait_ge(tensor_done, dve.at("tensor", pre + "ss"))
                nc.vector.tensor_scalar(mlt("rs"), bank(6), 1.0 / P, EPS, ALU.mult, ALU.add).then_inc(vector_done, dve.mark())
                dve.eng.wait_ge(vector_done, dve.now())
                nc.vector.reciprocal(mlt("rs"), mlt("rs")).then_inc(vector_done, dve.mark(pre + "mean"))
                dve.eng.wait_ge(vector_done, dve.now())
                dve.eng.wait_ge(scalar_done, dve.at("scalar", pre + "rstd"))
                nc.vector.scalar_tensor_tensor(mlt("den"), mlt("ho"), gain, mlt("rs"), ALU.mult, ALU.mult).then_inc(vector_done, dve.mark())
                dve.eng.wait_ge(vector_done, dve.now())
                nc.vector.tensor_tensor(mixed, mlt("den"), mlt("o"), ALU.mult).then_inc(vector_done, dve.mark(pre + "mixed"))

            with dve.loop(4, "ml") as it:
                dve.eng.wait_ge(tensor_done, dve.at("tensor", "ml q"))
                conv4(dve, mlt("qs"), bank(0), lambda j: dyn_col("ml_taps", it, 4, j), dyn_col("ml_cb", it, 1)).then_inc(vector_done, dve.mark())
                dve.eng.wait_ge(tensor_done, dve.at("tensor", ("chunk", first + 3)))
                conv4(dve, mlt("cq"), bank(1), lambda j: dyn_col("ml_taps", it, 4, 16 + j), dyn_col("ml_cb", it, 1, 4)).then_inc(vector_done, dve.mark("ml qk conv"))
                tail("ml ", dyn_col("ml_norm", it, 1, -1), ab_mixed[:, ds(it + 4, 1), :].rearrange("p a t -> p (a t)"))
                dve.eng.wait_ge(tensor_done, dve.at("tensor", "ml v"))
                nc.vector.tensor_copy(mv[:, :, 0:P], bank(2).rearrange("p (c n) -> p c n", c=NC_)).then_inc(vector_done, dve.mark("ml v"))
                dve.eng.wait_ge(tensor_done, dve.at("tensor", "ml kT"))
                for c in range(NC_ - 1):
                    nc.vector.tensor_scalar(mlt("kw")[:, c * CH:(c + 1) * CH], bank(0)[:, c * CH:(c + 1) * CH],
                                                     rcol[:, 1, c, ds(it, 1)], None, ALU.mult).then_inc(vector_done, dve.mark("ml kw" if c == NC_ - 2 else None))
                dve.eng.wait_ge(scalar_done, dve.at("scalar", "ml E"))
                dve.eng.wait_ge(tensor_done, dve.at("tensor", "ml s"))
                nc.vector.scalar_tensor_tensor(mlt("P"), bank(7), scale, mlt("E"), ALU.mult, ALU.mult).then_inc(vector_done, dve.mark("ml P"))
                dve.eng.wait_ge(tensor_done, dve.at("tensor", "ml sc"))
                nc.vector.scalar_tensor_tensor(mlt("qs"), mlt("q"), scale, bank(5), ALU.mult, ALU.mult).then_inc(vector_done, dve.mark())
                dve.eng.wait_ge(tensor_done, dve.at("tensor", "ml state"))
                nc.vector.tensor_copy(mlt("rs")[:, 0:4], bank(5)[:, CH - 1:T:CH]).then_inc(vector_done, dve.mark())
                nc.vector.tensor_copy(state[:, 0, :], bank(1)[:, 0:256]).then_inc(vector_done, dve.mark())
                dve.eng.wait_ge(vector_done, dve.now())
                for c in (1, 2):
                    nc.vector.scalar_tensor_tensor(state[:, c, :], state[:, c - 1, :], mlt("rs")[:, c:c + 1],
                                                             bank(1 + c // 2)[:, 256 * (c % 2):256 * (c % 2) + 256], ALU.mult, ALU.add).then_inc(vector_done, dve.mark("ml states" if c == 2 else None))
                    dve.eng.wait_ge(vector_done, dve.now())
                dve.eng.wait_ge(scalar_done, dve.at("scalar", "ml |den|"))
                nc.vector.tensor_tensor(mlt("den"), mlt("den"), bank(6), ALU.max).then_inc(vector_done, dve.mark())
                dve.eng.wait_ge(vector_done, dve.now())
                nc.vector.reciprocal(mlt("den"), mlt("den")).then_inc(vector_done, dve.mark())
                dve.eng.wait_ge(vector_done, dve.now())
                nc.vector.tensor_tensor(mlt("ho"), mlt("den"), bank(4), ALU.mult).then_inc(vector_done, dve.mark("ml h"))
                dve.eng.wait_ge(vector_done, dve.now())
            tail("ml last ", col("ml_norm", 3, 1), ab_mixed[:, 8, :])
            dve.chunk += 5
            out_vector(dve, "ab")

        MIXERS["ab"] = {"sync": ab_sync, "tensor": ab_tensor, "scalar": ab_scalar, "vector": ab_vector}

        class Step:

            def __init__(self, scores, masks, parts, values, out, group, gates=None, any_key=None):
                self.scores, self.masks, self.parts, self.values, self.out = scores, masks, parts, values, out
                self.group, self.gates, self.any_key = group, gates, any_key

        def att_carve():
            return carve(2, 2 * T), carve(2, 2 * T), carve(2, 12)

        def area(n):
            return psum[:, 2 * (n % 2):2 * (n % 2) + 2, :].rearrange("p b t -> p (b t)")

        def turned_blocks(step):
            runs = []
            for m, (_, keys, _) in enumerate(step.values):
                if runs and runs[-1][2] == keys:
                    runs[-1] = (runs[-1][0], m + 1, keys)
                else:
                    runs.append((m, m + 1, keys))
            return runs

        def att_tensor(pe, tag, steps, buf):
            p, pT, _ = buf
            turned = psum[:, 4:6, :].rearrange("p b t -> p (b t)")
            last = len(steps) - 1

            def scores(n):
                if n >= 2:
                    pe.eng.wait_ge(scalar_done, pe.at("scalar", (tag, "exp", n - 2)))
                for q, k, at in steps[n].scores:
                    ins = nc.tensor.matmul(area(n)[:, at:at + k.free_size()], q, k, start=True, stop=True)
                ins.then_inc(tensor_done, pe.mark((tag, "scores", n)))

            def turn(n):
                pe.eng.wait_ge(vector_done, pe.at("vector", (tag, "p", n)))
                for m, (at, keys, _) in enumerate(steps[n].values):
                    ins = nc.tensor.transpose(turned[0:keys, P * m:P * m + P], p[:, n % 2, at:at + keys], ident)
                ins.then_inc(tensor_done, pe.mark((tag, "turn", n)))

            def values(n):
                b, parts, where = steps[n].out
                for m, (_, keys, v) in enumerate(steps[n].values):
                    ins = nc.tensor.matmul(bank(b)[parts, where], v, pT[0:keys, n % 2, P * m:P * m + P],
                                           start=m == 0, stop=m == len(steps[n].values) - 1)
                ins.then_inc(tensor_done, pe.mark((tag, "values", n)))

            scores(0)
            scores(1)
            for n in range(last + 2):
                if n + 2 <= last:
                    scores(n + 2)
                if n >= 1:
                    pe.eng.wait_ge(scalar_done, pe.at("scalar", (tag, "turned", n - 1)))
                if n <= last:
                    turn(n)
                if n >= 1:
                    values(n - 1)

        def att_scalar(act, tag, steps, buf, mixed):
            p, pT, stats = buf
            last = len(steps) - 1

            def exps(n):
                act.eng.wait_ge(vector_done, act.at("vector", (tag, "max", n)))
                for m, (a, b) in enumerate(steps[n].parts):
                    nc.scalar.activation(p[:, n % 2, a:b], area(n)[:, a:b], ACT.Exp, bias=stats[:, n % 2, m:m + 1],
                                         accum_out=stats[:, n % 2, 4 + m:5 + m]).then_inc(
                        scalar_done, act.mark((tag, "exp", n) if m == len(steps[n].parts) - 1 else None))

            def copy_turned(n):
                act.eng.wait_ge(tensor_done, act.at("tensor", (tag, "turn", n)))
                if n >= 2:
                    act.eng.wait_ge(tensor_done, act.at("tensor", (tag, "values", n - 2)))
                runs = turned_blocks(steps[n])
                for i, (a, b, keys) in enumerate(runs):
                    src = psum[0:keys, 4:6, :].rearrange("p b t -> p (b t)")[:, P * a:P * b]
                    nc.scalar.copy(pT[0:keys, n % 2, P * a:P * b], src).then_inc(
                        scalar_done, act.mark((tag, "turned", n) if i == len(runs) - 1 else None))

            exps(0)
            exps(1)
            for n in range(last + 2):
                if n <= last:
                    copy_turned(n)
                if n + 2 <= last:
                    exps(n + 2)
                if n >= 1 and (n == last + 1 or steps[n].group != steps[n - 1].group):
                    group = steps[n - 1].group
                    act.eng.wait_ge(tensor_done, act.at("tensor", (tag, "values", n - 1)))
                    to = mixed(group)
                    nc.scalar.copy(to, bank(steps[n - 1].out[0]) if len(to.shape) == 2 else in_order(bank(steps[n - 1].out[0]))).then_inc(
                        scalar_done, act.mark((tag, "mixed", group)))

        def att_vector(dve, tag, steps, buf):
            p, _, stats = buf
            last = len(steps) - 1

            def maxima(n):
                step = steps[n]
                dve.eng.wait_ge(tensor_done, dve.at("tensor", (tag, "scores", n)))
                for mask in step.masks:
                    mask(dve, area(n)).then_inc(vector_done, dve.mark())
                if step.masks:
                    dve.eng.wait_ge(vector_done, dve.now())
                for m, (a, b) in enumerate(step.parts):
                    nc.vector.tensor_reduce(stats[:, n % 2, m:m + 1], area(n)[:, a:b], AX, ALU.max, negate=True).then_inc(
                        vector_done, dve.mark((tag, "max", n) if m == len(step.parts) - 1 else None))

            def weigh(n):
                step = steps[n]
                k = len(step.parts)
                r = stats[:, n % 2, 8:8 + k]
                dve.eng.wait_ge(scalar_done, dve.at("scalar", (tag, "exp", n)))
                nc.vector.reciprocal(r, stats[:, n % 2, 4:4 + k]).then_inc(vector_done, dve.mark())
                dve.eng.wait_ge(vector_done, dve.now())
                if step.any_key is not None:
                    nc.vector.tensor_tensor(r[:, 0:1], r[:, 0:1], step.any_key, ALU.mult).then_inc(vector_done, dve.mark())
                    dve.eng.wait_ge(vector_done, dve.now())
                for m, (a, b) in enumerate(step.parts):
                    at = p[:, n % 2, a:b]
                    if step.gates is None:
                        ins = nc.vector.tensor_scalar(at, at, r[:, m:m + 1], None, ALU.mult)
                    else:
                        ins = nc.vector.tensor_scalar(at, at, r[:, m:m + 1], step.gates(dve, m), ALU.mult, ALU.mult)
                    ins.then_inc(vector_done, dve.mark((tag, "p", n) if m == k - 1 else None))

            maxima(0)
            maxima(1)
            weigh(0)
            for n in range(last + 1):
                if n + 2 <= last:
                    maxima(n + 2)
                if n + 1 <= last:
                    weigh(n + 1)

        carve_reset()
        ns_mixed = carve(8, T)
        ns_mixed_tiles = [ns_mixed[:, k, :] for k in range(8)]
        ns_gates = carve(4, 48)
        ns_q = carve(4, T)
        ns_k = carve(2, 4, T)
        ns_v = carve(4, P)
        ns_h = carve(4, 4 * N_CMP)
        ns_b1 = carve(4)
        ns_kc = carve(4 * N_CMP)
        ns_vcs, ns_vc = carve(4 * 64), carve(64)
        ns_free = carve_at[0]
        ns_w1 = carve(2, SLOT)
        carve_reset(ns_free)
        att_buf = att_carve()
        ns_c = arena[:, 0:8 * T].rearrange("p (a g t) -> p a g t", a=2, g=4)

        def ns_steps(it=None):
            steps = []
            group = ds(0 if it is None else it, 1)
            keys = lambda a, lo, hi: ns_k[:, a, group, lo:hi].rearrange("p a t -> p (a t)")
            kc = ns_kc[:, 0:N_CMP] if it is None else ns_kc[:, ds(it * N_CMP, N_CMP)]
            for h in range(4):
                half = slice(64 * (h % 2), 64 * (h % 2) + 64)
                for i in range(4):
                    q = ns_q[:, h, P * i:P * (i + 1)]
                    lo = max(0, i - 2)
                    wide, win, at_win = P * (i + 1), P * (i + 1 - lo), T + N_CMP
                    scores = [(q, keys(0, 0, wide), T - wide), (q, kc, T), (q, keys(1, P * i, P * (i + 1)), at_win)]
                    if i > 0:
                        scores.append((q, keys(1, P * lo, P * i), at_win + P))
                    masked = P + N_CMP + P + (P if i >= 2 else 0)

                    def mask(dve, s, i=i, n=masked):
                        return nc.vector.tensor_tensor(s[:, T - P:T - P + n], s[:, T - P:T - P + n], tab("nsa_masks", NSA_MASK * i, n), ALU.add)

                    values = [(T - wide + P * j, P, ns_v[:, j, 0:64]) for j in range(i + 1)] + [(at_win, P, ns_v[:, i, 64:128])]
                    values += [(at_win + P + P * j, P, ns_v[:, lo + j, 64:128]) for j in range(i - lo)] + [(T, N_CMP, ns_vc[0:N_CMP, :])]
                    gates = lambda dve, m, i=i, h=h: ns_gates[:, i, ds(dve.it * 12 + (3 * h + m), 1)]
                    steps.append(Step(scores, [mask], [(T, T + N_CMP), (T - wide, T), (at_win, at_win + win)], values,
                                      (6 + h // 2, half, slice(P * i, P * (i + 1))), h // 2, gates, tab("cmp_any") if i == 0 else None))
            return steps

        NS_C_BANKS, NS_K_BANKS = (3, 4, 5, 6), (7, 0, 3, 4)

        def nsa_sync(sp):
            load(sp, arrays["nsa_gates"][0], 384)
            sp.eng.wait_ge(tensor_done, sp.at("tensor", ("nsa", "sum")))
            for a in range(2):
                sp.eng.dma_start(ns_w1[:, a, :], arrays["nsa_w1"][a]).then_inc(w1_loaded, 16)
            load(sp, arrays["nsa_c"][0], 4096)
            load(sp, arrays["nsa_k"][0], 4096)
            with sp.loop(4, "nsa") as it:
                sp.first = sp.chunk
                load(sp, arrays["nsa_q"][ds(it, 1)].rearrange("a p n -> (a p) n"), 2048, 2)
                load(sp, arrays["nsa_v"][ds(it, 1)].rearrange("a p n -> (a p) n"), 1024, 2)
            out_sync(sp, "nsa", "nsa_out", 8)

        def nsa_tensor(pe):
            norm_tensor(pe, "nsa", xn_tiles, KD, after=after_of["nsa"])
            pe.eng.wait_ge(slot_loaded[pe.slot()], pe.chunk_loaded())
            w = ring[:, pe.slot(), :]
            for i in range(4):
                for k in range(KD):
                    if i == 0:
                        normed(pe, "nsa")(k)
                    nc.tensor.matmul(bank(1)[:, 48 * i:48 * i + 48], xn[:, k, P * i:P * (i + 1)], w[:, 48 * k:48 * k + 48],
                                     start=k == 0, stop=False)
                ins = nc.tensor.matmul(bank(1)[:, 48 * i:48 * i + 48], ones[0:1, :], col("nsa_bg")[0:1, :], start=False, stop=True)
            ins.then_inc(tensor_done, pe.used())
            pe.eng.wait_ge(w1_loaded, 16 * 2)
            for a in range(2):
                for m in range(2):
                    for l in range(16):
                        ins = nc.tensor.matmul(bank(2)[:, 2 * a + m:2 * a + m + 1], ns_w1[:, a, 256 * l + P * m:256 * l + P * m + P],
                                               col("nsa_pe", 16 * a + l, 1), start=l == 0, stop=l == 15)
            ins.then_inc(tensor_done, pe.mark("nsa pe"))
            for n, banks in (("c", NS_C_BANKS), ("k", NS_K_BANKS)):
                pe.eng.wait_ge(slot_loaded[pe.slot()], pe.chunk_loaded())
                w = ring[:, pe.slot(), :]
                for j, b in enumerate(banks):
                    if n == "k" and j >= 2:
                        pe.eng.wait_ge(vector_done, pe.at("vector", ("nsa c", j - 2)))
                    product(bank(b), w, xn_tiles, KD, at=1024 * j).then_inc(tensor_done, pe.mark(("nsa", n, j)) if j < 3 else pe.used())
            pe.eng.wait_ge(vector_done, pe.at("vector", ("nsa c", 3)))
            for a in range(2):
                for m in range(2):
                    for l in range(16):
                        ins = nc.tensor.matmul(bank(5)[:, 4 * N_CMP * (2 * a + m):4 * N_CMP * (2 * a + m + 1)].rearrange("p (g n) -> p g n", g=4),
                                               ns_w1[:, a, 256 * l + P * m:256 * l + P * m + P],
                                               ns_c[:, a, :, 2 * l:2 * l + 16 * (N_CMP - 1) + 1:16], start=l == 0, stop=l == 15)
            ins.then_inc(tensor_done, pe.mark("nsa h"))
            pe.eng.wait_ge(scalar_done, pe.at("scalar", "nsa h"))
            pe.eng.wait_ge(vector_done, pe.at("vector", "nsa b1"))
            for m in range(2):
                nc.tensor.matmul(bank(6)[:, 0:4 * N_CMP], col("nsa_k_w2", P * m, P), ns_h[:, m, :], start=m == 0, stop=m == 1)
            for g in range(4):
                for m in range(2):
                    ins = nc.tensor.matmul(bank(2)[0:N_CMP, 64 * g:64 * g + 64], ns_h[:, 2 + m, N_CMP * g:N_CMP * (g + 1)], col("nsa_v_w2", 64 * m, 64),
                                           start=m == 0, stop=m == 1)
            ins.then_inc(tensor_done, pe.mark("nsa kvc"))
            pe.eng.wait_ge(scalar_done, pe.at("scalar", "nsa k"))
            pe.eng.wait_ge(vector_done, pe.at("vector", "nsa kvc"))
            with pe.loop(4, "nsa") as it:
                pe.eng.wait_ge(scalar_done, pe.at("scalar", ("nsa", "mixed", 1), back=1))
                pe.eng.wait_ge(slot_loaded[pe.slot()], pe.chunk_loaded())
                w = ring[:, pe.slot(), :]
                product(bank(0), w, xn_tiles, KD).then_inc(tensor_done, pe.mark("nsa q"))
                product(bank(1), w, xn_tiles, KD, at=1024).then_inc(tensor_done, pe.used())
                pe.eng.wait_ge(slot_loaded[pe.slot()], pe.chunk_loaded())
                w = ring[:, pe.slot(), :]
                for i in range(4):
                    for k in range(KD):
                        ins = nc.tensor.matmul(bank(2)[:, P * i:P * (i + 1)], xn[:, k, P * i:P * (i + 1)],
                                               w[:, P * k:P * (k + 1)], start=k == 0, stop=k == KD - 1)
                ins.then_inc(tensor_done, pe.used())
                pe.eng.wait_ge(scalar_done, pe.at("scalar", "nsa q"))
                pe.eng.wait_ge(vector_done, pe.at("vector", "nsa v"))
                att_tensor(pe, "nsa", ns_steps(it), att_buf)
            pe.eng.wait_ge(scalar_done, pe.at("scalar", ("nsa", "mixed", 1)))
            out_tensor(pe, "nsa", ns_mixed_tiles, 8)

        def nsa_scalar(act, ready):
            def nsa_mixed(group):
                return ns_mixed[:, ds(act.it * 2 + group, 1), :].rearrange("p a t -> p (a t)")

            norm_scalar(act, "nsa", x_tiles, xn_tiles, KD, ready, after=after_of["nsa"])
            act.eng.wait_ge(tensor_done, act.at("tensor", ("chunk", act.chunk)))
            nc.scalar.activation(ns_gates[:, :, :], bank(1)[:, 0:192].rearrange("p (i n) -> p i n", i=4), ACT.Sigmoid).then_inc(scalar_done, act.mark("nsa gates"))
            for j, b in enumerate(NS_K_BANKS):
                act.eng.wait_ge(tensor_done, act.at("tensor", ("nsa", "k", j) if j < 3 else ("chunk", act.chunk + 2)))
                for e in range(2):
                    for to in range(2):
                        nc.scalar.copy(ns_k[64 * to:64 * to + 64, j % 2, 2 * (j // 2) + e, :], bank(b)[64 * e:64 * e + 64, :]).then_inc(
                            scalar_done, act.mark("nsa k" if (j, e, to) == (3, 1, 1) else None))
            act.eng.wait_ge(tensor_done, act.at("tensor", "nsa h"))
            act.eng.wait_ge(vector_done, act.at("vector", "nsa b1"))
            for j in range(4):
                nc.scalar.activation(ns_h[:, j, :], bank(5)[:, 4 * N_CMP * j:4 * N_CMP * (j + 1)], ACT.Gelu_apprx_tanh,
                                     bias=ns_b1[:, j:j + 1]).then_inc(scalar_done, act.mark("nsa h" if j == 3 else None))
            with act.loop(4, "nsa"):
                for h in range(4):
                    half = slice(64 * (h % 2), 64 * (h % 2) + 64)
                    act.eng.wait_ge(tensor_done, act.at("tensor", "nsa q" if h < 2 else ("chunk", act.chunk + 3)))
                    nc.scalar.mul(ns_q[half, h, :], bank(h // 2)[half, :], 0.125).then_inc(scalar_done, act.mark("nsa q" if h == 3 else None))
                att_scalar(act, "nsa", ns_steps(), att_buf, nsa_mixed)
            act.chunk += 5
            out_scalar(act, "nsa")

        def nsa_vector(dve):
            norm_vector(dve, "nsa", x_tiles, xn_tiles, KD, model_norm(4))
            first = dve.chunk
            dve.eng.wait_ge(tensor_done, dve.at("tensor", "nsa pe"))
            nc.vector.tensor_tensor(ns_b1, bank(2)[:, 0:4], col("nsa_b1"), ALU.add).then_inc(vector_done, dve.mark("nsa b1"))
            for h in range(4):
                other = slice(64 - 64 * (h % 2), 128 - 64 * (h % 2))
                nc.vector.memset(ns_q[other, h, :], 0.0).then_inc(vector_done, dve.mark())
            nc.vector.memset(ns_c[64:128, :, :, T - 1:T], 0.0).then_inc(vector_done, dve.mark())
            for j, b in enumerate(NS_C_BANKS):
                dve.eng.wait_ge(tensor_done, dve.at("tensor", ("nsa", "c", j) if j < 3 else ("chunk", first + 1)))
                for e in range(2):
                    src, g = bank(b)[64 * e:64 * e + 64, :], 2 * (j // 2) + e
                    nc.vector.tensor_copy(ns_c[0:64, j % 2, g, :], src).then_inc(vector_done, dve.mark())
                    nc.vector.tensor_copy(ns_c[64:128, j % 2, g, 0:T - 1], src[:, 1:T]).then_inc(vector_done, dve.mark(("nsa c", j) if e else None))
            dve.eng.wait_ge(tensor_done, dve.at("tensor", "nsa kvc"))
            nc.vector.tensor_copy(ns_kc, bank(6)[:, 0:4 * N_CMP]).then_inc(vector_done, dve.mark())
            nc.vector.tensor_copy(ns_vcs[0:N_CMP, :], bank(2)[0:N_CMP, 0:256]).then_inc(vector_done, dve.mark("nsa kvc"))
            dve.eng.wait_ge(vector_done, dve.now())
            with dve.loop(4, "nsa") as it:
                dve.eng.wait_ge(tensor_done, dve.at("tensor", ("chunk", first + 4)))
                nc.vector.tensor_copy(ns_v[:, :, :], bank(2).rearrange("p (i n) -> p i n", i=4)).then_inc(vector_done, dve.mark())
                nc.vector.tensor_copy(ns_vc[0:N_CMP, :], ns_vcs[0:N_CMP, ds(it * 64, 64)]).then_inc(vector_done, dve.mark("nsa v"))
                att_vector(dve, "nsa", ns_steps(), att_buf)
            dve.chunk += 5
            out_vector(dve, "nsa")

        MIXERS["nsa"] = {"sync": nsa_sync, "tensor": nsa_tensor, "scalar": nsa_scalar, "vector": nsa_vector}

        carve_reset()
        m2_mixed = carve(6, T)
        m2_mixed_tiles = [m2_mixed[:, k, :] for k in range(6)]
        lat = carve(6, T)
        lat_n = carve(5, T)
        m2_t = carve(2, T)
        mla_q, mla_k = carve(2, T), carve(2, T)
        mla_v = carve(4, P)
        m2_buf = att_carve()
        carve_reset(6 * T)
        dil_q, dil_k = carve(2, 3, T), carve(3, T)
        dil_v = carve(4, 384)
        dil_buf = att_carve()
        MLA_SCALE = float(96) ** -0.5
        by_class = lambda ap: ap.rearrange("p (q c) -> p c q", c=4)
        in_order = lambda ap: ap.rearrange("p (c q) -> p c q", c=4)

        def mla_steps():
            steps = []
            for h in range(2):
                for i in range(4):
                    steps.append(Step([(mla_q[0:96, h, P * i:P * (i + 1)], mla_k[0:96, h, :], 0)], [], [(0, T)],
                                      [(P * j, P, mla_v[:, j, 64 * h:64 * h + 64]) for j in range(4)],
                                      (6, slice(64 * h, 64 * h + 64), slice(P * i, P * (i + 1))), 0))
            return steps

        def dil_steps():
            steps = []
            for s in range(2):
                for c in range(DIL_CLASSES):
                    own = slice(P * c, P * (c + 1))
                    scores = [(dil_q[:, s, 0, own], dil_k[:, 0, :], 0)]
                    scores += [(dil_q[:, s, g, own], dil_k[:, g, own], T + P * (g - 1)) for g in (1, 2)]

                    def bias(g, a, n, table, s=s):
                        def put(dve, area):
                            slope = tab("slopes")[:, ds(dve.it * 2 + (4 * g + s), 1)]
                            return nc.vector.scalar_tensor_tensor(area[:, a:a + n], table, slope, area[:, a:a + n], ALU.mult, ALU.add)
                        return put

                    masks = [bias(0, 0, T, tab("dist0", T * c, T)), bias(1, T, P, tab("dist1")), bias(2, T + P, P, tab("dist2"))]
                    values = [(P * j, P, dil_v[:, j, 64 * s:64 * s + 64]) for j in range(4)]
                    values += [(T + P * (g - 1), P, dil_v[:, c, P * g + 64 * s:P * g + 64 * s + 64]) for g in (1, 2)]
                    steps.append(Step(scores, masks, [(0, T + 2 * P)], values, (6, slice(64 * s, 64 * s + 64), own), 0))
            return steps

        def m2_sync(sp):
            load(sp, arrays["mla_z"][0], 3072)
            load(sp, arrays["mla_z"][1][:, 0:2816], 2816)
            with sp.loop(4, "mla") as it:
                sp.first = sp.chunk
                load(sp, arrays["mla_q"][ds(it, 1)].rearrange("a p n -> (a p) n"), 576, 2)
                load(sp, arrays["mla_kv"][ds(it, 1)].rearrange("a p n -> (a p) n"), 512, 2)
            with sp.loop(2, "dil") as it:
                sp.first = sp.chunk
                for j in range(2):
                    load(sp, arrays["dil_qk"][ds(it * 2 + j, 1)].rearrange("a p n -> (a p) n"), 3072, 4)
                load(sp, arrays["dil_va"][ds(it, 1)].rearrange("a p n -> (a p) n"), 2048, 4)
                load(sp, arrays["dil_vb"][ds(it, 1)].rearrange("a p n -> (a p) n"), 1024, 4)
            out_sync(sp, "m2", "ab2_out", 6)

        lat_q = [lat[:, k, :] for k in range(3)]
        lat_kv = [lat[:, 3 + k, :] for k in range(2)]
        lat_qn = [lat_n[:, k, :] for k in range(3)]
        lat_kvn = [lat_n[:, 3 + k, :] for k in range(2)]

        def m2_tensor(pe):
            norm_tensor(pe, "m2", xn_tiles, KD, after=after_of["m2"])
            pe.eng.wait_ge(slot_loaded[pe.slot()], pe.chunk_loaded())
            w = ring[:, pe.slot(), :]
            for j in range(3):
                ins = product(bank(j), w, xn_tiles, KD, at=1024 * j, wait=normed(pe, "m2") if j == 0 else None)
                if j < 2:
                    ins.then_inc(tensor_done, pe.mark(("m2 z", j)))
            ins.then_inc(tensor_done, pe.used())
            pe.eng.wait_ge(slot_loaded[pe.slot()], pe.chunk_loaded())
            w = ring[:, pe.slot(), :]
            product(bank(3), w, xn_tiles, KD).then_inc(tensor_done, pe.mark(("m2 z", 3)))
            norm_tensor(pe, "mla gq", lat_qn, 3, b=6)
            product(bank(4), w, xn_tiles, KD, at=1024).then_inc(tensor_done, pe.mark(("m2 z", 4)))
            product(bank(5)[0:96, :], w, xn_tiles, KD, width=96, at=2048).then_inc(tensor_done, pe.used())
            norm_tensor(pe, "mla gkv", lat_kvn, 2, b=7)
            pe.eng.wait_ge(vector_done, pe.at("vector", "m2 z"))
            nc.tensor.matmul(bank(2)[0:96, :], tab("mla_rot")[0:96, :], lat[0:96, 5, :], start=True, stop=True).then_inc(tensor_done, pe.mark("mla rot k"))
            pe.eng.wait_ge(vector_done, pe.at("vector", ("mla gq", "normed", 2)))
            steps = mla_steps()
            with pe.loop(4, "mla"):
                pe.eng.wait_ge(scalar_done, pe.at("scalar", ("mla", "mixed", 0), back=1))
                pe.eng.wait_ge(slot_loaded[pe.slot()], pe.chunk_loaded())
                w = ring[:, pe.slot(), :]
                product(bank(0)[0:96, :], w, lat_qn, 3, width=96).then_inc(tensor_done, pe.mark(("mla q", 0)))
                product(bank(1)[0:96, :], w, lat_qn, 3, width=96, at=288).then_inc(tensor_done, pe.used())
                pe.eng.wait_ge(slot_loaded[pe.slot()], pe.chunk_loaded())
                w = ring[:, pe.slot(), :]
                pe.eng.wait_ge(vector_done, pe.at("vector", ("mla gkv", "normed", 1)))
                pe.eng.wait_ge(vector_done, pe.at("vector", "mla k rope"))
                for h in range(2):
                    product(bank(2 + h)[0:64, :], w, lat_kvn, 2, width=64, at=128 * h).then_inc(tensor_done, pe.mark(("mla k", h)))
                for h in range(2):
                    pe.eng.wait_ge(scalar_done, pe.at("scalar", ("mla raw", h)))
                    nc.tensor.matmul(bank(5 + h)[0:96, :], tab("mla_rot")[0:96, :], m2_t[0:96, h, :], start=True, stop=True).then_inc(tensor_done, pe.mark(("mla rot", h)))
                for i in range(4):
                    for k in range(2):
                        ins = nc.tensor.matmul(bank(4)[:, P * i:P * (i + 1)], lat_kvn[k][:, P * i:P * (i + 1)],
                                               w[:, 256 + P * k:256 + P * (k + 1)], start=k == 0, stop=k == 1)
                ins.then_inc(tensor_done, pe.used())
                pe.eng.wait_ge(scalar_done, pe.at("scalar", ("mla k", 1)))
                pe.eng.wait_ge(vector_done, pe.at("vector", ("mla q", 1)))
                att_tensor(pe, "mla", steps, m2_buf)
            pe.eng.wait_ge(scalar_done, pe.at("scalar", ("mla", "mixed", 0)))
            steps = dil_steps()
            with pe.loop(2, "dil"):
                pe.eng.wait_ge(scalar_done, pe.at("scalar", ("dil", "mixed", 0), back=1))
                for n in range(2):
                    pe.eng.wait_ge(slot_loaded[pe.slot()], pe.chunk_loaded())
                    w = ring[:, pe.slot(), :]
                    for j in range(3):
                        ins = product(bank(3 * n + j), w, xn_tiles, KD, at=1024 * j)
                        if j < 2:
                            ins.then_inc(tensor_done, pe.mark(("dil qk", 3 * n + j)))
                    ins.then_inc(tensor_done, pe.used())
                pe.eng.wait_ge(slot_loaded[pe.slot()], pe.chunk_loaded())
                w = ring[:, pe.slot(), :]
                for c in range(4):
                    for k in range(KD):
                        ins = nc.tensor.matmul(bank(6 + c // 2)[:, 256 * (c % 2):256 * (c % 2) + 256], by_class(xn[:, k, :])[:, c, :],
                                               w[:, 256 * k:256 * (k + 1)], start=k == 0, stop=k == KD - 1)
                ins.then_inc(tensor_done, pe.used())
                pe.eng.wait_ge(slot_loaded[pe.slot()], pe.chunk_loaded())
                w = ring[:, pe.slot(), :]
                pe.eng.wait_ge(scalar_done, pe.at("scalar", "dil q"))
                for c in range(4):
                    for k in range(KD):
                        ins = nc.tensor.matmul(bank(0)[:, P * c:P * (c + 1)], by_class(xn[:, k, :])[:, c, :],
                                               w[:, P * k:P * (k + 1)], start=k == 0, stop=k == KD - 1)
                ins.then_inc(tensor_done, pe.used())
                pe.eng.wait_ge(vector_done, pe.at("vector", "dil v"))
                pe.eng.wait_ge(scalar_done, pe.at("scalar", "dil q"))
                att_tensor(pe, "dil", steps, dil_buf)
            pe.eng.wait_ge(scalar_done, pe.at("scalar", ("dil", "mixed", 0)))
            out_tensor(pe, "m2", m2_mixed_tiles, 6)

        def m2_scalar(act, ready):
            def mla_mixed(group):
                return m2_mixed[:, ds(act.it, 1), :].rearrange("p a t -> p (a t)")

            def dil_mixed(group):
                return m2_mixed[:, ds(act.it + 4, 1), :].rearrange("p a (q c) -> p (a c) q", c=4)

            norm_scalar(act, "m2", x_tiles, xn_tiles, KD, ready, after=after_of["m2"])
            norm_scalar(act, "mla gq", lat_q, lat_qn, 3, (vector_done, act.at("vector", "m2 q latents")))
            norm_scalar(act, "mla gkv", lat_kv, lat_kvn, 2, (vector_done, act.at("vector", "m2 z")))
            steps = mla_steps()
            with act.loop(4, "mla"):
                act.eng.wait_ge(vector_done, act.at("vector", "mla k rope"))
                act.eng.wait_ge(tensor_done, act.at("tensor", ("mla q", 0)))
                nc.scalar.copy(m2_t[0:96, 0, :], bank(0)[0:96, :]).then_inc(scalar_done, act.mark(("mla raw", 0)))
                act.eng.wait_ge(tensor_done, act.at("tensor", ("chunk", act.chunk + 2)))
                nc.scalar.copy(m2_t[0:96, 1, :], bank(1)[0:96, :]).then_inc(scalar_done, act.mark(("mla raw", 1)))
                for h in range(2):
                    act.eng.wait_ge(tensor_done, act.at("tensor", ("mla k", h)))
                    nc.scalar.copy(mla_k[0:64, h, :], bank(2 + h)[0:64, :]).then_inc(scalar_done, act.mark(("mla k", h)))
                att_scalar(act, "mla", steps, m2_buf, mla_mixed)
            steps = dil_steps()
            with act.loop(2, "dil"):
                for j in range(3):
                    act.eng.wait_ge(tensor_done, act.at("tensor", ("dil qk", j) if j < 2 else ("chunk", act.chunk + 4)))
                    for s in range(2):
                        half = slice(64 * s, 64 * s + 64)
                        nc.scalar.mul(in_order(dil_q[half, s, j, :]), by_class(bank(j)[half, :]), 0.125).then_inc(
                            scalar_done, act.mark("dil q" if j == 2 and s == 1 else None))
                att_scalar(act, "dil", steps, dil_buf, dil_mixed)
            act.chunk += 8
            out_scalar(act, "m2")

        def m2_vector(dve):
            norm_vector(dve, "m2", x_tiles, xn_tiles, KD, model_norm(7))
            first = dve.chunk
            for j in range(6):
                dve.eng.wait_ge(tensor_done, dve.at("tensor", ("chunk", first) if j == 2 else ("chunk", first + 1) if j == 5 else ("m2 z", j)))
                n = 96 if j == 5 else P
                nc.vector.tensor_copy(lat[0:n, j, :], bank(j)[0:n, :]).then_inc(vector_done, dve.mark({2: "m2 q latents", 5: "m2 z"}.get(j)))
                if j == 3:
                    norm_vector(dve, "mla gq", lat_q, lat_qn, 3, lambda k: col("mla_gq", k, 1), b=6)
            norm_vector(dve, "mla gkv", lat_kv, lat_kvn, 2, lambda k: col("mla_gkv", k, 1), b=7)
            dve.eng.wait_ge(tensor_done, dve.at("tensor", "mla rot k"))
            at = slice(64, 96)
            nc.vector.tensor_tensor(m2_t[at, 0, :], lat[at, 5, :], tab("mla_cos")[at, :], ALU.mult).then_inc(vector_done, dve.mark())
            nc.vector.tensor_tensor(m2_t[at, 1, :], tab("mla_sin")[at, :], bank(2)[at, :], ALU.mult).then_inc(vector_done, dve.mark())
            dve.eng.wait_ge(vector_done, dve.now())
            for h in range(2):
                nc.vector.tensor_tensor(mla_k[at, h, :], m2_t[at, 0, :], m2_t[at, 1, :], ALU.add).then_inc(vector_done, dve.mark("mla k rope" if h else None))
            steps = mla_steps()
            with dve.loop(4, "mla"):
                for h in range(2):
                    dve.eng.wait_ge(scalar_done, dve.at("scalar", ("mla raw", h)))
                    nc.vector.scalar_tensor_tensor(mla_q[0:96, h, :], m2_t[0:96, h, :], MLA_SCALE, tab("mla_cos")[0:96, :], ALU.mult, ALU.mult).then_inc(vector_done, dve.mark())
                dve.eng.wait_ge(vector_done, dve.now())
                for h in range(2):
                    dve.eng.wait_ge(tensor_done, dve.at("tensor", ("mla rot", h)))
                    nc.vector.scalar_tensor_tensor(m2_t[0:96, h, :], bank(5 + h)[0:96, :], MLA_SCALE, tab("mla_sin")[0:96, :], ALU.mult, ALU.mult).then_inc(vector_done, dve.mark())
                    dve.eng.wait_ge(vector_done, dve.now())
                    nc.vector.tensor_tensor(mla_q[0:96, h, :], mla_q[0:96, h, :], m2_t[0:96, h, :], ALU.add).then_inc(vector_done, dve.mark())
                dve.eng.wait_ge(tensor_done, dve.at("tensor", ("chunk", first + 3)))
                nc.vector.tensor_copy(mla_v[:, :, :], bank(4).rearrange("p (i n) -> p i n", i=4)).then_inc(vector_done, dve.mark(("mla q", 1)))

                att_vector(dve, "mla", steps, m2_buf)
            steps = dil_steps()
            for s in range(2):
                nc.vector.memset(dil_q[64 - 64 * s:128 - 64 * s, s, :, :], 0.0).then_inc(vector_done, dve.mark())
            with dve.loop(2, "dil"):
                for j in range(3):
                    dve.eng.wait_ge(tensor_done, dve.at("tensor", ("dil qk", 3 + j) if j < 2 else ("chunk", first + 5)))
                    nc.vector.tensor_copy(in_order(dil_k[:, j, :]), by_class(bank(3 + j))).then_inc(vector_done, dve.mark())
                dve.eng.wait_ge(tensor_done, dve.at("tensor", ("chunk", first + 6)))
                for b in range(2):
                    nc.vector.tensor_copy(dil_v[:, 2 * b:2 * b + 2, 0:256], bank(6 + b).rearrange("p (c n) -> p c n", c=2)).then_inc(vector_done, dve.mark())
                dve.eng.wait_ge(tensor_done, dve.at("tensor", ("chunk", first + 7)))
                nc.vector.tensor_copy(dil_v[:, :, 256:384], bank(0).rearrange("p (c n) -> p c n", c=4)).then_inc(vector_done, dve.mark("dil v"))

                att_vector(dve, "dil", steps, dil_buf)
            dve.chunk += 8
            out_vector(dve, "m2")

        MIXERS["m2"] = {"sync": m2_sync, "tensor": m2_tensor, "scalar": m2_scalar, "vector": m2_vector}

        carve_reset()
        gq_mixed = carve(8, T)
        gq_mixed_tiles = [gq_mixed[:, k, :] for k in range(8)]
        gq_raw, gq_sq, gq_n = carve(2, T), carve(2, T), carve(2, T)
        gq_r, gq_t = carve(2, T), carve(T)
        gq_q = carve(4, T)
        gq_k = carve(4, T)
        gq_vs = carve(4, 256)
        gq_v = carve(4, 64)
        gq_buf = att_carve()

        def gqa_steps(it=None):
            steps = []
            key = (gq_k[:, 3:4, :] if it is None else gq_k[:, ds(it, 1), :]).rearrange("p a t -> p (a t)")
            for h in range(4):
                half = slice(64 * (h % 2), 64 * (h % 2) + 64)
                for i in range(4):
                    steps.append(Step([(gq_q[:, h, P * i:P * (i + 1)], key, 0)], [], [(0, T)],
                                      [(P * j, P, gq_v[:, j, :]) for j in range(4)],
                                      (6 + h // 2, half, slice(P * i, P * (i + 1))), h // 2))
            return steps

        def gqa_sync(sp):
            load(sp, arrays["gqa_k"][0], 2048)
            load(sp, arrays["gqa_v"][0], 2048)
            for j in range(2):
                load(sp, arrays["gqa_q"][j], 1024)
            with sp.loop(3, "gqa") as it:
                sp.first = sp.chunk
                for j in range(2):
                    load(sp, arrays["gqa_q"][ds(it * 2 + (2 + j), 1)].rearrange("a p n -> (a p) n"), 1024, 2)
            out_sync(sp, "gqa", "gqa_out", 8)

        def gqa_tensor(pe):
            def raw(tag):
                for j in range(2):
                    pe.eng.wait_ge(slot_loaded[pe.slot()], pe.chunk_loaded())
                    product(bank(j), ring[:, pe.slot(), :], xn_tiles, KD).then_inc(tensor_done, pe.used())

            def sums(tag, before, back=0):
                for j in range(2):
                    pe.eng.wait_ge(scalar_done, pe.at("scalar", (before, "square", j), back=back))
                    nc.tensor.matmul(bank(4 + j), tab("ones64"), gq_sq[:, j, :], start=True, stop=True).then_inc(tensor_done, pe.mark((tag, "sum", j)))

            def rotate(tag):
                for j in range(2):
                    pe.eng.wait_ge(vector_done, pe.at("vector", (tag, "normed", j)))
                    nc.tensor.matmul(bank(2 + j), tab("gqa_rot"), gq_n[:, j, :], start=True, stop=True).then_inc(tensor_done, pe.mark((tag, "rot", j)))

            norm_tensor(pe, "gqa x", xn_tiles, KD, after=after_of["gqa"])
            pe.eng.wait_ge(slot_loaded[pe.slot()], pe.chunk_loaded())
            w = ring[:, pe.slot(), :]
            product(bank(0), w, xn_tiles, KD, wait=normed(pe, "gqa x")).then_inc(tensor_done, pe.mark("gqa k"))
            product(bank(1), w, xn_tiles, KD, at=1024).then_inc(tensor_done, pe.used())
            sums("gk", "gqa k")
            pe.eng.wait_ge(slot_loaded[pe.slot()], pe.chunk_loaded())
            w = ring[:, pe.slot(), :]
            for i in range(4):
                for k in range(KD):
                    ins = nc.tensor.matmul(bank(6 + i // 2)[:, 256 * (i % 2):256 * (i % 2) + 256], xn[:, k, P * i:P * (i + 1)],
                                           w[:, 256 * k:256 * (k + 1)], start=k == 0, stop=k == KD - 1)
            ins.then_inc(tensor_done, pe.used())
            raw("gk")
            rotate("gk")
            for j in range(2):
                pe.eng.wait_ge(scalar_done, pe.at("scalar", ("gk", "square", j)))
            pe.eng.wait_ge(vector_done, pe.at("vector", ("gk", "rotated")))
            with pe.loop(3, "gqa") as it:
                sums("gqa", "gqa", back=1)
                raw("gqa")
                rotate("gqa")
                pe.eng.wait_ge(scalar_done, pe.at("scalar", ("gqa", "square", 1)))
                pe.eng.wait_ge(scalar_done, pe.at("scalar", ("gqa", "mixed", 1), back=1))
                pe.eng.wait_ge(vector_done, pe.at("vector", ("gqa", "rotated")))
                att_tensor(pe, "gqa", gqa_steps(it), gq_buf)
            sums("gql", "gqa")
            rotate("gql")
            pe.eng.wait_ge(scalar_done, pe.at("scalar", ("gqa", "mixed", 1)))
            pe.eng.wait_ge(vector_done, pe.at("vector", ("gql", "rotated")))
            att_tensor(pe, "gql", gqa_steps(), gq_buf)
            pe.eng.wait_ge(scalar_done, pe.at("scalar", ("gql", "mixed", 1)))
            out_tensor(pe, "gqa", gq_mixed_tiles, 8)

        def gqa_scalar(act, ready):
            def taken(tag, by=None):
                for j in range(2):
                    act.eng.wait_ge(tensor_done, act.at("tensor", ("chunk", act.chunk + j) if by is None else by[j]))
                    if by is None:
                        act.eng.wait_ge(vector_done, act.at("vector", (tag, "normed", j)))
                    nc.scalar.copy(gq_raw[:, j, :], bank(j)).then_inc(scalar_done, act.mark())
                    nc.scalar.activation(gq_sq[:, j, :], bank(j), ACT.Square).then_inc(scalar_done, act.mark((tag, "square", j)))

            def roots(tag):
                act.eng.wait_ge(scalar_done, act.now())
                nc.scalar.activation(warm[:, :], ones[:, 0:1], ACT.Sqrt).then_inc(scalar_done, act.mark())
                for j in range(2):
                    act.eng.wait_ge(vector_done, act.at("vector", (tag, "mean", j)))
                    nc.scalar.activation(gq_r[:, j, :], gq_r[:, j, :], ACT.Sqrt).then_inc(scalar_done, act.mark((tag, "rstd", j)))

            norm_scalar(act, "gqa x", x_tiles, xn_tiles, KD, ready, after=after_of["gqa"])
            taken("gqa k", ["gqa k", ("chunk", act.chunk)])
            roots("gk")
            act.chunk += 2
            taken("gk")
            act.chunk += 2
            with act.loop(3, "gqa"):
                roots("gqa")
                taken("gqa")
                att_scalar(act, "gqa", gqa_steps(), gq_buf,
                           lambda group: gq_mixed[:, ds(act.it * 2 + group, 1), :].rearrange("p a t -> p (a t)"))
            act.chunk += 2
            roots("gql")
            att_scalar(act, "gql", gqa_steps(), gq_buf, lambda group: gq_mixed[:, 6 + group, :])
            out_scalar(act, "gqa")

        def gqa_vector(dve):
            def norms(tag, gain):
                for j in range(2):
                    dve.eng.wait_ge(tensor_done, dve.at("tensor", (tag, "sum", j)))
                    nc.vector.tensor_scalar(gq_r[:, j, :], bank(4 + j), 1.0 / 64, EPS, ALU.mult, ALU.add).then_inc(vector_done, dve.mark())
                    dve.eng.wait_ge(vector_done, dve.now())
                    nc.vector.reciprocal(gq_r[:, j, :], gq_r[:, j, :]).then_inc(vector_done, dve.mark((tag, "mean", j)))
                for j in range(2):
                    dve.eng.wait_ge(scalar_done, dve.at("scalar", (tag, "rstd", j)))
                    nc.vector.scalar_tensor_tensor(gq_n[:, j, :], gq_raw[:, j, :], gain, gq_r[:, j, :], ALU.mult, ALU.mult).then_inc(vector_done, dve.mark((tag, "normed", j)))

            def rotated(tag, scale, outs):
                for j in range(2):
                    dve.eng.wait_ge(vector_done, dve.now())
                    nc.vector.scalar_tensor_tensor(gq_r[:, j, :], gq_n[:, j, :], scale, tab("gqa_cos"), ALU.mult, ALU.mult).then_inc(vector_done, dve.mark())
                    dve.eng.wait_ge(tensor_done, dve.at("tensor", (tag, "rot", j)))
                    nc.vector.scalar_tensor_tensor(gq_t, bank(2 + j), scale, tab("gqa_sin"), ALU.mult, ALU.mult).then_inc(vector_done, dve.mark())
                    dve.eng.wait_ge(vector_done, dve.now())
                    for n, (half, to) in enumerate(outs(j)):
                        nc.vector.tensor_tensor(to, gq_r[half, j, :], gq_t[half, :], ALU.add).then_inc(
                            vector_done, dve.mark((tag, "rotated") if j == 1 and n == len(outs(j)) - 1 else None))

            halves = (slice(0, 64), slice(64, 128))
            queries = lambda j: [(half, gq_q[half, 2 * j + e, :]) for e, half in enumerate(halves)]
            norm_vector(dve, "gqa x", x_tiles, xn_tiles, KD, model_norm(9))
            for h in range(4):
                nc.vector.memset(gq_q[halves[1 - h % 2], h, :], 0.0).then_inc(vector_done, dve.mark())
            norms("gk", col("gqa_gk"))
            for b in range(2):
                dve.eng.wait_ge(tensor_done, dve.at("tensor", ("chunk", dve.chunk + 1)))
                nc.vector.tensor_copy(gq_vs[:, 2 * b:2 * b + 2, :], bank(6 + b).rearrange("p (i n) -> p i n", i=2)).then_inc(vector_done, dve.mark())
            rotated("gk", 1.0, lambda j: [(halves[e], gq_k[to, 2 * j + e, :]) for e in range(2) for to in halves])
            with dve.loop(3, "gqa") as it:
                norms("gqa", col("gqa_gq"))
                nc.vector.tensor_copy(gq_v[:, :, :], gq_vs[:, :, ds(it * 64, 64)]).then_inc(vector_done, dve.mark())
                rotated("gqa", 0.125, queries)
                att_vector(dve, "gqa", gqa_steps(), gq_buf)
            norms("gql", col("gqa_gq"))
            nc.vector.tensor_copy(gq_v[:, :, :], gq_vs[:, :, 192:256]).then_inc(vector_done, dve.mark())
            rotated("gql", 0.125, queries)
            att_vector(dve, "gql", gqa_steps(), gq_buf)
            dve.chunk += 6
            out_vector(dve, "gqa")

        MIXERS["gqa"] = {"sync": gqa_sync, "tensor": gqa_tensor, "scalar": gqa_scalar, "vector": gqa_vector}

        todo = stages or ["f0", "ab", "f1", "f2", "nsa", "f3", "n1", "m2", "f4", "gqa", "f5", "n2"]
        FFN = {"f0": (0, 0, 0.5), "f1": (1, 2, 0.5), "f2": (2, 3, 0.5), "f3": (3, 5, 0.5), "f4": (4, 8, 1.0), "f5": (5, 10, 1.0)}

        updating = [s for s in todo if s in FFN or s in MIXERS]
        stage_no = {s: n for n, s in enumerate(updating)}
        after_of = {s: stage_no[todo[i - 1]] + 1 if i > 0 and todo[i - 1] in stage_no else None for i, s in enumerate(todo)}

        def ready_for(e, i):
            if i == 0:
                return vector_done, e.at("vector", "x")
            s = todo[i - 1]
            if s in stage_no:
                return x_updated, KD * (stage_no[s] + 1) + 2
            return vector_done, e.at("vector", (s, "normed", KD - 1))

        def mixer_sync(sp, s, i):
            if i:
                sp.eng.wait_ge(*ready_for(sp, i))
            if s in tables_at:
                sp.eng.dma_start(tabbuf[s][:, 0:tables_at[s][1]], arrays["t_" + s]).then_inc(tables_loaded, 16)
            sp.base = sp.chunk
            MIXERS[s]["sync"](sp)

        def wait_tables(e, s):
            mixers = [m for m in todo if m in MIXERS]
            e.eng.wait_ge(tables_loaded, 16 * (mixers.index(s) + 1))

        if todo[-1] != "n2":
            todo = todo + ["end"]

        n_chunks = []
        block = ctx.enter_context(nc.Block())

        @block.sync
        def _(eng):
            sp = Engine(eng, None, counts, [counts["slot0"], counts["slot1"]])
            start_sync(sp)
            for i, s in enumerate(todo):
                if s in FFN:
                    ffn_sync(sp, s, FFN[s][0], i > 0 and todo[i - 1] in MIXERS)
                elif s in MIXERS:
                    mixer_sync(sp, s, i)
            end_sync(sp)
            n_chunks.append(sp.chunk)

        @block.tensor
        def _(eng):
            pe = Engine(eng, counts["tensor"], counts)
            eng.sem_inc(tensor_done, LEAD)
            eng.sem_inc(unit_used, 2)
            start_tensor(pe)
            for i, s in enumerate(todo):
                if s in FFN:
                    ffn_tensor(pe, s, FFN[s][0])
                elif s in MIXERS:
                    wait_tables(pe, s)
                    MIXERS[s]["tensor"](pe)
                elif s in ("n1", "n2"):
                    norm_tensor(pe, s, xn_tiles, KD, after=after_of[s])
            end_tensor(pe, ("n2", "normed", KD - 1) if todo[-1] == "n2" else "end")
            n_chunks.append(pe.chunk)

        @block.scalar
        def _(eng):
            act = Engine(eng, counts["scalar"], counts)
            eng.sem_inc(scalar_done, LEAD)
            for i, s in enumerate(todo):
                if s in FFN:
                    ffn_scalar(act, s, FFN[s][0], ready_for(act, i))
                elif s in MIXERS:
                    MIXERS[s]["scalar"](act, ready_for(act, i))
                elif s in ("n1", "n2"):
                    norm_scalar(act, s, x_tiles, xn_tiles, KD, ready_for(act, i), after=after_of[s])
            n_chunks.append(act.chunk)

        @block.vector
        def _(eng):
            dve = Engine(eng, counts["vector"], counts)
            eng.sem_inc(vector_done, LEAD)
            eng.sem_inc(unit_ready, 4)
            eng.sem_inc(hidden_ready, 2)
            eng.sem_inc(x_updated, 2)
            start_vector(dve)
            for i, s in enumerate(todo):
                if s in FFN:
                    ffn_vector(dve, s, *FFN[s])
                elif s in MIXERS:
                    wait_tables(dve, s)
                    MIXERS[s]["vector"](dve)
                elif s in ("n1", "n2"):
                    norm_vector(dve, s, x_tiles, x_tiles if s == "n1" else xn_tiles, KD, model_norm(6 if s == "n1" else 11))
                elif s == "end":
                    dve.eng.wait_ge(vector_done, dve.now())
                    dve.eng.wait_ge(*ready_for(dve, i))
                    dve.eng.wait_ge(summed, KD * len(updating))
                    nc.vector.tensor_copy(xn[:, :, :], x[:, :, :]).then_inc(vector_done, dve.mark("end"))
            end_vector(dve)
            n_chunks.append(dve.chunk)

    assert len(set(n_chunks)) == 1, n_chunks
    return seen


def program(Bacc, shapes, columns_at, tables_at, stages=None):
    marks = {}
    while True:
        nc = Bacc("TRN2", target_bir_lowering=False, num_devices=1)
        arrays = {n: nc.dram_tensor(f"in_{n}", s, F32, kind="ExternalInput").ap() for n, s in shapes.items()}
        out = nc.dram_tensor("out_0", (T, D), F32, kind="ExternalOutput").ap()
        seen = build(nc, arrays, columns_at, tables_at, out, marks, stages)
        if seen == marks:
            return nc
        marks = seen


def prepare(inputs):
    tables = make_tables()
    weights, columns = lay_out(inputs)
    columns_at, _ = offsets(columns)
    tables_at = {stage: offsets(t) for stage, t in tables.items()}
    sent = {"x": inputs["x"][0], "columns": np.concatenate(list(columns.values()), 1)}
    sent.update(weights)
    sent.update({"t_" + stage: np.concatenate(list(t.values()), 1) for stage, t in tables.items()})
    return {n: np.ascontiguousarray(a) for n, a in sent.items()}, columns_at, tables_at


def kernel(**inputs):
    import concourse.bacc as _bacc
    from concourse.bass_utils import run_bass_kernel_spmd as _run

    inputs = {n: np.asarray(a) for n, a in inputs.items()}
    sent, columns_at, tables_at = prepare(inputs)
    nc = program(_bacc.Bacc, {n: a.shape for n, a in sent.items()}, columns_at, tables_at)
    r = _run(nc, [{f"in_{n}": a for n, a in sent.items()}], core_ids=[0])
    return r.results[0]["out_0"].reshape(1, T, D)
```
